# Optimizing a Trainium2 kernel written in Bass

```python
import math
import jax, jax.numpy as jnp
from jax import lax
import numpy as np

D_MODEL = 1024
BATCH = 1
SEQ = 256
DEPTH = 2

GRID_W = 64
CTX_LEN = 256
N_MIXERS = 3
N_MOD = 6
EPS = 1e-6
S5_GROUP = 16
S5_GROUPS = D_MODEL // S5_GROUP
S5_STATE = 64
N_DIRS = 2
DT_MIN = 1e-3
DT_MAX = 1e-1
POOL_WINDOWS = (2, 4, 8, 16)
POOL_GROUPS = len(POOL_WINDOWS)
POOL_WIDTH = D_MODEL // POOL_GROUPS
FNET_GROUPS = 4
FNET_WIDTH = D_MODEL // FNET_GROUPS
D_FF = 2816
N_EXPERTS = 8
TOP_K = 2
D_FF_EXPERT = 3584
N_S5_LAYERS = (DEPTH - 1) // N_MIXERS + 1
N_POOL_LAYERS = (DEPTH - 2) // N_MIXERS + 1
N_FNET_LAYERS = (DEPTH - 3) // N_MIXERS + 1
N_DENSE_LAYERS = (DEPTH + 1) // 2
N_MOE_LAYERS = DEPTH // 2

kernel_name = "hybrid_s5_pool_fourier_moe_dit"

def rms_norm(h, gain):
    hf = h.astype(jnp.float32)
    inv = lax.rsqrt(jnp.mean(hf * hf, axis=-1, keepdims=True) + EPS)
    return (hf * inv * gain.astype(jnp.float32)).astype(h.dtype)

def ada_params(cond, w, b):
    m = jax.nn.silu(cond) @ w + b
    return jnp.split(m[..., None, :], N_MOD, axis=-1)

def modulate(h, shift, scale):
    return h * (1 + scale) + shift

def s5_discretise(lam_re, lam_im, log_step, b_re, b_im):
    lam = lax.complex(lam_re.astype(jnp.float32), lam_im.astype(jnp.float32))
    step = jnp.exp(log_step.astype(jnp.float32))[:, None]
    lam_bar = jnp.exp(lam * step)
    b = lax.complex(b_re.astype(jnp.float32), b_im.astype(jnp.float32))
    b_bar = ((lam_bar - 1.0) / lam)[..., None] * b
    return lam_bar, b_bar

def linear_recurrence(bu, lam_bar, reverse):
    decay = jnp.broadcast_to(lam_bar, bu.shape[1:])[None]

    def combine(left, right):
        a_l, b_l = left
        a_r, b_r = right
        return a_r * a_l, a_r * b_l + b_r

    _, h = lax.associative_scan(combine, (decay, bu), reverse=reverse, axis=1)
    return h

def s5_glu(y, glu_w, glu_b):
    z = jax.nn.gelu(y)
    return z * jax.nn.sigmoid(z @ glu_w.astype(jnp.float32) + glu_b.astype(jnp.float32))

def s5_mixer(u_lat, u_ctx, lam_re, lam_im, log_step, b_re, b_im, c_re, c_im, d, glu_w, glu_b, need_ctx):
    bsz, n_lat, _ = u_lat.shape
    n_ctx = u_ctx.shape[1]
    ul = u_lat.astype(jnp.float32).reshape(bsz, n_lat, S5_GROUPS, S5_GROUP).astype(jnp.complex64)
    uc = u_ctx.astype(jnp.float32).reshape(bsz, n_ctx, S5_GROUPS, S5_GROUP).astype(jnp.complex64)
    d32 = d.astype(jnp.float32)
    y_lat = d32 * u_lat.astype(jnp.float32)
    y_ctx = d32 * u_ctx.astype(jnp.float32) if need_ctx else None
    for direction in range(N_DIRS):
        reverse = direction == 1
        lam_bar, b_bar = s5_discretise(lam_re[direction], lam_im[direction], log_step[direction],
                                       b_re[direction], b_im[direction])
        c_mat = lax.complex(c_re[direction].astype(jnp.float32), c_im[direction].astype(jnp.float32))
        h_ctx = linear_recurrence(jnp.einsum('bngh,gph->bngp', uc, b_bar), lam_bar, reverse)
        h_start = h_ctx[:, 0] if reverse else h_ctx[:, -1]
        bu_lat = jnp.einsum('bngh,gph->bngp', ul, b_bar)
        bu_lat = bu_lat.at[:, -1 if reverse else 0].add(lam_bar * h_start)
        h_lat = linear_recurrence(bu_lat, lam_bar, reverse)
        y_lat = y_lat + jnp.einsum('bngp,ghp->bngh', h_lat, c_mat).real.reshape(bsz, n_lat, D_MODEL)
        if need_ctx:
            y_ctx = y_ctx + jnp.einsum('bngp,ghp->bngh', h_ctx, c_mat).real.reshape(bsz, n_ctx, D_MODEL)
    out_lat = s5_glu(y_lat, glu_w, glu_b).astype(u_lat.dtype)
    out_ctx = s5_glu(y_ctx, glu_w, glu_b).astype(u_ctx.dtype) if need_ctx else None
    return out_lat, out_ctx

def centred_pool_residual(h, window):
    width = h.shape[2]
    csum = jnp.concatenate([jnp.zeros_like(h[:, :, :1]), jnp.cumsum(h, axis=2)], axis=2)
    pos = jnp.arange(width)
    lo = jnp.clip(pos - window // 2, 0, width)
    hi = jnp.clip(pos + window // 2, 0, width)
    count = (hi - lo).astype(h.dtype)[:, None]
    return (jnp.take(csum, hi, axis=2) - jnp.take(csum, lo, axis=2)) / count - h

def pool_mixer(u, rows, width, w, b, scale):
    bsz, n, _ = u.shape
    hf = u.astype(jnp.float32).reshape(bsz, rows, width, D_MODEL)
    res = jnp.stack([centred_pool_residual(hf[..., g * POOL_WIDTH:(g + 1) * POOL_WIDTH], win)
                     for g, win in enumerate(POOL_WINDOWS)], axis=3)
    mixed = jnp.einsum('brwgc,gcd->brwgd', res, w.astype(jnp.float32)) + b.astype(jnp.float32).reshape(POOL_GROUPS, POOL_WIDTH)
    return (mixed.reshape(bsz, n, D_MODEL) * scale.astype(jnp.float32)).astype(u.dtype)

def fourier_mixer(u, w, b):
    bsz, n, _ = u.shape
    hg = u.astype(jnp.float32).reshape(bsz, n, FNET_GROUPS, FNET_WIDTH)
    mixed = jnp.fft.fftn(hg, axes=(1, 3), norm="ortho").real.reshape(bsz, n, D_MODEL)
    return (mixed @ w.astype(jnp.float32) + b.astype(jnp.float32)).astype(u.dtype)

def swiglu(h, w_gate, w_up, w_down):
    return (jax.nn.silu(h @ w_gate) * (h @ w_up)) @ w_down

def moe_swiglu(h, router, w_gate, w_up, w_down):
    logits = h.astype(jnp.float32) @ router.astype(jnp.float32)
    top_vals, top_idx = lax.top_k(logits, TOP_K)
    weights = jax.nn.softmax(top_vals, axis=-1)
    combine = jnp.sum(jax.nn.one_hot(top_idx, N_EXPERTS, dtype=jnp.float32) * weights[..., None], axis=-2)
    combine = combine.astype(h.dtype)
    out = jnp.zeros_like(h)
    for e in range(N_EXPERTS):
        out = out + combine[..., e:e + 1] * swiglu(h, w_gate[e], w_up[e], w_down[e])
    return out

def setup_inputs(seed: int = 0) -> dict:
    key = jax.random.key(seed)
    ks = iter(jax.random.split(key, 40))
    f32 = jnp.float32

    def nrm(shape, scale):
        return jax.random.normal(next(ks), shape, f32) * scale

    d = D_MODEL
    lam_im_base = jnp.pi * jnp.arange(S5_STATE, dtype=f32)
    s5_shape = (N_S5_LAYERS, N_DIRS, S5_GROUPS, S5_STATE)
    return {
        "x": nrm((BATCH, SEQ, d), 1.0),
        "c": nrm((BATCH, d), 1.0),
        "ctx": nrm((BATCH, CTX_LEN, d), 1.0),
        "c_ctx": nrm((d,), 1.0),
        "ada_w": nrm((DEPTH, d, N_MOD * d), 0.5 * d ** -0.5),
        "ada_b": nrm((DEPTH, N_MOD * d), 0.02),
        "norm_mix": 1.0 + nrm((DEPTH, d), 0.1),
        "norm_ffn": 1.0 + nrm((DEPTH, d), 0.1),
        "norm_final": 1.0 + nrm((d,), 0.1),
        "s5_lambda_re": -0.5 + nrm(s5_shape, 0.01),
        "s5_lambda_im": lam_im_base + nrm(s5_shape, 0.01),
        "s5_log_step": jax.random.uniform(next(ks), (N_S5_LAYERS, N_DIRS, S5_GROUPS), f32,
                                           math.log(DT_MIN), math.log(DT_MAX)),
        "s5_b_re": nrm(s5_shape + (S5_GROUP,), (2 * S5_GROUP) ** -0.5),
        "s5_b_im": nrm(s5_shape + (S5_GROUP,), (2 * S5_GROUP) ** -0.5),
        "s5_c_re": nrm((N_S5_LAYERS, N_DIRS, S5_GROUPS, S5_GROUP, S5_STATE), (2 * S5_STATE) ** -0.5),
        "s5_c_im": nrm((N_S5_LAYERS, N_DIRS, S5_GROUPS, S5_GROUP, S5_STATE), (2 * S5_STATE) ** -0.5),
        "s5_d": nrm((N_S5_LAYERS, d), 1.0),
        "s5_glu_w": nrm((N_S5_LAYERS, d, d), d ** -0.5),
        "s5_glu_b": nrm((N_S5_LAYERS, d), 0.02),
        "pool_w": nrm((N_POOL_LAYERS, POOL_GROUPS, POOL_WIDTH, POOL_WIDTH), POOL_WIDTH ** -0.5),
        "pool_b": nrm((N_POOL_LAYERS, d), 0.02),
        "pool_scale": 1.0 + nrm((N_POOL_LAYERS, d), 0.1),
        "fnet_w": nrm((N_FNET_LAYERS, d, d), d ** -0.5),
        "fnet_b": nrm((N_FNET_LAYERS, d), 0.02),
        "ffn_w_gate": nrm((N_DENSE_LAYERS, d, D_FF), d ** -0.5),
        "ffn_w_up": nrm((N_DENSE_LAYERS, d, D_FF), d ** -0.5),
        "ffn_w_down": nrm((N_DENSE_LAYERS, D_FF, d), D_FF ** -0.5),
        "moe_router": nrm((N_MOE_LAYERS, d, N_EXPERTS), d ** -0.5),
        "moe_w_gate": nrm((N_MOE_LAYERS, N_EXPERTS, d, D_FF_EXPERT), d ** -0.5),
        "moe_w_up": nrm((N_MOE_LAYERS, N_EXPERTS, d, D_FF_EXPERT), d ** -0.5),
        "moe_w_down": nrm((N_MOE_LAYERS, N_EXPERTS, D_FF_EXPERT, d), D_FF_EXPERT ** -0.5),
    }

def reference(x, c, ctx, c_ctx, ada_w, ada_b, norm_mix, norm_ffn, norm_final,
              s5_lambda_re, s5_lambda_im, s5_log_step, s5_b_re, s5_b_im, s5_c_re, s5_c_im,
              s5_d, s5_glu_w, s5_glu_b, pool_w, pool_b, pool_scale, fnet_w, fnet_b,
              ffn_w_gate, ffn_w_up, ffn_w_down, moe_router, moe_w_gate, moe_w_up, moe_w_down):
    rows = x.shape[1] // GRID_W
    h_lat, h_ctx = x, ctx
    for i in range(DEPTH):
        last = i == DEPTH - 1
        kind, j = i % N_MIXERS, i // N_MIXERS
        sh_m, sc_m, g_m, sh_f, sc_f, g_f = ada_params(c, ada_w[i], ada_b[i])
        csh_m, csc_m, cg_m, csh_f, csc_f, cg_f = ada_params(c_ctx, ada_w[i], ada_b[i])

        u_lat = modulate(rms_norm(h_lat, norm_mix[i]), sh_m, sc_m)
        u_ctx = modulate(rms_norm(h_ctx, norm_mix[i]), csh_m, csc_m)
        if kind == 0:
            y_lat, y_ctx = s5_mixer(u_lat, u_ctx, s5_lambda_re[j], s5_lambda_im[j], s5_log_step[j],
                                    s5_b_re[j], s5_b_im[j], s5_c_re[j], s5_c_im[j],
                                    s5_d[j], s5_glu_w[j], s5_glu_b[j], need_ctx=not last)
        elif kind == 1:
            y_lat = pool_mixer(u_lat, rows, GRID_W, pool_w[j], pool_b[j], pool_scale[j])
            y_ctx = None if last else pool_mixer(u_ctx, 1, u_ctx.shape[1], pool_w[j], pool_b[j], pool_scale[j])
        else:
            y_lat = fourier_mixer(u_lat, fnet_w[j], fnet_b[j])
            y_ctx = None if last else fourier_mixer(u_ctx, fnet_w[j], fnet_b[j])
        h_lat = h_lat + g_m * y_lat
        if not last:
            h_ctx = h_ctx + cg_m * y_ctx

        k = i // 2
        if i % 2 == 0:
            ffn = lambda h: swiglu(h, ffn_w_gate[k], ffn_w_up[k], ffn_w_down[k])
        else:
            ffn = lambda h: moe_swiglu(h, moe_router[k], moe_w_gate[k], moe_w_up[k], moe_w_down[k])
        h_lat = h_lat + g_f * ffn(modulate(rms_norm(h_lat, norm_ffn[i]), sh_f, sc_f))
        if not last:
            h_ctx = h_ctx + cg_f * ffn(modulate(rms_norm(h_ctx, norm_ffn[i]), csh_f, csc_f))
    return rms_norm(h_lat, norm_final)


_drawn_inputs = setup_inputs


def setup_inputs(seed=0):
    import zlib

    import numpy as np

    out = dict(_drawn_inputs(seed))
    spreads = {}
    factors = {'ctx': 47.624,
     'c_ctx': 8.0,
     's5_lambda_re': 64.0,
     's5_lambda_im': 4.092,
     's5_log_step': 3.841,
     's5_b_re': 14.308,
     's5_b_im': 6.515,
     's5_c_re': 13.537,
     's5_c_im': 6.006,
     's5_glu_b': 35.964,
     'pool_b': 6.383}
    for name, (base, spread) in spreads.items():
        noise = np.random.default_rng([zlib.crc32(name.encode()), seed]).standard_normal(out[name].shape)
        drawn = base * np.exp(spread * noise) if base else spread * noise
        out[name] = __import__('jax').numpy.asarray(drawn.astype(out[name].dtype))
    for name, factor in factors.items():
        out[name] = (out[name] * factor).astype(out[name].dtype)
    return out
```

```python
import concourse.bass as bass
from concourse import mybir
from contextlib import ExitStack

P = 128
D = 1024
SEQ = 256
TT = SEQ // P
KT = D // P
GROUPS, GW, NST = 64, 16, 64
CH = 8
NCH = SEQ // CH
HG = GROUPS // 2
BG = 8
NMOD = 6
DFF = 2816
FC0 = 256
NF0 = DFF // FC0
NE = 8
DFE = 3584
FC1 = 512
NF1 = DFE // FC1
NSLOT = 7
SLOT = 4096
NADA = 3
EPS = 1e-6
SQ = 6
ORD = 7


def build(nc, x_in, ctx_in, cond_in, ada_w, ada_b, norm_mix, norm_ffn, norm_final,
          lam_re, lam_im, log_step, b_re, b_im, c_re, c_im, d_skip, glu_w, glu_b,
          pool_w, pool_b, pool_scale, w_gate, w_up, w_down, router, e_gate, e_up, e_down,
          consts, pool_mat, out):
    F32, I32 = mybir.dt.float32, mybir.dt.int32
    ALU, ACT, AX = mybir.AluOpType, mybir.ActivationFunctionType, mybir.AxisListType
    MUL, ADD, SUB = ALU.mult, ALU.add, ALU.subtract

    mod_d = nc.dram_tensor("mod_scratch", (2, 2, NMOD * D), F32).ap()
    u_d = nc.dram_tensor("u_scratch", (GROUPS, GW, CH, 2 * NCH), F32).ap()
    t_d = nc.dram_tensor("kernel_scratch", (GROUPS, GW, 240), F32).ap()
    z_d = nc.dram_tensor("z_scratch", (CH, GW, GROUPS, NCH), F32).ap()

    ctx = ExitStack()
    with ctx:
        mem = ctx.enter_context(nc.sbuf_tensor("mem", [P, 52980], F32))
        sems = {}

        def S(name):
            if name not in sems:
                sems[name] = ctx.enter_context(nc.semaphore(name))
            return sems[name]

        def at(o, *dims):
            n = 1
            for d in dims:
                n *= d
            v = mem[:, o:o + n]
            if len(dims) == 1:
                return v
            names = "abcd"[:len(dims)]
            return v.rearrange(f"p ({' '.join(names)}) -> p {' '.join(names)}", **{k: d for k, d in zip(names, dims)})

        ident, tri, ones, iota = (at(i * P, P) for i in range(4))
        hlat = at(512, TT, D)
        flag_i = ctx.enter_context(nc.sbuf_tensor("flag", [P, 8], I32))
        small = at(2560, P)
        BASE = 2560 + P
        o = [BASE]

        def take(*dims):
            n = 1
            for d in dims:
                n *= d
            o[0] += n
            return at(o[0] - n, *dims)

        G_re = take(HG, CH, GW)
        G_nim = take(HG, CH, GW)
        E_off = o[0]
        E_sb = take(2, BG, 2, P)
        b_raw = at(E_off, 2, GROUPS, GW)
        e_off = o[0]
        e_sb = take(2 * NCH, 2, HG)
        bc = at(e_off, 4, D)
        U_off = o[0]
        U_sb = take(GROUPS, 2 * NCH)
        tmp = at(U_off, 32, GROUPS)
        M_off = o[0]
        M_sb = take(2, BG, P)
        S_rhs = take(2, HG, NCH)
        ut = at(M_off, 2, TT, D)
        P_re = take(BG, CH, GW)
        P_im = take(BG, CH, GW)
        C_sb = take(2, GROUPS, GW)
        Bp_sb = take(2, GROUPS, GW)
        Bb_sb = take(2, GROUPS + 1, GW)
        pw = take(4, GROUPS, CH)
        T_sb = take(4, 2, 240)
        DU_off = o[0]
        DU = take(HG, NCH)
        y_sb = take(HG, NCH)
        stage = at(DU_off, 4, 512)
        N_off = o[0]
        tmpP = take(BG, CH, GW)
        tmpG = take(BG, CH, GW)
        Npow = at(N_off, CH + 1, 2, GROUPS)
        LT = take(2, 2, GROUPS)
        sc4 = take(2, 2, HG)
        sc2 = take(2, HG)
        D_sb = take(GROUPS)
        adab = take(2, 512)
        mod_sb = take(512)
        cs = take(2, KT, 2)
        assert o[0] <= 52980 - NADA * 2048, o[0]
        ring_a = at(52980 - NADA * 2048, NADA, 2048)
        glu_sb = at(44788, KT, D)
        o = [BASE]
        poolw = take(4, 2, 256)
        poolP = take(4, TT, SEQ)
        xT = take(KT, SEQ)
        u_tok = take(TT, D)
        acc = take(TT, D)
        bd = take(4, D)
        xgT = take(KT, P)
        h_sb = take(2, 512)
        sg = take(512)
        hT = take(4, P)
        Ysb = take(D)
        sel = take(TT, P)
        selT = take(TT, P)
        rt_sb = take(KT, NE)
        rb = take(40, TT, NE)
        rankx = take(TT, 2 * NE + 1)
        combx = take(TT, 2 * NE + 2)
        zT = xT
        z_tok = acc
        RING = 52980 - NSLOT * SLOT
        assert o[0] <= RING, o[0]
        slots = [mem[:, RING + i * SLOT:RING + (i + 1) * SLOT] for i in range(NSLOT)]

        bank = [ctx.enter_context(nc.psum_tensor(f"bank{i}", [P, 512], F32)) for i in range(8)]

        def psum(i, *dims):
            v = bank[i][:, :]
            names = "abcd"[:len(dims)]
            return v.rearrange(f"p ({' '.join(names)}) -> p {' '.join(names)}", **{k: d for k, d in zip(names, dims)})

        for name in ("slot_full", "slot_used"):
            for i in range(NSLOT):
                S(f"{name}{i}")
        ada_full = [S(f"ada_full{i}") for i in range(NADA)]
        full = [S(f"slot_full{i}") for i in range(NSLOT)]
        used = [S(f"slot_used{i}") for i in range(NSLOT)]
        block = ctx.enter_context(nc.Block())

        ADA_UNITS = 2 * 3 * KT
        FFN_LOADS = [6, 6, 5, 5, 0, 0, 0]
        FFN_FULL = [6 * 32, 6 * 16, 5 * 32, 5 * 16, 0, 0, 0]

        @block.sync
        def _(sp):
            sp.dma_start(at(0, 4, P), consts).then_inc(S("consts_in"), 16)
            sp.dma_start(cs[:, 0], cond_in).then_inc(S("cond_in"), 16)
            for j, src in enumerate((lam_re, lam_im, log_step)):
                sp.dma_start(tmp[:, j], src).then_inc(S("lam_in"), 16)
            for j, src in enumerate((b_re, b_im)):
                sp.dma_start(b_raw[:, j], src).then_inc(S("b_in"), 16)
            for j, src in enumerate((c_re, c_im)):
                sp.dma_start(C_sb[:, j], src).then_inc(S("c_in"), 16)
            sp.dma_start(D_sb, d_skip).then_inc(S("d_in"), 16)
            sp.dma_start(hlat, x_in.rearrange("(t p) n -> p t n", p=P)).then_inc(S("x_in"), 16)
            sp.dma_start(ut[:, 1], ctx_in.rearrange("(t p) n -> p t n", p=P)).then_inc(S("x_in"), 16)
            for n in range(ADA_UNITS):
                l, r, k = n // (3 * KT), n // KT % 3, n % KT
                if n >= NADA:
                    sp.wait_ge(S("ada_used"), n - NADA + 1)
                sp.dma_start(ring_a[:, n % NADA], ada_w[l, k * P:(k + 1) * P, r * 2048:(r + 1) * 2048]).then_inc(ada_full[n % NADA], 16)
            sp.wait_ge(S("ada_used"), ADA_UNITS)
            sp.wait_ge(S("y_done"), 2)
            sp.dma_start(glu_sb, glu_w.rearrange("(k p) n -> p k n", p=P)).then_inc(S("glu_in"), 16)
            sp.wait_ge(S("z_out"), 32)
            sp.dma_start(poolw, pool_w.rearrange("g (k p) n -> p g k n", p=P)).then_inc(S("pool_in"), 16)
            sp.dma_start(poolP, pool_mat).then_inc(S("pool_in"), 16)
            sp.dma_start(rt_sb, router.rearrange("(k p) n -> p k n", p=P)).then_inc(S("pool_in"), 16)
            gate_v = w_gate.rearrange("(k p) n -> p k n", p=P)
            up_v = w_up.rearrange("(k p) n -> p k n", p=P)

            def ffn_load(c, src_c, w):
                gu, dn = 2 * (c % 2), 2 * (c % 2) + 1
                if w is not None:
                    sp.wait_ge(used[gu], w)
                for j, v in enumerate((gate_v, up_v)):
                    sp.dma_start(slots[gu][:, j * 2048:(j + 1) * 2048].rearrange("p (k n) -> p k n", k=KT),
                                 v[:, :, bass.ds(src_c * FC0, FC0)]).then_inc(full[gu], 16)
                if w is not None:
                    sp.wait_ge(used[dn], w)
                sp.dma_start(slots[dn][:, 0:2048].rearrange("p (f n) -> p f n", f=2),
                             w_down[bass.ds(src_c * FC0, FC0), :].rearrange("(f p) n -> p f n", p=P)).then_inc(full[dn], 16)

            ffn_load(0, 0, None)
            ffn_load(1, 1, None)
            with sp.Fori(1, NF0 // 2) as i:
                ffn_load(0, 2 * i, i)
                ffn_load(1, 2 * i + 1, i)
            ffn_load(0, NF0 - 1, NF0 // 2)

            def experts(first):
                def body(i):
                    e = i if first == 0 else i - first
                    for c in range(NF1):
                        cols = slice(c * FC1, (c + 1) * FC1)
                        for j, v in enumerate((e_gate, e_up, e_down)):
                            u = 3 * c + j
                            s = u % NSLOT
                            sp.wait_ge(used[s], FFN_LOADS[s] + i * 3 + u // NSLOT)
                            if j < 2:
                                src = v[bass.ds(e, 1), :, cols].rearrange("o (k p) n -> p (o k) n", p=P)
                                dst = slots[s].rearrange("p (k n) -> p k n", k=KT)
                            else:
                                src = v[bass.ds(e, 1), cols, :].rearrange("o (f p) n -> p (o f) n", p=P)
                                dst = slots[s].rearrange("p (f n) -> p f n", f=4)
                            sp.dma_start(dst, src).then_inc(full[s], 16)
                return body

            def first_expert():
                for c in range(NF1):
                    cols = slice(c * FC1, (c + 1) * FC1)
                    for j, v in enumerate((e_gate, e_up, e_down)):
                        u = 3 * c + j
                        s = u % NSLOT
                        n = FFN_LOADS[s] + u // NSLOT
                        if n:
                            sp.wait_ge(used[s], n)
                        if s >= 5 and u < NSLOT:
                            sp.wait_ge(S("glu_done"), 1)
                        if j < 2:
                            src = v[0, :, cols].rearrange("(k p) n -> p k n", p=P)
                            dst = slots[s].rearrange("p (k n) -> p k n", k=KT)
                        else:
                            src = v[0, cols, :].rearrange("(f p) n -> p f n", p=P)
                            dst = slots[s].rearrange("p (f n) -> p f n", f=4)
                        sp.dma_start(dst, src).then_inc(full[s], 16)

            first_expert()
            with sp.Fori(1, NE) as i:
                experts(0)(i)
            sp.wait_ge(S("overflow_known"), 1)
            more = sp.value_load(flag_i[0:1, 0:1], min_val=0, max_val=1)
            with sp.If(more):
                with sp.Fori(NE, 2 * NE) as i:
                    experts(NE)(i)

        @block.gpsimd
        def _(pool):
            def g_table(b):
                g0, q = b * BG, b % 4
                G = slice(g0, g0 + BG)
                Cr, Ci = (C_sb[:, j, G].unsqueeze(2).to_broadcast([P, BG, CH, GW]) for j in range(2))
                W = [pw[:, j, G].unsqueeze(3).to_broadcast([P, BG, CH, GW]) for j in range(4)]
                if b >= 4:
                    pool.wait_ge(S("y_done"), 1)
                gr, gi = (t[:, q * BG:(q + 1) * BG] for t in (G_re, G_nim))
                k = 6 * b
                nc.gpsimd.tensor_tensor(gr, Cr, W[0], MUL).then_inc(S("g_chain"), 1)
                nc.gpsimd.tensor_tensor(tmpG, Ci, W[2], MUL).then_inc(S("g_chain"), 1)
                pool.wait_ge(S("g_chain"), k + 2)
                nc.gpsimd.tensor_tensor(gr, gr, tmpG, ADD).then_inc(S("g_chain"), 1)
                nc.gpsimd.tensor_tensor(gi, Cr, W[2], MUL).then_inc(S("g_chain"), 1)
                pool.wait_ge(S("g_chain"), k + 4)
                nc.gpsimd.tensor_tensor(tmpG, Ci, W[3], MUL).then_inc(S("g_chain"), 1)
                pool.wait_ge(S("g_chain"), k + 5)
                nc.gpsimd.tensor_tensor(gi, gi, tmpG, ADD).then_inc(S("g_chain"), 1)
                pool.wait_ge(S("g_chain"), k + 6)

            pool.wait_ge(S("pw_ready"), 1)
            pool.wait_ge(S("c_in"), 32)
            for b in range(8):
                g_table(b)

        @block.scalar
        def _(act):
            def copy(dst, src, name, n=1):
                nc.scalar.activation(dst, src, ACT.Copy).then_inc(S(name), n)

            act.wait_ge(S("cond_in"), 16)
            nc.scalar.activation(cs[:, 1], cs[:, 0], ACT.Silu).then_inc(S("cond_silu"), 1)
            act.wait_ge(S("lam_in"), 48)
            nc.scalar.activation(tmp[:, 3], tmp[:, 2], ACT.Exp).then_inc(S("step_exp"), 1)

            def squares(src, junk, where, name):
                for t in range(TT):
                    nc.scalar.activation(junk[:, t], src[:, t], ACT.Square, accum_out=where[:, t:t + 1]).then_inc(S(name), 1)

            act.wait_ge(S("x_in"), 32)
            squares(hlat, bc[:, 0:2], small[:, 0:2], "sq0")
            squares(ut[:, 1], bc[:, 2:4], small[:, 2:4], "sq0")

            def mod_bias(n):
                l, r = n // 3, n % 3
                for q in range(4):
                    act.dma_start(adab[32 * q:32 * q + 2, n % 2],
                                  ada_b[l:l + 1, r * 2048 + q * 512:r * 2048 + (q + 1) * 512].to_broadcast([2, 512])).then_inc(S(f"adab_in{n % 2}"), 16)

            def mod_out(n):
                l, r = n // 3, n % 3
                act.wait_ge(S("mod_sb_full"), 4 * (n + 1))
                for q in range(4):
                    act.dma_start(mod_d[l, :, r * 2048 + q * 512:r * 2048 + (q + 1) * 512],
                                  mod_sb[32 * q:32 * q + 2, :]).then_inc(S("mod_out"), 16)
                if n + 2 < 6:
                    mod_bias(n + 2)

            def rows(dst, src, name):
                act.dma_start(dst, src.to_broadcast([P, D])).then_inc(S(name), 16)

            mod_bias(0)
            mod_bias(1)
            act.wait_ge(S("ms0"), 1)
            nc.scalar.activation(small[:, 4:8], small[:, 4:8], ACT.Sqrt).then_inc(S("rt0"), 1)
            mod_out(0)
            act.wait_ge(S("mod_out"), 64)
            act.wait_ge(S("sq0"), 4)
            rows(bc[:, 0], mod_d[0, 0:1, 0:D], "bc_in")
            rows(bc[:, 1], mod_d[0, 0:1, D:2 * D], "bc_in")
            rows(bc[:, 2], mod_d[0, 1:2, 0:D], "bc_in")
            rows(bc[:, 3], mod_d[0, 1:2, D:2 * D], "bc_in")
            rows(at(DU_off, D), norm_mix[0:1, :], "bc_in")

            def p_evac(b):
                if b >= 2:
                    act.wait_ge(S("e_done"), b - 1)
                for j in range(4):
                    n = 4 * b + j
                    act.wait_ge(S("pt_done"), n + 1)
                    nc.scalar.activation(E_sb[:, b % 2, 2 * j:2 * j + 2], psum(2 + n % 2, 2, 2, P), ACT.Copy).then_inc(S("pt_out"), 1)

            def u_evac():
                for k in range(KT):
                    act.wait_ge(S("ut_done"), k + 1)
                    if k >= 4:
                        act.wait_ge(S(f"u_out{k % 4}"), 16 * (k // 4))
                    if k == 0:
                        act.wait_ge(S("u_ready"), 4)
                    nc.scalar.activation(stage[:, k % 4].rearrange("p (b s a) -> p s b a", b=CH, s=2),
                                         psum(2 + k % 2, 2, CH, NCH), ACT.Copy).then_inc(S("ut_out"), 1)
                    act.wait_ge(S("ut_out"), k + 1)
                    act.dma_start(u_d[k * 8:(k + 1) * 8].rearrange("g h b a -> (g h) (b a)"), stage[:, k % 4]).then_inc(S(f"u_out{k % 4}"), 16)
                for k in range(4):
                    act.wait_ge(S(f"u_out{k}"), 16 * KT // 4)
                for c in range(CH):
                    act.dma_start(U_sb[c * GW:(c + 1) * GW], u_d[:, :, CH - 1 - c, :].rearrange("g h a -> h g a")).then_inc(S("U_in"), 16)

            def du_in(h):
                for b in range(CH):
                    act.dma_start(DU[b * GW:(b + 1) * GW],
                                  u_d[h * HG:(h + 1) * HG, :, b, NCH:2 * NCH].rearrange("g h a -> h g a")).then_inc(S("du_in"), 16)

            def e_evac(b):
                q = b % 4
                if b == 4:
                    act.wait_ge(S("srhs_done"), 2)
                for j in range(2):
                    n = 2 * b + j
                    act.wait_ge(S("e_bank"), n + 1)
                    src = psum(6 + j, 4, 2, 2 * NCH)
                    dst = e_sb.rearrange("p i r g -> p g r i")[:, q * BG + 4 * j:q * BG + 4 * j + 4]
                    nc.scalar.activation(dst[0:64], src[0:64], ACT.Copy).then_inc(S("e_out"), 1)
                    for s in range(2):
                        back = src[64:P, :, :, s * NCH:(s + 1) * NCH][:, :, :, ::-1]
                        nc.scalar.activation(dst[64:P, :, :, s * NCH:(s + 1) * NCH], back, ACT.Copy).then_inc(S("e_out"), 1)

            def kernels_to_dram(h):
                act.wait_ge(S("T_ready"), 12 * (h + 1))
                for q in range(4):
                    act.dma_start(t_d[h * HG + q:(h + 1) * HG:4].rearrange("m h n -> h m n"),
                                  T_sb[32 * q:32 * q + GW].rearrange("p b j n -> p (b j) n")).then_inc(S("t_out"), 16)
                act.wait_ge(S("t_out"), 64 * (h + 1))

            def toeplitz_in(b):
                if b >= 2:
                    act.wait_ge(S("m_done"), b)
                for c in range(CH):
                    act.dma_start(M_sb[c * GW:(c + 1) * GW].rearrange("p b g n -> p (b g) n"),
                                  t_d[b * BG:(b + 2) * BG, :, c * GW:c * GW + P].rearrange("g h n -> h g n")).then_inc(S("M_in"), 16)

            def s_copy():
                src = e_sb[:, NCH - 1:2 * NCH - 1].rearrange("p i r g -> p r g i")
                nc.scalar.activation(S_rhs[0:64], src[0:64], ACT.Copy).then_inc(S("srhs_done"), 1)
                nc.scalar.activation(S_rhs[64:P], src[64:P][:, :, :, ::-1], ACT.Copy).then_inc(S("srhs_done"), 1)

            def y_gelu(h):
                act.wait_ge(S("y_ready"), 2 * (h + 1))
                if h == 0:
                    du_in(1)
                nc.scalar.activation(y_sb, y_sb, ACT.Gelu_apprx_tanh).then_inc(S("z_ready"), 1)
                act.wait_ge(S("z_ready"), h + 1)
                act.dma_start(z_d[:, :, h * HG:(h + 1) * HG, :].rearrange("b h g a -> (b h) g a"), y_sb).then_inc(S("z_out"), 16)

            p_evac(0)
            p_evac(1)
            u_evac()
            du_in(0)
            mod_out(1)
            for b in range(4):
                if b >= 2:
                    p_evac(b)
                e_evac(b)
            mod_out(2)
            kernels_to_dram(0)
            toeplitz_in(0)
            mod_out(3)
            toeplitz_in(2)
            mod_out(4)
            act.wait_ge(S("scan_done"), 1)
            s_copy()
            y_gelu(0)
            mod_out(5)
            for b in range(4, 8):
                p_evac(b)
                e_evac(b)
            kernels_to_dram(1)
            toeplitz_in(4)
            toeplitz_in(6)
            act.wait_ge(S("scan_done"), 2)
            s_copy()
            y_gelu(1)

            act.wait_ge(S("z_out"), 32)
            for g in range(8):
                act.dma_start(zT[g * GW:(g + 1) * GW].rearrange("h k (b a) -> h k b a", b=CH),
                              z_d.rearrange("b h (k g) a -> g h k b a", g=8)[g]).then_inc(S("zT_in"), 16)
            act.wait_ge(S("mod_out"), 6 * 64)
            rows(bd[:, 0], glu_b, "bd_in")
            rows(bd[:, 1], mod_d[0, 0:1, 2 * D:3 * D], "bd_in")
            rows(bd[:, 2], mod_d[0, 0:1, 4 * D:5 * D], "bd_in")
            rows(bd[:, 3], norm_ffn[0:1, :], "bd_in")
            for j in range(4):
                act.wait_ge(S("zt_done"), j + 1)
                nc.scalar.activation(z_tok.rearrange("p t (c n) -> p (t c) n", c=2)[:, j], bank[j % 2][:, :], ACT.Copy).then_inc(S("zt_out"), 1)
            for j in range(4):
                act.wait_ge(S("gate_in"), j + 1)
                v = u_tok.rearrange("p t (c n) -> p (t c) n", c=2)[:, j]
                nc.scalar.activation(v, v, ACT.Sigmoid).then_inc(S("sigm"), 1)
            act.wait_ge(S("h1"), 1)
            squares(hlat, u_tok, small[:, 8:10], "sq1")
            act.wait_ge(S("ms1"), 1)
            nc.scalar.activation(small[:, 8:10], small[:, 8:10], ACT.Sqrt).then_inc(S("rt1"), 1)
            rows(bd[:, 0], mod_d[0, 0:1, 3 * D:4 * D], "bd_in")
            rows(bd[:, 1], mod_d[0, 0:1, 5 * D:6 * D], "bd_in")

            def xT_evac(base, bks):
                for j in range(4):
                    act.wait_ge(S("xt_done"), base + j + 1)
                    nc.scalar.activation(xT[:, 2 * j:2 * j + 2], psum(bks[j % 2], 2, SEQ), ACT.Copy).then_inc(S("xt_out"), 1)

            xT_evac(0, (0, 1))

            def ffn_act(c):
                act.wait_ge(S("f_gate"), c + 1)
                if not (isinstance(c, int) and c == 0):
                    act.wait_ge(S("f_h"), c)
                nc.scalar.activation(sg, bank[4][:, :], ACT.Silu).then_inc(S("f_silu"), 1)

            def ffn_hT(c):
                act.wait_ge(S("f_tr"), c + 1)
                if not (isinstance(c, int) and c == 0):
                    act.wait_ge(S("f_down"), c)
                nc.scalar.activation(hT, psum(6, 4, P), ACT.Copy).then_inc(S("f_hT"), 1)

            ffn_act(0)
            ffn_act(1)
            ffn_hT(0)
            with act.Fori(2, NF0) as c:
                ffn_act(c)
                ffn_hT(c - 1)
            ffn_hT(NF0 - 1)

            act.wait_ge(S("h2"), 1)
            squares(hlat, u_tok, small[:, 12:14], "sq2")
            act.wait_ge(S("ms2"), 1)
            nc.scalar.activation(small[:, 12:14], small[:, 12:14], ACT.Sqrt).then_inc(S("rt2"), 1)
            rows(bd[:, 0], mod_d[1, 0:1, 0:D], "bd_in")
            rows(bd[:, 1], mod_d[1, 0:1, D:2 * D], "bd_in")
            rows(bd[:, 2], mod_d[1, 0:1, 2 * D:3 * D], "bd_in")
            rows(bd[:, 3], norm_mix[1:2, :], "bd_in")
            xT_evac(4, (0, 1))
            act.wait_ge(S("u2_ready"), 1)
            rows(bd[:, 0], pool_b, "bd_in")
            rows(bd[:, 1], pool_scale, "bd_in")
            act.wait_ge(S("h3"), 1)
            squares(hlat, u_tok, small[:, 16:18], "sq3")
            act.wait_ge(S("ms3"), 1)
            nc.scalar.activation(small[:, 16:18], small[:, 16:18], ACT.Sqrt).then_inc(S("rt3"), 1)
            rows(bd[:, 0], mod_d[1, 0:1, 3 * D:4 * D], "bd_in")
            rows(bd[:, 1], mod_d[1, 0:1, 4 * D:5 * D], "bd_in")
            rows(bd[:, 2], mod_d[1, 0:1, 5 * D:6 * D], "bd_in")
            rows(bd[:, 3], norm_ffn[1:2, :], "bd_in")
            xT_evac(8, (0, 1))
            act.wait_ge(S("top2"), 1)
            nc.scalar.activation(small[:, 24:26], small[:, 22:24], ACT.Exp).then_inc(S("top_exp"), 1)
            act.wait_ge(S("u3_ready"), 1)
            rows(bd[:, 3], norm_final, "bd_in")

            def gather_out(half, n):
                act.wait_ge(S(f"gather{half}"), n)
                nc.scalar.activation(xgT[:, 4 * half:4 * half + 4], psum(7, 4, P), ACT.Copy).then_inc(S(f"gather_out{half}"), 1)

            def expert(i, k):
                def silu(c):
                    act.wait_ge(S("x_gate"), i * NF1 + c + 1)
                    if not (isinstance(i, int) and i == 0 and c == 0):
                        act.wait_ge(S("x_h"), i * NF1 + c)
                    nc.scalar.activation(sg, bank[c % 2][:, :], ACT.Silu).then_inc(S("x_silu"), 1)

                def hTs(c):
                    act.wait_ge(S("x_tr"), i * NF1 + c + 1)
                    if not (isinstance(i, int) and i == 0 and c == 0):
                        act.wait_ge(S("x_down"), i * NF1 + c)
                    nc.scalar.activation(hT, psum(6, 4, P), ACT.Copy).then_inc(S("x_hT"), 1)

                silu(0)
                for c in range(1, NF1):
                    silu(c)
                    hTs(c - 1)
                    if c == 2:
                        act.wait_ge(S("seltr"), i + 1)
                        nc.scalar.activation(selT, bank[7][:, 0:2 * P].rearrange("p (t n) -> p t n", t=2), ACT.Copy).then_inc(S("selT_out"), 1)
                hTs(NF1 - 1)
                gather_out(0, i + 2)
                gather_out(1, i + 2)
                act.wait_ge(S("x_down"), (i + 1) * NF1)
                act.wait_ge(S("scat_pe"), i * 4 + 4 + 4 * k)
                for j in range(2):
                    nc.scalar.activation(Ysb[:, j * 512:(j + 1) * 512], bank[4 + j][:, :], ACT.Copy).then_inc(S("Y_out"), 1)

            gather_out(0, 1)
            gather_out(1, 1)
            expert(0, 0)
            with act.Fori(1, NE) as i:
                expert(i, 0)
            act.wait_ge(S("overflow_known"), 1)
            more = act.value_load(flag_i[0:1, 0:1], min_val=0, max_val=1)
            with act.If(more):
                with act.Fori(NE, 2 * NE) as i:
                    expert(i, 1)
            act.wait_ge(S("h4"), 1)
            squares(hlat, u_tok, small[:, 32:34], "sq4")
            act.wait_ge(S("ms4"), 1)
            nc.scalar.activation(small[:, 32:34], small[:, 32:34], ACT.Sqrt).then_inc(S("rt4"), 1)
            for t in range(TT):
                act.wait_ge(S("result"), t + 1)
                act.dma_start(out[t * P:(t + 1) * P, :], u_tok[:, t]).then_inc(S("out_done"), 16)
            act.wait_ge(S("out_done"), 32)

        @block.tensor
        def _(pe):
            mm, tr = nc.tensor.matmul, nc.tensor.transpose

            def ada_round(n):
                if n == 0:
                    pe.wait_ge(S("cond_silu"), 1)
                if n >= 2:
                    pe.wait_ge(S("mod_sb_full"), 4 * (n - 1))
                for k in range(KT):
                    u = n * KT + k
                    pe.wait_ge(ada_full[u % NADA], 16 * (u // NADA + 1))
                    for q in range(4):
                        ins = mm(bank[n % 2][32 * q:32 * q + 2, :], cs[:, 1, k], ring_a[:, u % NADA, q * 512:(q + 1) * 512],
                                 start=k == 0, stop=k == KT - 1, tile_position=(0, 32 * q), skip_group_check=True)
                    ins.then_inc(S("ada_used"), 1)

            def p_transpose(b):
                pe.wait_ge(S("P_ready"), b + 1)
                for j in range(4):
                    n = 4 * b + j
                    if n >= 2 and b == 0 or b > 0:
                        pe.wait_ge(S("pt_out"), n - 1)
                    if b == 2 and j == 0:
                        pe.wait_ge(S("ut_out"), KT)
                    for i in range(4):
                        g, t = 2 * j + i // 2, (P_re, P_im)[i % 2]
                        ins = tr(psum(2 + n % 2, 4, P)[:, i], t[:, g].rearrange("p k h -> p (k h)"), ident)
                    ins.then_inc(S("pt_done"), 1)

            def u_transpose():
                pe.wait_ge(S("u_ready"), 4)
                pe.wait_ge(S("pt_out"), 8)
                for k in range(KT):
                    if k >= 2:
                        pe.wait_ge(S("ut_out"), k - 1)
                    for i in range(4):
                        ins = tr(psum(2 + k % 2, 4, P)[:, i], ut[:, 1 - i // 2, i % 2, k * P:(k + 1) * P], ident)
                    ins.then_inc(S("ut_done"), 1)

            def e_matmul(b):
                pe.wait_ge(S("U_in"), 16 * CH)
                pe.wait_ge(S("pt_out"), 4 * (b + 1))
                for j in range(2):
                    if b >= 1:
                        pe.wait_ge(S("e_out"), 3 * (2 * (b - 1) + j + 1))
                    for i in range(8):
                        g, r = 4 * j + i // 2, i % 2
                        ins = mm(psum(6 + j, 8, 2 * NCH)[:, i], E_sb[:, b % 2, g, r], U_sb[:, b * BG + g], start=True, stop=True)
                    ins.then_inc(S("e_bank"), 1)
                    if j:
                        pe.wait_ge(S("e_bank"), 2 * (b + 1))
                        pe.sem_inc(S("e_done"), 1)

            def kernels(b):
                pe.wait_ge(S("g_chain"), 6 * (b + 1))
                if b >= 1:
                    pe.wait_ge(S("T_ready"), 3 * b)
                if b == 4:
                    pe.wait_ge(S("yi_out"), 4)
                for d in range(2):
                    rows = slice(64 * d, 64 * d + 64)
                    for g in range(BG):
                        q, j = g % 4, g // 4
                        lhs = [Bb_sb[rows, r, b * BG + g:b * BG + g + 2].rearrange("p g h -> p (g h)") for r in range(2)]
                        dst = psum(4 + d, 4, P)[32 * q:32 * q + 32, j]
                        for r, t in enumerate((G_re, G_nim)):
                            ins = mm(dst, lhs[r], t[rows, b % 4 * BG + g].rearrange("p k h -> p (k h)"),
                                     start=r == 0, stop=r == 1, tile_position=(64 * d, 32 * q), skip_group_check=True)
                ins.then_inc(S("tk_done"), 1)

            def inside(b):
                pe.wait_ge(S("M_in"), 16 * CH * (b // 2 + 1))
                pe.wait_ge(S("T_ready"), 3 * (b // 4 * 4 + 4))
                if b >= 2:
                    pe.wait_ge(S("yi_out"), b - 1)
                for g in range(BG):
                    ins = mm(psum(4 + b % 2, 16, NCH)[:, g], M_sb[:, b % 2, g], U_sb[:, b * BG + g, NCH:2 * NCH], start=True, stop=True)
                ins.then_inc(S("m_done"), 1)

            def from_states(h):
                pe.wait_ge(S("srhs_done"), 2 * (h + 1))
                if h:
                    pe.wait_ge(S("y_ready"), 2)
                for g in range(HG):
                    for r, t in enumerate((G_re, G_nim)):
                        ins = mm(psum(6 + g // 16, 16, NCH)[:, g % 16], t[:, g].rearrange("p k h -> p (k h)"), S_rhs[:, r, g],
                                 start=r == 0, stop=r == 1)
                ins.then_inc(S("y_done"), 1)

            pe.wait_ge(S("consts_in"), 16)
            ada_round(0)
            p_transpose(0)
            p_transpose(1)
            u_transpose()
            ada_round(1)
            for b in range(4):
                if b >= 2:
                    p_transpose(b)
                e_matmul(b)
            ada_round(2)
            ada_round(3)
            for b in range(4):
                kernels(b)
            inside(0)
            inside(1)
            ada_round(4)
            inside(2)
            inside(3)
            from_states(0)
            ada_round(5)
            for b in range(4, 8):
                p_transpose(b)
                e_matmul(b)
            for b in range(4, 8):
                kernels(b)
            for b in range(4, 8):
                inside(b)
            from_states(1)

            pe.wait_ge(S("zT_in"), 128)
            for j in range(4):
                t, c = j // 2, j % 2
                if j == 0:
                    pe.wait_ge(S("mod_sb_full"), 24)
                if j >= 2:
                    pe.wait_ge(S("zt_out"), j - 1)
                for k in range(4):
                    ins = tr(psum(j % 2, 4, P)[:, k], zT[:, 4 * c + k, t * P:(t + 1) * P], ident)
                ins.then_inc(S("zt_done"), 1)
            pe.wait_ge(S("glu_in"), 16)
            pe.wait_ge(S("y_ready"), 4)
            for j in range(4):
                t, c = j // 2, j % 2
                for k in range(KT):
                    ins = mm(bank[4 + j][:, :], zT[:, k, t * P:(t + 1) * P], glu_sb[:, k, c * 512:(c + 1) * 512],
                             start=k == 0, stop=k == KT - 1)
                ins.then_inc(S("glu_pe"), 1)

            def x_transpose(base):
                for j in range(4):
                    if j >= 2:
                        pe.wait_ge(S("xt_out"), base + j - 1)
                    for i in range(4):
                        ins = tr(psum(j % 2, 4, P)[:, i], u_tok[:, i % 2, (2 * j + i // 2) * P:(2 * j + i // 2 + 1) * P], ident)
                    ins.then_inc(S("xt_done"), 1)

            pe.wait_ge(S("u1_ready"), 2)
            x_transpose(0)
            pe.wait_ge(S("xt_out"), 4)

            def ffn_in(c, w, m):
                s = 2 * c
                for t in range(TT):
                    for k in range(KT):
                        ins = mm(bank[4 + w][:, t * FC0:(t + 1) * FC0], xT[:, k, t * P:(t + 1) * P],
                                 slots[s][:, w * 2048 + k * FC0:w * 2048 + (k + 1) * FC0], start=k == 0, stop=k == KT - 1)
                return ins

            def ffn_gate(c, p, m):
                pe.wait_ge(full[2 * p], 32 * m)
                if not (isinstance(c, int) and c == 0):
                    pe.wait_ge(S("f_silu"), c)
                ffn_in(p, 0, m).then_inc(S("f_gate"), 1)

            def ffn_up(c, p):
                if not (isinstance(c, int) and c == 0):
                    pe.wait_ge(S("f_h"), c)
                ins = ffn_in(p, 1, 0)
                ins.then_inc(S("f_up"), 1)
                pe.wait_ge(S("f_up"), c + 1)
                pe.sem_inc(used[2 * p], 1)

            def ffn_tr(c):
                pe.wait_ge(S("f_h"), c + 1)
                if not (isinstance(c, int) and c == 0):
                    pe.wait_ge(S("f_hT"), c)
                for i in range(4):
                    ins = tr(psum(6, 4, P)[:, i], h_sb[:, 0, (i % 2) * FC0 + (i // 2) * P:(i % 2) * FC0 + (i // 2 + 1) * P], ident)
                ins.then_inc(S("f_tr"), 1)

            def ffn_down(c, p, m, first=False, last=False):
                pe.wait_ge(full[2 * p + 1], 16 * m)
                pe.wait_ge(S("f_hT"), c + 1)
                for j in range(4):
                    t, n = j // 2, j % 2
                    for f in range(2):
                        ins = mm(bank[j][:, :], hT[:, 2 * f + t], slots[2 * p + 1][:, f * D + n * 512:f * D + (n + 1) * 512],
                                 start=first and f == 0, stop=last and f == 1)
                ins.then_inc(S("f_down"), 1)
                pe.wait_ge(S("f_down"), c + 1)
                pe.sem_inc(used[2 * p + 1], 1)

            ffn_gate(0, 0, 1)
            ffn_up(0, 0)
            ffn_gate(1, 1, 1)
            ffn_tr(0)
            ffn_up(1, 1)
            ffn_down(0, 0, 1, first=True)
            ffn_gate(2, 0, 2)
            ffn_tr(1)
            ffn_up(2, 0)
            ffn_down(1, 1, 1)
            with pe.Fori(1, NF0 // 2) as i:
                ffn_gate(2 * i + 1, 1, i + 1)
                ffn_tr(2 * i)
                ffn_up(2 * i + 1, 1)
                ffn_down(2 * i, 0, i + 1)
                ffn_gate(2 * i + 2, 0, i + 2)
                ffn_tr(2 * i + 1)
                ffn_up(2 * i + 2, 0)
                ffn_down(2 * i + 1, 1, i + 1)
            ffn_tr(NF0 - 1)
            ffn_down(NF0 - 1, 0, NF0 // 2 + 1, last=True)

            pe.wait_ge(S("u2_ready"), 1)
            pe.wait_ge(S("pool_in"), 48)
            for j in range(4):
                if j >= 2:
                    pe.wait_ge(S("xt_out"), 4 + j - 1)
                for i in range(2):
                    k = 2 * j + i
                    for t in range(TT):
                        ins = mm(psum(j % 2, 2, SEQ)[:, i], u_tok[:, t, k * P:(k + 1) * P], poolP[:, j, t], start=t == 0, stop=t == 1)
                ins.then_inc(S("xt_done"), 1)
            pe.wait_ge(S("xt_out"), 8)
            for t in range(TT):
                for g in range(4):
                    for k in range(2):
                        ins = mm(bank[4 + 2 * t + g // 2][:, (g % 2) * 256:(g % 2) * 256 + 256], xT[:, 2 * g + k, t * P:(t + 1) * P],
                                 poolw[:, g, k], start=k == 0, stop=k == 1)
            ins.then_inc(S("pool_pe"), 1)
            pe.wait_ge(S("u3_ready"), 1)
            x_transpose(8)
            pe.wait_ge(S("xt_out"), 12)
            for t in range(TT):
                for k in range(KT):
                    ins = mm(psum(2, 64, NE)[:, t], xT[:, k, t * P:(t + 1) * P], rt_sb[:, k], start=k == 0, stop=k == KT - 1)
            ins.then_inc(S("logits"), 1)
            pe.wait_ge(S("mask"), 1)
            M_ = rb[:, 8]
            mm(psum(3, 64, NE)[:, 0], tri, M_[:, 0], start=True, stop=True)
            mm(psum(3, 64, NE)[:, 1], ones, M_[:, 0], start=True, stop=False)
            mm(psum(3, 64, NE)[:, 1], tri, M_[:, 1], start=False, stop=True)
            mm(psum(3, 64, NE)[:, 2], ones, M_[:, 0], start=True, stop=False)
            mm(psum(3, 64, NE)[:, 2], ones, M_[:, 1], start=False, stop=True).then_inc(S("rank_pe"), 1)

            def gather(half, n, zero=False):
                if half == 0:
                    pe.wait_ge(S("sel_ready"), n)
                else:
                    pe.wait_ge(S("gather_out0"), n)
                for k in range(4):
                    for t in range(TT):
                        kk = 4 * half + k
                        ins = mm(psum(7, 4, P)[:, k], u_tok[:, t, kk * P:(kk + 1) * P], sel[:, t], start=t == 0, stop=t == 1)
                ins.then_inc(S(f"gather{half}"), 1)

            def scatter(r, n, y):
                if y is not None:
                    pe.wait_ge(S("Y_out"), y)
                if not (isinstance(n, int) and n == 0):
                    pe.wait_ge(S("scat_acc"), n)
                t, c = r // 2, r % 2
                mm(bank[7][:, :], selT[:, t], Ysb[:, c * 512:(c + 1) * 512], start=True, stop=True).then_inc(S("scat_pe"), 1)

            def expert(i, k):
                zero = isinstance(i, int) and i == 0

                def slot_of(c, j):
                    u = 3 * c + j
                    s = u % NSLOT
                    return s, FFN_FULL[s] + 16 * (3 * i + u // NSLOT + 1)

                def used_up(s, c, name):
                    pe.wait_ge(S(name), i * NF1 + c + 1)
                    pe.sem_inc(used[s], 1)

                def products(c, j):
                    s, v = slot_of(c, j)
                    pe.wait_ge(full[s], v)
                    back = 0 if c == 0 else 1
                    if not (zero and c - back <= 0):
                        pe.wait_ge(S(("x_silu", "x_h")[j]), i * NF1 + c - back)
                    for kk in range(KT):
                        ins = mm(bank[2 * j + c % 2][:, :], xgT[:, kk], slots[s][:, kk * FC1:(kk + 1) * FC1], start=kk == 0, stop=kk == KT - 1)
                    ins.then_inc(S(("x_gate", "x_up")[j]), 1)

                def trans(c):
                    pe.wait_ge(S("x_h"), i * NF1 + c + 1)
                    if not (zero and c == 0):
                        pe.wait_ge(S("x_hT"), i * NF1 + c)
                    for f in range(4):
                        ins = tr(psum(6, 4, P)[:, f], h_sb[:, 0, f * P:(f + 1) * P], ident)
                    ins.then_inc(S("x_tr"), 1)

                def down(c, fs):
                    s, v = slot_of(c, 2)
                    if fs[0] == 0:
                        pe.wait_ge(full[s], v)
                        pe.wait_ge(S("x_hT"), i * NF1 + c + 1)
                        if c == 0 and not zero:
                            pe.wait_ge(S("Y_out"), 2 * i)
                    for f in fs:
                        for n in range(2):
                            ins = mm(bank[4 + n][:, :], hT[:, f], slots[s][:, f * D + n * 512:f * D + (n + 1) * 512],
                                     start=c == 0 and f == 0, stop=c == NF1 - 1 and f == 3)
                    if fs[-1] == 3:
                        ins.then_inc(S("x_down"), 1)

                pe.wait_ge(S("gather_out1"), i + 1)
                for c in range(NF1):
                    products(c, 0)
                    if c < 2:
                        if zero:
                            pe.wait_ge(S("moe_init"), 1)
                        scatter(2 * c, i * 4 + 4 * k + 2 * c, None if zero else 2 * i)
                    if c == 2:
                        pe.wait_ge(S("scat_acc"), i * 4 + 4 * k + 4)
                        for t in range(TT):
                            ins = tr(bank[7][:, t * P:(t + 1) * P], sel[:, t], ident)
                        ins.then_inc(S("seltr"), 1)
                    if c:
                        trans(c - 1)
                    used_up(slot_of(c, 0)[0], c, "x_gate")
                    products(c, 1)
                    if c < 2:
                        scatter(2 * c + 1, i * 4 + 4 * k + 2 * c + 1, None)
                    if c:
                        down(c - 1, (0, 1, 2, 3))
                        used_up(slot_of(c - 1, 2)[0], c - 1, "x_down")
                    used_up(slot_of(c, 1)[0], c, "x_up")
                trans(NF1 - 1)
                pe.wait_ge(S("selT_out"), i + 1)
                gather(0, i + 2)
                down(NF1 - 1, (0, 1))
                gather(1, i + 2)
                down(NF1 - 1, (2, 3))
                used_up(slot_of(NF1 - 1, 2)[0], NF1 - 1, "x_down")

            gather(0, 1)
            gather(1, 1)
            expert(0, 0)
            with pe.Fori(1, NE) as i:
                expert(i, 0)
            for r in range(4):
                scatter(r, 4 * NE + r, 2 * NE)
            pe.wait_ge(S("overflow_known"), 1)
            more = pe.value_load(flag_i[0:1, 0:1], min_val=0, max_val=1)
            with pe.If(more):
                with pe.Fori(NE, 2 * NE) as i:
                    expert(i, 1)
                for r in range(4):
                    scatter(r, 8 * NE + 4 + r, 4 * NE)

        @block.vector
        def _(dve):
            V = nc.vector
            tt, ts, stt = V.tensor_tensor, V.tensor_scalar, V.scalar_tensor_tensor
            chain = [0]

            def link(ins, more=None):
                chain[0] += 1
                ins.then_inc(S("dve_chain"), 1)
                dve.wait_ge(S("dve_chain"), chain[0])

            dve.wait_ge(S("lam_in"), 48)
            dve.wait_ge(S("step_exp"), 1)
            V.memset(Bb_sb[:, :, GROUPS], 0.0)
            stt(tmp[:, 6], tmp[:, 0], 0.5 ** SQ, tmp[:, 3], MUL, MUL)
            link(stt(tmp[:, 7], tmp[:, 1], 0.5 ** SQ, tmp[:, 3], MUL, MUL))
            V.tensor_copy(tmp[:, 9], tmp[:, 6])
            ts(tmp[:, 8], tmp[:, 7], -1.0, None, MUL)
            V.memset(tmp[:, 10], 1.0)
            link(V.memset(tmp[:, 11], 0.0))
            quad = lambda a: tmp[:, a:a + 4].rearrange("p (c r) g -> p c r g", c=2)
            twice = lambda a: tmp[:, a:a + 2].unsqueeze(2).to_broadcast([P, 2, 2, GROUPS])
            for n in range(ORD, 1, -1):
                stt(quad(12)[:, 0], twice(10)[:, 0], 1.0 / n, quad(6)[:, 0], MUL, MUL)
                link(stt(quad(12)[:, 1], twice(10)[:, 1], 1.0 / n, quad(6)[:, 1], MUL, MUL))
                link(tt(tmp[:, 10:12], tmp[:, 12:14], tmp[:, 14:16], ADD))
                link(ts(tmp[:, 10], tmp[:, 10], 1.0, None, ADD))
            link(tt(quad(12), twice(10), quad(6), MUL))
            link(tt(tmp[:, 16:18], tmp[:, 12:14], tmp[:, 14:16], ADD))
            for n in range(SQ):
                ts(tmp[:, 6:10:3], tmp[:, 16:17].to_broadcast([P, 2, GROUPS]), 2.0, None, ADD)
                V.tensor_copy(tmp[:, 7], tmp[:, 17])
                link(ts(tmp[:, 8], tmp[:, 17], -1.0, None, MUL))
                link(tt(quad(12), twice(16), quad(6), MUL))
                link(tt(tmp[:, 16:18], tmp[:, 12:14], tmp[:, 14:16], ADD))
            V.memset(Npow[:, 0, 0], 1.0)
            V.memset(Npow[:, 0, 1], 0.0)
            ts(Npow[:, 1, 0], tmp[:, 16], 1.0, None, ADD)
            V.tensor_copy(Npow[:, 1, 1], tmp[:, 17])
            ts(tmp[:, 28], tmp[:, 16], 1.0, None, ADD)
            link(V.tensor_copy(tmp[:, 29], tmp[:, 17]))
            for m in (1, 2, 4):
                ts(tmp[:, 18], Npow[:, m, 1], -1.0, None, MUL)
                link(V.tensor_copy(tmp[:, 19], Npow[:, m, 0]))
                lo = Npow[:, 1:1 + m]
                hi = Npow[:, 1 + m:1 + 2 * m]
                part = tmp[:, 20:20 + 2 * m].rearrange("p (m r) g -> p m r g", m=m)
                shape = [P, m, 2, GROUPS]
                tt(hi, lo[:, :, 0:1].to_broadcast(shape), Npow[:, m:m + 1].to_broadcast(shape), MUL)
                link(tt(part, lo[:, :, 1:2].to_broadcast(shape), tmp[:, 18:20].unsqueeze(1).to_broadcast(shape), MUL))
                link(tt(hi, hi, part, ADD))
            V.tensor_copy(LT[:, 0], Npow[:, CH])
            ts(LT[:, 1, 0], Npow[:, CH, 1], -1.0, None, MUL)
            V.tensor_copy(LT[:, 1, 1], Npow[:, CH, 0])
            V.tensor_copy(pw[0:64, 0:2].rearrange("p r g k -> p k r g"), Npow[0:64, 0:CH])
            link(V.tensor_copy(pw[64:P, 0:2].rearrange("p r g k -> p k r g"), Npow[64:P, 0:CH][:, ::-1]))
            ts(pw[:, 2], pw[:, 1], -1.0, None, MUL)
            ts(pw[:, 3], pw[:, 0], -1.0, None, MUL).then_inc(S("pw_ready"), 1)
            er, ei, lr, li = tmp[:, 16], tmp[:, 17], tmp[:, 0], tmp[:, 1]
            tt(tmp[:, 4], lr, lr, MUL)
            link(tt(tmp[:, 5], li, li, MUL))
            link(tt(tmp[:, 4], tmp[:, 4], tmp[:, 5], ADD))
            link(V.reciprocal(tmp[:, 5], tmp[:, 4]))
            tt(tmp[:, 6], er, lr, MUL)
            tt(tmp[:, 7], ei, li, MUL)
            tt(tmp[:, 8], ei, lr, MUL)
            link(tt(tmp[:, 9], er, li, MUL))
            tt(tmp[:, 10], tmp[:, 6], tmp[:, 7], ADD)
            link(tt(tmp[:, 11], tmp[:, 8], tmp[:, 9], SUB))
            link(tt(tmp[:, 10:12], tmp[:, 10:12], tmp[:, 5:6].to_broadcast([P, 2, GROUPS]), MUL))
            tt(tmp[:, 12], tmp[:, 28], tmp[:, 10], MUL)
            tt(tmp[:, 13], tmp[:, 29], tmp[:, 11], MUL)
            tt(tmp[:, 14], tmp[:, 28], tmp[:, 11], MUL)
            link(tt(tmp[:, 15], tmp[:, 29], tmp[:, 10], MUL))
            tt(tmp[:, 18], tmp[:, 12], tmp[:, 13], SUB)
            link(tt(tmp[:, 19], tmp[:, 14], tmp[:, 15], ADD))
            dve.wait_ge(S("b_in"), 32)
            scratch = tmpP.rearrange("p a b c -> p (a b c)").rearrange("p (g h) -> p g h", h=GW)
            for dst, f in ((Bb_sb, 10), (Bp_sb, 18)):
                fr, fi = (tmp[:, f + j].unsqueeze(2).to_broadcast([P, GROUPS, GW]) for j in range(2))
                br, bi = b_raw[:, 0], b_raw[:, 1]
                re, im = dst[:, 0, 0:GROUPS], dst[:, 1, 0:GROUPS]
                tt(re, br, fr, MUL)
                link(tt(scratch, bi, fi, MUL))
                link(tt(re, re, scratch, SUB))
                tt(im, br, fi, MUL)
                link(tt(scratch, bi, fr, MUL))
                link(tt(im, im, scratch, ADD))

            def p_table(b):
                G = slice(b * BG, (b + 1) * BG)
                Br, Bi = (Bp_sb[:, j, G].unsqueeze(2).to_broadcast([P, BG, CH, GW]) for j in range(2))
                W = [pw[:, j, G].unsqueeze(3).to_broadcast([P, BG, CH, GW]) for j in range(4)]
                if b:
                    dve.wait_ge(S("pt_done"), 4 * b)
                tt(P_re, Br, W[0], MUL)
                link(tt(tmpP, Bi, W[2], MUL))
                link(tt(P_re, P_re, tmpP, ADD))
                tt(P_im, Br, W[1], MUL)
                link(tt(tmpP, Bi, W[0], MUL))
                tt(P_im, P_im, tmpP, ADD).then_inc(S("P_ready"), 1)
                dve.wait_ge(S("P_ready"), b + 1)

            def inverse_rms(cols, sq, n, name):
                dve.wait_ge(S(f"sq{name}"), n)
                src = small[:, 0:4] if name == 0 else cols
                ts(cols, src, 1.0 / D, EPS, MUL, ADD).then_inc(S(f"ms{name}"), 1)
                dve.wait_ge(S(f"rt{name}"), 1)
                link(V.reciprocal(cols, cols))

            def mod_add(n):
                dve.wait_ge(S("ada_used"), KT * (n + 1))
                dve.wait_ge(S(f"adab_in{n % 2}"), 64 * (n // 2 + 1))
                if n:
                    dve.wait_ge(S("mod_out"), 64 * n)
                for q in range(4):
                    r = slice(32 * q, 32 * q + 2)
                    tt(mod_sb[r], bank[n % 2][r, :], adab[r, n % 2], ADD).then_inc(S("mod_sb_full"), 1)

            inverse_rms(small[:, 4:8], None, 4, 0)
            p_table(0)
            mod_add(0)
            p_table(1)
            dve.wait_ge(S("bc_in"), 80)
            nrow = at(DU_off, D)
            stt(bc[:, 1], bc[:, 1], 1.0, nrow, ADD, MUL)
            link(stt(bc[:, 3], bc[:, 3], 1.0, nrow, ADD, MUL))
            for j in range(4):
                s, t = j // 2, j % 2
                src = (hlat if s == 0 else ut[:, 1])[:, t]
                link(stt(ut[:, s, t], src, small[:, 4 + j:5 + j], bc[:, 2 * s + 1], MUL, MUL))
                tt(ut[:, s, t], ut[:, s, t], bc[:, 2 * s], ADD).then_inc(S("u_ready"), 1)

            def du(h):
                dve.wait_ge(S("du_in"), 16 * CH * (h + 1))
                if h == 0:
                    dve.wait_ge(S("d_in"), 16)
                link(tt(DU, DU,
                        D_sb[:, h * HG:(h + 1) * HG].unsqueeze(2).to_broadcast([P, HG, NCH]), MUL))

            def kernels_out(b):
                dve.wait_ge(S("tk_done"), b + 1)
                if b >= 4:
                    dve.wait_ge(S("t_out"), 64)
                T_b = T_sb[:, b % 4]
                V.tensor_copy(T_b[:, :, 0:P], psum(5, 4, P)[:, 0:2]).then_inc(S("T_ready"), 1)
                V.tensor_copy(T_b[:, :, P:240], psum(4, 4, P)[:, 0:2, GW:P]).then_inc(S("T_ready"), 1)
                dve.wait_ge(S("T_ready"), 3 * b + 2)
                tt(T_b[:, :, P - GW:P], T_b[:, :, P - GW:P], psum(4, 4, P)[:, 0:2, 0:GW], ADD).then_inc(S("T_ready"), 1)

            def inside_out(b):
                q = b % 4
                dve.wait_ge(S("m_done"), b + 1)
                tt(DU[:, q * BG:(q + 1) * BG], DU[:, q * BG:(q + 1) * BG], psum(4 + b % 2, 16, NCH)[:, 0:BG], ADD).then_inc(S("yi_out"), 1)

            def scan(h):
                dve.wait_ge(S("e_out"), 24 * (h + 1))
                L8 = LT[:, :, :, h * HG:(h + 1) * HG]
                base = h * 3 * (2 * NCH - 2)
                for i in range(1, 2 * NCH - 1):
                    prev = e_sb[:, i - 1].unsqueeze(2).to_broadcast([P, 2, 2, HG])
                    tt(sc4, prev, L8, MUL).then_inc(S("scan"), 1)
                    dve.wait_ge(S("scan"), i * 3 + base - 2)
                    tt(sc2, sc4[:, 0], e_sb[:, i], ADD).then_inc(S("scan"), 1)
                    dve.wait_ge(S("scan"), i * 3 + base - 1)
                    tt(e_sb[:, i], sc2, sc4[:, 1], ADD).then_inc(S("scan"), 1)
                    dve.wait_ge(S("scan"), i * 3 + base)
                dve.sem_inc(S("scan_done"), 1)

            def y_out(h):
                dve.wait_ge(S("y_done"), h + 1)
                dve.wait_ge(S("yi_out"), 4 * (h + 1))
                if h:
                    dve.wait_ge(S("z_out"), 16)
                for j in range(2):
                    tt(y_sb[:, 16 * j:16 * j + 16], psum(6 + j, 16, NCH), DU[:, 16 * j:16 * j + 16], ADD).then_inc(S("y_ready"), 1)

            mod_add(1)
            p_table(2)
            p_table(3)
            du(0)
            mod_add(2)
            mod_add(3)
            for b in range(4):
                kernels_out(b)
            scan(0)
            mod_add(4)
            for b in range(4):
                inside_out(b)
            p_table(4)
            y_out(0)
            mod_add(5)
            for b in range(5, 8):
                p_table(b)
            dve.wait_ge(S("y_ready"), 2)
            du(1)
            for b in range(4, 8):
                kernels_out(b)
            scan(1)
            for b in range(4, 8):
                inside_out(b)
            y_out(1)

            dve.wait_ge(S("bd_in"), 64)
            quarters = lambda v: v.rearrange("p t (c n) -> p (t c) n", c=2)
            uq, zq, hq, aq = quarters(u_tok), quarters(z_tok), quarters(hlat), quarters(acc)
            half = lambda row, j: row[:, (j % 2) * 512:(j % 2 + 1) * 512]
            for j in range(4):
                dve.wait_ge(S("glu_pe"), j + 1)
                tt(uq[:, j], bank[4 + j][:, :], half(bd[:, 0], j), ADD).then_inc(S("gate_in"), 1)
            for j in range(4):
                dve.wait_ge(S("sigm"), j + 1)
                dve.wait_ge(S("zt_out"), j + 1)
                link(tt(uq[:, j], uq[:, j], zq[:, j], MUL))
                link(tt(uq[:, j], uq[:, j], half(bd[:, 1], j), MUL))
                ins = tt(hq[:, j], hq[:, j], uq[:, j], ADD)
                link(ins)
            dve.sem_inc(S("glu_done"), 1)
            dve.sem_inc(S("h1"), 1)

            def norm(cols, name, shift, scale, gain, rows1, rows2, done, n):
                inverse_rms(cols, None, 2, name)
                dve.wait_ge(S("bd_in"), rows1)
                link(stt(scale, scale, 1.0, gain, ADD, MUL))
                dve.wait_ge(S("bd_in"), rows2)
                for t in range(TT):
                    link(stt(u_tok[:, t], hlat[:, t], cols[:, t:t + 1], scale, MUL, MUL))
                    link(tt(u_tok[:, t], u_tok[:, t], shift, ADD))
                dve.sem_inc(S(done), n)

            norm(small[:, 8:10], 1, bd[:, 0], bd[:, 2], bd[:, 3], 64, 96, "u1_ready", 2)

            def ffn_h(c):
                dve.wait_ge(S("f_silu"), c + 1)
                dve.wait_ge(S("f_up"), c + 1)
                if not (isinstance(c, int) and c == 0):
                    dve.wait_ge(S("f_tr"), c)
                tt(h_sb[:, 0], sg, bank[5][:, :], MUL).then_inc(S("f_h"), 1)

            ffn_h(0)
            with dve.Fori(1, NF0) as c:
                ffn_h(c)
            dve.wait_ge(S("f_down"), NF0)
            for j in range(4):
                link(tt(uq[:, j], bank[j][:, :], half(bd[:, 1], j), MUL))
                link(tt(hq[:, j], hq[:, j], uq[:, j], ADD))
            dve.sem_inc(S("h2"), 1)

            norm(small[:, 12:14], 2, bd[:, 0], bd[:, 1], bd[:, 3], 160, 160, "u2_ready", 1)
            dve.wait_ge(S("pool_pe"), 1)
            dve.wait_ge(S("bd_in"), 192)
            for j in range(4):
                link(tt(uq[:, j], bank[4 + j][:, :], half(bd[:, 0], j), ADD))
                link(tt(uq[:, j], uq[:, j], half(bd[:, 1], j), MUL))
                link(tt(uq[:, j], uq[:, j], half(bd[:, 2], j), MUL))
                link(tt(hq[:, j], hq[:, j], uq[:, j], ADD))
            dve.sem_inc(S("h3"), 1)
            norm(small[:, 16:18], 3, bd[:, 0], bd[:, 1], bd[:, 3], 256, 256, "u3_ready", 1)

            R = lambda k: rb[:, k]
            V.memset(acc, 0.0)
            V.memset(selT, 0.0)
            V.memset(Ysb, 0.0).then_inc(S("moe_init"), 1)
            V.memset(rankx[:, :, 2 * NE], -5.0)
            V.memset(combx, 0.0)
            for t in range(TT):
                link(ts(R(4)[:, t], iota[:, 0:NE], -float(NE), None, ADD))
            dve.wait_ge(S("logits"), 1)
            link(V.tensor_copy(R(0), psum(2, 64, NE)[:, 0:TT]))

            def best(src, top, eq, key, idx, mask):
                wide = [P, TT, NE]
                link(V.reduce_max(top, src, AX.X))
                link(tt(eq, src, top.unsqueeze(2).to_broadcast(wide), ALU.is_equal))
                link(tt(key, eq, R(4), MUL))
                link(V.tensor_reduce(idx, key, AX.X, ALU.min))
                link(tt(mask, R(4), idx.unsqueeze(2).to_broadcast(wide), ALU.is_equal))

            best(R(0), small[:, 18:20], R(1), R(2), small[:, 26:28], R(3))
            link(stt(R(5), R(3), -3.0e38, R(0), MUL, ADD))
            best(R(5), small[:, 20:22], R(1), R(2), small[:, 28:30], R(6))
            tt(small[:, 22:24], small[:, 20:22], small[:, 18:20], SUB).then_inc(S("top2"), 1)
            tt(R(8), R(3), R(6), ADD).then_inc(S("mask"), 1)
            dve.wait_ge(S("top_exp"), 1)
            dve.wait_ge(S("mask"), 1)
            link(ts(small[:, 30:32], small[:, 24:26], 1.0, None, ADD))
            link(V.reciprocal(small[:, 30:32], small[:, 30:32]))
            link(tt(small[:, 34:36], small[:, 24:26], small[:, 30:32], MUL))
            wide = [P, TT, NE]
            tt(R(9), R(3), small[:, 30:32].unsqueeze(2).to_broadcast(wide), MUL)
            link(tt(R(10), R(6), small[:, 34:36].unsqueeze(2).to_broadcast(wide), MUL))
            tt(combx[:, :, 1:NE + 1], R(9), R(10), ADD)
            tt(combx[:, :, NE + 2:2 * NE + 2], R(9), R(10), ADD)
            dve.wait_ge(S("rank_pe"), 1)
            link(stt(R(11), psum(3, 64, NE)[:, 0:TT], -1000.0, R(8), ADD, MUL))
            ts(rankx[:, :, 0:NE], R(11), 1000.0, None, ADD)
            link(ts(rankx[:, :, NE:2 * NE], R(11), 1000.0 - P, None, ADD))
            link(V.reduce_max(small[:, 36:37], psum(3, 64, NE)[:, 2], AX.X))
            ts(flag_i[:, 0:1], small[:, 36:37], float(P), None, ALU.is_gt).then_inc(S("overflow_known"), 1)

            def select(col, n):
                for t in range(TT):
                    ins = ts(sel[:, t], iota, rankx[:, t, col], None, ALU.is_equal)
                    if t:
                        ins.then_inc(S("sel_ready"), 1)

            def accumulate(r, n, col):
                dve.wait_ge(S("scat_pe"), n)
                stt(aq[:, r], bank[7][:, :], combx[:, r // 2, col], aq[:, r], MUL, ADD).then_inc(S("scat_acc"), 1)

            def expert(i, k):
                zero = isinstance(i, int) and i == 0
                for c in range(NF1):
                    dve.wait_ge(S("x_silu"), i * NF1 + c + 1)
                    dve.wait_ge(S("x_up"), i * NF1 + c + 1)
                    if not (zero and c == 0):
                        dve.wait_ge(S("x_tr"), i * NF1 + c)
                    tt(h_sb[:, 0], sg, bank[2 + c % 2][:, :], MUL).then_inc(S("x_h"), 1)
                    if c < 2:
                        for r in (2 * c, 2 * c + 1):
                            accumulate(r, i * 4 + 4 * k + r + 1, bass.ds(i + k, 1))
                    if c == 3:
                        dve.wait_ge(S("seltr"), i + 1)
                        select(bass.ds(i + 1, 1), i + 2)

            select(bass.ds(0, 1), 1)
            expert(0, 0)
            with dve.Fori(1, NE) as i:
                expert(i, 0)
            for r in range(4):
                accumulate(r, 4 * NE + r + 1, bass.ds(NE, 1))
            dve.wait_ge(S("overflow_known"), 1)
            more = dve.value_load(flag_i[0:1, 0:1], min_val=0, max_val=1)
            with dve.If(more):
                with dve.Fori(NE, 2 * NE) as i:
                    expert(i, 1)
                for r in range(4):
                    accumulate(r, 8 * NE + 4 + r + 1, bass.ds(2 * NE + 1, 1))
            link(V.memset(small[:, 40:41], 0.0))
            for j in range(4):
                link(tt(uq[:, j], aq[:, j], half(bd[:, 2], j), MUL))
                link(tt(hq[:, j], hq[:, j], uq[:, j], ADD))
            dve.sem_inc(S("h4"), 1)
            inverse_rms(small[:, 32:34], None, 2, 4)
            dve.wait_ge(S("bd_in"), 272)
            for t in range(TT):
                stt(u_tok[:, t], hlat[:, t], small[:, 32 + t:33 + t], bd[:, 3], MUL, MUL).then_inc(S("result"), 1)


def _pool_matrix(np):
    width = 64
    m = np.zeros((4, SEQ, SEQ), np.float32)
    for g, win in enumerate((2, 4, 8, 16)):
        for tok in range(SEQ):
            row, pos = divmod(tok, width)
            lo, hi = max(pos - win // 2, 0), min(pos + win // 2, width)
            m[g, row * width + lo:row * width + hi, tok] = np.float32(1) / np.float32(hi - lo)
            m[g, tok, tok] -= np.float32(1)
    order = np.arange(SEQ).reshape(NCH, CH).T.reshape(-1)
    m = m[:, order][:, :, order]
    return np.ascontiguousarray(m.reshape(4, TT, P, SEQ).transpose(2, 0, 1, 3))


def kernel(x, c, ctx, c_ctx, ada_w, ada_b, norm_mix, norm_ffn, norm_final,
           s5_lambda_re, s5_lambda_im, s5_log_step, s5_b_re, s5_b_im, s5_c_re, s5_c_im,
           s5_d, s5_glu_w, s5_glu_b, pool_w, pool_b, pool_scale, fnet_w, fnet_b,
           ffn_w_gate, ffn_w_up, ffn_w_down, moe_router, moe_w_gate, moe_w_up, moe_w_down):
    import numpy as np
    import concourse.bacc as bacc
    from concourse.bass_utils import run_bass_kernel_spmd

    A = np.asarray

    def rows(v):
        return A(v).reshape(NCH, CH, D).transpose(1, 0, 2).reshape(SEQ, D)

    def lam(v):
        return A(v)[0].transpose(0, 2, 1).reshape(P, GROUPS)

    eye = np.eye(P, dtype=np.float32)
    tri = np.triu(np.ones((P, P), np.float32), 1)
    iota = np.tile(np.arange(P, dtype=np.float32), (P, 1))
    arrays = dict(
        x_in=rows(x), ctx_in=rows(ctx),
        cond_in=np.stack([A(c)[0], A(c_ctx)], 1).reshape(KT, P, 2).transpose(1, 0, 2),
        ada_w=A(ada_w), ada_b=A(ada_b), norm_mix=A(norm_mix), norm_ffn=A(norm_ffn), norm_final=A(norm_final)[None],
        lam_re=lam(s5_lambda_re), lam_im=lam(s5_lambda_im),
        log_step=np.broadcast_to(A(s5_log_step)[0][:, None, :], (2, NST, GROUPS)).reshape(P, GROUPS),
        b_re=A(s5_b_re)[0].transpose(0, 2, 1, 3).reshape(P, GROUPS, GW),
        b_im=A(s5_b_im)[0].transpose(0, 2, 1, 3).reshape(P, GROUPS, GW),
        c_re=A(s5_c_re)[0].transpose(0, 3, 1, 2).reshape(P, GROUPS, GW),
        c_im=A(s5_c_im)[0].transpose(0, 3, 1, 2).reshape(P, GROUPS, GW),
        d_skip=np.tile(A(s5_d)[0].reshape(GROUPS, GW).T, (CH, 1)),
        glu_w=A(s5_glu_w)[0], glu_b=A(s5_glu_b), pool_w=A(pool_w)[0], pool_b=A(pool_b), pool_scale=A(pool_scale),
        w_gate=A(ffn_w_gate)[0], w_up=A(ffn_w_up)[0], w_down=A(ffn_w_down)[0], router=A(moe_router)[0],
        e_gate=A(moe_w_gate)[0], e_up=A(moe_w_up)[0], e_down=A(moe_w_down)[0],
        consts=np.stack([eye, tri, np.ones((P, P), np.float32), iota], 1),
        pool_mat=_pool_matrix(np),
    )
    arrays = {k: np.ascontiguousarray(v) for k, v in arrays.items()}
    nc = bacc.Bacc("TRN2", target_bir_lowering=False, num_devices=1)
    aps = {k: nc.dram_tensor(k, v.shape, mybir.dt.from_np(v.dtype), kind="ExternalInput").ap() for k, v in arrays.items()}
    out = nc.dram_tensor("out", (SEQ, D), mybir.dt.float32, kind="ExternalOutput").ap()
    build(nc, out=out, **aps)
    got = run_bass_kernel_spmd(nc, [arrays], core_ids=[0]).results[0]["out"]
    return got.reshape(CH, NCH, D).transpose(1, 0, 2).reshape(1, SEQ, D)
```

```python
import concourse.bass as bass
from concourse import mybir
from contextlib import ExitStack

P = 128
D = 1024
SEQ = 256
TT = SEQ // P
KT = D // P
GROUPS, GW, NST = 64, 16, 64
CH = 8
NCH = SEQ // CH
HG = GROUPS // 2
BG = 8
NMOD = 6
DFF = 2816
FC0 = 256
NF0 = DFF // FC0
NE = 8
DFE = 3584
FC1 = 512
NF1 = DFE // FC1
NSLOT = 7
SLOT = 2048
NPIECE = 6
PIECE = 1024
NADA = 3
EPS = 1e-6
SQ = 6
ORD = 7


def build(nc, x_in, ctx_in, cond_in, ada_w, ada_b, norm_mix, norm_ffn, norm_final,
          lam_re, lam_im, log_step, b_re, b_im, c_re, c_im, d_skip, glu_w, glu_b,
          pool_w, pool_b, pool_scale, w_gate, w_up, w_down, router, e_gate, e_up, e_down,
          consts, pool_mat, out):
    F32, I32 = mybir.dt.float32, mybir.dt.int32
    ALU, ACT, AX = mybir.AluOpType, mybir.ActivationFunctionType, mybir.AxisListType
    MUL, ADD, SUB = ALU.mult, ALU.add, ALU.subtract

    mod_d = nc.dram_tensor("mod_scratch", (2, 2, NMOD * D), F32).ap()
    u_d = nc.dram_tensor("u_scratch", (GROUPS, GW, CH, 2 * NCH), F32).ap()
    t_d = nc.dram_tensor("kernel_scratch", (GROUPS, GW, 240), F32).ap()
    z_d = nc.dram_tensor("z_scratch", (CH, GW, GROUPS, NCH), F32).ap()

    ctx = ExitStack()
    with ctx:
        mem = ctx.enter_context(nc.sbuf_tensor("common_mem", [P, 2560 + P], F32))
        sems = {}

        def S(name):
            if name not in sems:
                sems[name] = ctx.enter_context(nc.semaphore(name))
            return sems[name]

        def at(o, *dims, of=None):
            n = 1
            for d in dims:
                n *= d
            v = (of or mem)[:, o:o + n]
            if len(dims) == 1:
                return v
            names = "abcd"[:len(dims)]
            return v.rearrange(f"p ({' '.join(names)}) -> p {' '.join(names)}", **{k: d for k, d in zip(names, dims)})

        ident, tri, ones, iota = (at(i * P, P) for i in range(4))
        hlat = at(512, TT, D)
        flag_i = ctx.enter_context(nc.sbuf_tensor("flag", [P, 8], I32))
        small = at(2560, P)
        TOTAL = 52980 - 2560 - P
        with nc.sbuf_tensor("s5_mem", [P, TOTAL], F32) as s5_mem:
            pass
        era = [s5_mem]
        o = [0]

        def take(*dims):
            n = 1
            for d in dims:
                n *= d
            o[0] += n
            return at(o[0] - n, *dims, of=era[0])

        G_re = take(HG, CH, GW)
        G_nim = take(HG, CH, GW)
        E_off = o[0]
        E_sb = take(2, BG, 2, P)
        b_raw = at(E_off, 2, GROUPS, GW, of=s5_mem)
        e_off = o[0]
        e_sb = take(2 * NCH, 2, HG)
        bc = at(e_off, 4, D, of=s5_mem)
        U_off = o[0]
        U_sb = take(GROUPS, 2 * NCH)
        tmp = at(U_off, 32, GROUPS, of=s5_mem)
        M_off = o[0]
        M_sb = take(2, BG, P)
        S_rhs = take(2, HG, NCH)
        ut = at(M_off, 2, TT, D, of=s5_mem)
        P_re = take(BG, CH, GW)
        P_im = take(BG, CH, GW)
        C_sb = take(2, GROUPS, GW)
        Bp_sb = take(2, GROUPS, GW)
        Bb_sb = take(2, GROUPS + 1, GW)
        pw = take(4, GROUPS, CH)
        T_sb = take(4, 2, 240)
        DU_off = o[0]
        DU = take(HG, NCH)
        y_sb = take(HG, NCH)
        stage = at(DU_off, 4, 512, of=s5_mem)
        N_off = o[0]
        tmpP = take(BG, CH, GW)
        tmpG = take(BG, CH, GW)
        Npow = at(N_off, CH + 1, 2, GROUPS, of=s5_mem)
        LT = take(2, 2, GROUPS)
        sc4 = take(2, 2, HG)
        sc2 = take(2, HG)
        D_sb = take(GROUPS)
        adab = take(2, 512)
        mod_sb = take(512)
        cs = take(2, KT, 2)
        assert o[0] <= TOTAL - NADA * 2048, o[0]
        ring_a = at(TOTAL - NADA * 2048, NADA, 2048, of=s5_mem)
        LATE = 18000
        late_mem = ctx.enter_context(nc.sbuf_tensor("late_mem", [P, LATE], F32))
        era[0] = late_mem
        o = [0]
        poolw = take(4, 2, 256)
        acc = take(TT, D)
        poolP = at(o[0] - 2048, 4, TT, SEQ, of=late_mem)
        z_tok = acc
        xT = take(KT, SEQ)
        zT = xT
        u_tok = take(TT, D)
        bd = take(6, D)
        h_sb = take(512)
        sg = take(512)
        Ysb = take(D)
        sel = take(TT, P)
        selT = take(TT, P)
        rt_sb = take(KT, NE)
        rb = take(12, TT, NE)
        rankx = take(TT, 2 * NE + 1)
        combx = take(TT, 2 * NE + 2)
        assert o[0] <= LATE, o[0]
        with nc.sbuf_tensor("before_glu", [P, TOTAL - LATE - KT * D], F32), nc.sbuf_tensor("glu_sb", [P, KT, D], F32) as glu_sb:
            pass
        F32R = mybir.dt.float32r

        def parts(name, *dims):
            return ctx.enter_context(nc.sbuf_tensor(name, [P, *dims], F32R))

        x_hi, x_lo = parts("x_hi", KT, SEQ), parts("x_lo", KT, SEQ)
        h_hi, h_lo = parts("h_hi", 4, P), parts("h_lo", 4, P)
        ring = ctx.enter_context(nc.sbuf_tensor("weight_ring", [P, NSLOT, SLOT], F32))
        w_hi, w_lo = parts("w_hi", NPIECE, PIECE), parts("w_lo", NPIECE, PIECE)

        bank = [ctx.enter_context(nc.psum_tensor(f"bank{i}", [P, 512], F32)) for i in range(8)]

        def psum(i, *dims):
            v = bank[i][:, :]
            names = "abcd"[:len(dims)]
            return v.rearrange(f"p ({' '.join(names)}) -> p {' '.join(names)}", **{k: d for k, d in zip(names, dims)})

        ada_full = [S(f"ada_full{i}") for i in range(NADA)]
        full = [S(f"slot_full{i}") for i in range(NSLOT)]
        block = ctx.enter_context(nc.Block())

        ADA_UNITS = 2 * 3 * KT
        FFN_UNITS = 3 * NF0
        FFN_PIECES = 2 * FFN_UNITS
        FFN_LOADS = [len(range(s, FFN_UNITS, 6)) for s in range(6)] + [0]
        ORDER = []
        for c in range(NF1):
            ORDER += [("gate", c, 0), ("gate", c, 1), ("up", c, 0), ("up", c, 1)]
            if c:
                ORDER += [("down", c - 1, 0), ("down", c - 1, 1)]
        ORDER += [("down", NF1 - 1, 0), ("down", NF1 - 1, 1)]
        EXPERT_UNITS, EXPERT_PIECES = len(ORDER), 2 * len(ORDER)
        assert EXPERT_UNITS % NSLOT == 0 and EXPERT_PIECES % NPIECE == 0 and FFN_PIECES % NPIECE == 0

        def ffn_pieces(kind, c):
            if kind == "down":
                return FFN_PIECES if isinstance(c, int) and c == NF0 - 1 else 6 * c + 10
            if isinstance(c, int) and c == 0:
                return {"gate": 2, "up": 4}[kind]
            return 6 * c + {"gate": 0, "up": 2}[kind]

        def expert_pieces(i, kind, c):
            return i * EXPERT_PIECES + (FFN_PIECES + 2 * (ORDER.index((kind, c, 1)) + 1))

        @block.sync
        def _(sp):
            sp.dma_start(at(0, 4, P), consts).then_inc(S("consts_in"), 16)
            sp.dma_start(cs[:, 0], cond_in).then_inc(S("cond_in"), 16)
            for j, src in enumerate((lam_re, lam_im, log_step)):
                sp.dma_start(tmp[:, j], src).then_inc(S("lam_in"), 16)
            for j, src in enumerate((b_re, b_im)):
                sp.dma_start(b_raw[:, j], src).then_inc(S("b_in"), 16)
            for j, src in enumerate((c_re, c_im)):
                sp.dma_start(C_sb[:, j], src).then_inc(S("c_in"), 16)
            sp.dma_start(D_sb, d_skip).then_inc(S("d_in"), 16)
            sp.dma_start(hlat, x_in.rearrange("(t p) n -> p t n", p=P)).then_inc(S("x_in"), 16)
            sp.dma_start(ut[:, 1], ctx_in.rearrange("(t p) n -> p t n", p=P)).then_inc(S("x_in"), 16)
            for n in range(ADA_UNITS):
                l, r, k = n // (3 * KT), n // KT % 3, n % KT
                if n >= NADA:
                    sp.wait_ge(S("ada_used"), n - NADA + 1)
                sp.dma_start(ring_a[:, n % NADA], ada_w[l, k * P:(k + 1) * P, r * 2048:(r + 1) * 2048]).then_inc(ada_full[n % NADA], 16)
            sp.wait_ge(S("ada_used"), ADA_UNITS)
            sp.wait_ge(S("y_done"), 2)
            sp.dma_start(glu_sb[:], glu_w.rearrange("(k p) n -> p k n", p=P)).then_inc(S("glu_in"), 16)
            sp.wait_ge(S("z_out"), 32)
            sp.dma_start(poolw, pool_w.rearrange("g (k p) n -> p g k n", p=P)).then_inc(S("pool_in"), 16)
            sp.dma_start(rt_sb, router.rearrange("(k p) n -> p k n", p=P)).then_inc(S("pool_in"), 16)
            gate_v = w_gate.rearrange("(k p) n -> p k n", p=P)
            up_v = w_up.rearrange("(k p) n -> p k n", p=P)

            def ffn_load(kind, c, m, before):
                s = m % 6
                if before is not None:
                    sp.wait_ge(S("low"), before)
                if kind == "down":
                    dst = ring[:, s].rearrange("p (f n) -> p f n", f=2)
                    src = w_down[bass.ds(c * FC0, FC0), :].rearrange("(f p) n -> p f n", p=P)
                else:
                    dst = ring[:, s].rearrange("p (k n) -> p k n", k=KT)
                    src = (gate_v if kind == "gate" else up_v)[:, :, bass.ds(c * FC0, FC0)]
                sp.dma_start(dst, src).then_inc(full[s], 16)

            ffn_load("gate", 0, 0, None)
            ffn_load("up", 0, 1, None)
            for m, (kind, c) in enumerate((("gate", 1), ("up", 1), ("down", 0), ("gate", 2), ("up", 2), ("down", 1)), 2):
                ffn_load(kind, c, m, 2 * (m - 5) if m >= 6 else None)
            sp.wait_ge(S("h1"), 1)
            sp.dma_start(poolP, pool_mat).then_inc(S("pool_in"), 16)
            with sp.Fori(1, NF0 // 2) as i:
                for n, (kind, dc) in enumerate((("gate", 1), ("up", 1), ("down", 0), ("gate", 2), ("up", 2), ("down", 1))):
                    ffn_load(kind, 2 * i + dc, (2 + n) % 6, 12 * i - 8 + 2 * n + 2)
            ffn_load("down", NF0 - 1, FFN_UNITS - 1, 2 * (FFN_UNITS - 6))

            gates = {"gate": e_gate, "up": e_up}

            def expert_loads(i, e):
                for r, (kind, c, half) in enumerate(ORDER):
                    s = r % NSLOT
                    if isinstance(i, int) and r < NSLOT:
                        if s < 6:
                            last = max(range(s, FFN_UNITS, 6))
                            sp.wait_ge(S("low"), 2 * (last + 1))
                    else:
                        sp.wait_ge(S("low"), i * EXPERT_PIECES + (FFN_PIECES + 2 * (r - NSLOT + 1)))
                    cols = slice(c * FC1, (c + 1) * FC1)
                    if kind == "down":
                        rows_ = slice(c * FC1 + half * 256, c * FC1 + half * 256 + 256)
                        src = e_down[bass.ds(e, 1), rows_, :].rearrange("o (f p) n -> p (o f) n", p=P)
                        dst = ring[:, s].rearrange("p (f n) -> p f n", f=2)
                    else:
                        src = gates[kind][bass.ds(e, 1), half * 512:(half + 1) * 512, cols].rearrange("o (k p) n -> p (o k) n", p=P)
                        dst = ring[:, s].rearrange("p (k n) -> p k n", k=4)
                    sp.dma_start(dst, src).then_inc(full[s], 16)

            expert_loads(0, 0)
            with sp.Fori(1, NE) as i:
                expert_loads(i, i)
            sp.wait_ge(S("overflow_known"), 1)
            more = sp.value_load(flag_i[0:1, 0:1], min_val=0, max_val=1)
            with sp.If(more):
                with sp.Fori(NE, 2 * NE) as i:
                    expert_loads(i, i - NE)

        @block.gpsimd
        def _(pool):
            def g_table(b):
                g0, q = b * BG, b % 4
                G = slice(g0, g0 + BG)
                Cr, Ci = (C_sb[:, j, G].unsqueeze(2).to_broadcast([P, BG, CH, GW]) for j in range(2))
                W = [pw[:, j, G].unsqueeze(3).to_broadcast([P, BG, CH, GW]) for j in range(4)]
                if b >= 4:
                    pool.wait_ge(S("y_done"), 1)
                gr, gi = (t[:, q * BG:(q + 1) * BG] for t in (G_re, G_nim))
                k = 6 * b
                nc.gpsimd.tensor_tensor(gr, Cr, W[0], MUL).then_inc(S("g_chain"), 1)
                nc.gpsimd.tensor_tensor(tmpG, Ci, W[2], MUL).then_inc(S("g_chain"), 1)
                pool.wait_ge(S("g_chain"), k + 2)
                nc.gpsimd.tensor_tensor(gr, gr, tmpG, ADD).then_inc(S("g_chain"), 1)
                nc.gpsimd.tensor_tensor(gi, Cr, W[2], MUL).then_inc(S("g_chain"), 1)
                pool.wait_ge(S("g_chain"), k + 4)
                nc.gpsimd.tensor_tensor(tmpG, Ci, W[3], MUL).then_inc(S("g_chain"), 1)
                pool.wait_ge(S("g_chain"), k + 5)
                nc.gpsimd.tensor_tensor(gi, gi, tmpG, ADD).then_inc(S("g_chain"), 1)
                pool.wait_ge(S("g_chain"), k + 6)

            pool.wait_ge(S("pw_ready"), 1)
            pool.wait_ge(S("c_in"), 32)
            for b in range(8):
                g_table(b)

        @block.scalar
        def _(act):
            def copy(dst, src, name, n=1):
                nc.scalar.activation(dst, src, ACT.Copy).then_inc(S(name), n)

            act.wait_ge(S("cond_in"), 16)
            nc.scalar.activation(cs[:, 1], cs[:, 0], ACT.Silu).then_inc(S("cond_silu"), 1)
            act.wait_ge(S("lam_in"), 48)
            nc.scalar.activation(tmp[:, 3], tmp[:, 2], ACT.Exp).then_inc(S("step_exp"), 1)

            def squares(src, junk, where, name):
                for t in range(TT):
                    nc.scalar.activation(junk[:, t], src[:, t], ACT.Square, accum_out=where[:, t:t + 1]).then_inc(S(name), 1)

            act.wait_ge(S("x_in"), 32)
            squares(hlat, bc[:, 0:2], small[:, 0:2], "sq0")
            squares(ut[:, 1], bc[:, 2:4], small[:, 2:4], "sq0")

            def mod_bias(n):
                l, r = n // 3, n % 3
                for q in range(4):
                    act.dma_start(adab[32 * q:32 * q + 2, n % 2],
                                  ada_b[l:l + 1, r * 2048 + q * 512:r * 2048 + (q + 1) * 512].to_broadcast([2, 512])).then_inc(S(f"adab_in{n % 2}"), 16)

            def mod_out(n):
                l, r = n // 3, n % 3
                act.wait_ge(S("mod_sb_full"), 4 * (n + 1))
                for q in range(4):
                    act.dma_start(mod_d[l, :, r * 2048 + q * 512:r * 2048 + (q + 1) * 512],
                                  mod_sb[32 * q:32 * q + 2, :]).then_inc(S("mod_out"), 16)
                if n + 2 < 6:
                    mod_bias(n + 2)

            def rows(dst, src, name):
                act.dma_start(dst, src.to_broadcast([P, D])).then_inc(S(name), 16)

            mod_bias(0)
            mod_bias(1)
            act.wait_ge(S("ms0"), 1)
            nc.scalar.activation(small[:, 4:8], small[:, 4:8], ACT.Sqrt).then_inc(S("rt0"), 1)
            mod_out(0)
            act.wait_ge(S("mod_out"), 64)
            act.wait_ge(S("sq0"), 4)
            rows(bc[:, 0], mod_d[0, 0:1, 0:D], "bc_in")
            rows(bc[:, 1], mod_d[0, 0:1, D:2 * D], "bc_in")
            rows(bc[:, 2], mod_d[0, 1:2, 0:D], "bc_in")
            rows(bc[:, 3], mod_d[0, 1:2, D:2 * D], "bc_in")
            rows(at(DU_off, D, of=s5_mem), norm_mix[0:1, :], "bc_in")

            def p_evac(b):
                if b >= 2:
                    act.wait_ge(S("e_done"), b - 1)
                for j in range(4):
                    n = 4 * b + j
                    act.wait_ge(S("pt_done"), n + 1)
                    nc.scalar.activation(E_sb[:, b % 2, 2 * j:2 * j + 2], psum(2 + n % 2, 2, 2, P), ACT.Copy).then_inc(S("pt_out"), 1)

            def u_evac():
                for k in range(KT):
                    act.wait_ge(S("ut_done"), k + 1)
                    if k >= 4:
                        act.wait_ge(S(f"u_out{k % 4}"), 16 * (k // 4))
                    if k == 0:
                        act.wait_ge(S("u_ready"), 4)
                    nc.scalar.activation(stage[:, k % 4].rearrange("p (b s a) -> p s b a", b=CH, s=2),
                                         psum(2 + k % 2, 2, CH, NCH), ACT.Copy).then_inc(S("ut_out"), 1)
                    act.wait_ge(S("ut_out"), k + 1)
                    act.dma_start(u_d[k * 8:(k + 1) * 8].rearrange("g h b a -> (g h) (b a)"), stage[:, k % 4]).then_inc(S(f"u_out{k % 4}"), 16)
                for k in range(4):
                    act.wait_ge(S(f"u_out{k}"), 16 * KT // 4)
                for c in range(CH):
                    act.dma_start(U_sb[c * GW:(c + 1) * GW], u_d[:, :, CH - 1 - c, :].rearrange("g h a -> h g a")).then_inc(S("U_in"), 16)

            def du_in(h):
                for b in range(CH):
                    act.dma_start(DU[b * GW:(b + 1) * GW],
                                  u_d[h * HG:(h + 1) * HG, :, b, NCH:2 * NCH].rearrange("g h a -> h g a")).then_inc(S("du_in"), 16)

            def e_evac(b):
                q = b % 4
                if b == 4:
                    act.wait_ge(S("srhs_done"), 2)
                for j in range(2):
                    n = 2 * b + j
                    act.wait_ge(S("e_bank"), n + 1)
                    src = psum(6 + j, 4, 2, 2 * NCH)
                    dst = e_sb.rearrange("p i r g -> p g r i")[:, q * BG + 4 * j:q * BG + 4 * j + 4]
                    nc.scalar.activation(dst[0:64], src[0:64], ACT.Copy).then_inc(S("e_out"), 1)
                    for s in range(2):
                        back = src[64:P, :, :, s * NCH:(s + 1) * NCH][:, :, :, ::-1]
                        nc.scalar.activation(dst[64:P, :, :, s * NCH:(s + 1) * NCH], back, ACT.Copy).then_inc(S("e_out"), 1)

            def kernels_to_dram(h):
                act.wait_ge(S("T_ready"), 12 * (h + 1))
                for q in range(4):
                    act.dma_start(t_d[h * HG + q:(h + 1) * HG:4].rearrange("m h n -> h m n"),
                                  T_sb[32 * q:32 * q + GW].rearrange("p b j n -> p (b j) n")).then_inc(S("t_out"), 16)
                act.wait_ge(S("t_out"), 64 * (h + 1))

            def toeplitz_in(b):
                if b >= 2:
                    act.wait_ge(S("m_done"), b)
                for c in range(CH):
                    act.dma_start(M_sb[c * GW:(c + 1) * GW].rearrange("p b g n -> p (b g) n"),
                                  t_d[b * BG:(b + 2) * BG, :, c * GW:c * GW + P].rearrange("g h n -> h g n")).then_inc(S("M_in"), 16)

            def s_copy():
                src = e_sb[:, NCH - 1:2 * NCH - 1].rearrange("p i r g -> p r g i")
                nc.scalar.activation(S_rhs[0:64], src[0:64], ACT.Copy).then_inc(S("srhs_done"), 1)
                nc.scalar.activation(S_rhs[64:P], src[64:P][:, :, :, ::-1], ACT.Copy).then_inc(S("srhs_done"), 1)

            def y_gelu(h):
                act.wait_ge(S("y_ready"), 2 * (h + 1))
                if h == 0:
                    du_in(1)
                nc.scalar.activation(y_sb, y_sb, ACT.Gelu_apprx_tanh).then_inc(S("z_ready"), 1)
                act.wait_ge(S("z_ready"), h + 1)
                act.dma_start(z_d[:, :, h * HG:(h + 1) * HG, :].rearrange("b h g a -> (b h) g a"), y_sb).then_inc(S("z_out"), 16)

            p_evac(0)
            p_evac(1)
            u_evac()
            du_in(0)
            mod_out(1)
            for b in range(4):
                if b >= 2:
                    p_evac(b)
                e_evac(b)
            mod_out(2)
            kernels_to_dram(0)
            toeplitz_in(0)
            mod_out(3)
            toeplitz_in(2)
            mod_out(4)
            act.wait_ge(S("scan_done"), 1)
            s_copy()
            y_gelu(0)
            mod_out(5)
            for b in range(4, 8):
                p_evac(b)
                e_evac(b)
            kernels_to_dram(1)
            toeplitz_in(4)
            toeplitz_in(6)
            act.wait_ge(S("scan_done"), 2)
            s_copy()
            y_gelu(1)

            act.wait_ge(S("z_out"), 32)
            for g in range(8):
                act.dma_start(zT[g * GW:(g + 1) * GW].rearrange("h k (b a) -> h k b a", b=CH),
                              z_d.rearrange("b h (k g) a -> g h k b a", g=8)[g]).then_inc(S("zT_in"), 16)
            act.wait_ge(S("mod_out"), 6 * 64)
            rows(bd[:, 0], glu_b, "bd_in")
            rows(bd[:, 1], mod_d[0, 0:1, 2 * D:3 * D], "bd_in")
            rows(bd[:, 2], mod_d[0, 0:1, 4 * D:5 * D], "bd_in")
            rows(bd[:, 3], norm_ffn[0:1, :], "bd_in")
            for j in range(4):
                act.wait_ge(S("zt_done"), j + 1)
                nc.scalar.activation(z_tok.rearrange("p t (c n) -> p (t c) n", c=2)[:, j], bank[j % 2][:, :], ACT.Copy).then_inc(S("zt_out"), 1)
            for j in range(4):
                act.wait_ge(S("gate_in"), j + 1)
                v = u_tok.rearrange("p t (c n) -> p (t c) n", c=2)[:, j]
                nc.scalar.activation(v, v, ACT.Sigmoid).then_inc(S("sigm"), 1)
            act.wait_ge(S("h1"), 1)
            squares(hlat, u_tok, small[:, 8:10], "sq1")
            act.wait_ge(S("ms1"), 1)
            nc.scalar.activation(small[:, 8:10], small[:, 8:10], ACT.Sqrt).then_inc(S("rt1"), 1)
            rows(bd[:, 0], mod_d[0, 0:1, 3 * D:4 * D], "bd_in")
            rows(bd[:, 1], mod_d[0, 0:1, 5 * D:6 * D], "bd_in")

            def xT_evac(base, bks):
                for j in range(4):
                    act.wait_ge(S("xt_done"), base + j + 1)
                    nc.scalar.activation(xT[:, 2 * j:2 * j + 2], psum(bks[j % 2], 2, SEQ), ACT.Copy).then_inc(S("xt_out"), 1)

            for j in range(4):
                act.wait_ge(S("xt_done"), j + 1)
                nc.scalar.activation(x_hi[:, 2 * j:2 * j + 2], psum(j % 2, 2, SEQ), ACT.Copy).then_inc(S("x_hi"), 1)

            def high(n, b, slot, half, slot_loads=None):
                if slot_loads is not None:
                    act.wait_ge(full[slot], slot_loads)
                if not (isinstance(n, int) and n < NPIECE):
                    act.wait_ge(S("piece_used"), n - (NPIECE - 1))
                nc.scalar.activation(w_hi[:, b], ring[:, slot, half * PIECE:(half + 1) * PIECE], ACT.Copy).then_inc(S("high"), 1)

            def ffn_high(m, slot, loads):
                for half in range(2):
                    high(2 * m + half, (2 * slot + half) % NPIECE, slot, half, 16 * loads if half == 0 else None)

            def ffn_silu(c):
                act.wait_ge(S("piece_used"), ffn_pieces("gate", c))
                if not (isinstance(c, int) and c == 0):
                    act.wait_ge(S("f_h"), c)
                nc.scalar.activation(sg, bank[4][:, :], ACT.Silu).then_inc(S("f_silu"), 1)

            def ffn_hT(c):
                act.wait_ge(S("f_tr"), c + 1)
                if not (isinstance(c, int) and c == 0):
                    act.wait_ge(S("piece_used"), ffn_pieces("down", c - 1))
                nc.scalar.activation(h_hi[:], psum(6, 4, P), ACT.Copy).then_inc(S("f_hT"), 1)

            def ffn_chunk(c, s, loads):
                m = 3 * c - 1
                ffn_high(m, s, loads[0])
                ffn_high(m + 1, (s + 1) % 6, loads[1])
                ffn_silu(c)
                ffn_hT(c - 1)
                ffn_high(m + 2, (s + 2) % 6, loads[2])

            act.wait_ge(S("glu_pe"), 4)
            ffn_high(0, 0, 1)
            ffn_high(1, 1, 1)
            ffn_silu(0)
            ffn_chunk(1, 2, (1, 1, 1))
            ffn_chunk(2, 5, (1, 2, 2))
            with act.Fori(1, NF0 // 2) as i:
                ffn_chunk(2 * i + 1, 2, (i + 1, i + 1, i + 1))
                ffn_chunk(2 * i + 2, 5, (i + 1, i + 2, i + 2))
            ffn_high(FFN_UNITS - 1, (FFN_UNITS - 1) % 6, (FFN_UNITS - 1) // 6 + 1)
            ffn_hT(NF0 - 1)

            act.wait_ge(S("h2"), 1)
            squares(hlat, u_tok, small[:, 12:14], "sq2")
            act.wait_ge(S("ms2"), 1)
            nc.scalar.activation(small[:, 12:14], small[:, 12:14], ACT.Sqrt).then_inc(S("rt2"), 1)
            rows(bd[:, 0], mod_d[1, 0:1, 0:D], "bd_in")
            rows(bd[:, 1], mod_d[1, 0:1, D:2 * D], "bd_in")
            rows(bd[:, 2], mod_d[1, 0:1, 2 * D:3 * D], "bd_in")
            rows(bd[:, 3], norm_mix[1:2, :], "bd_in")
            xT_evac(4, (0, 1))
            act.wait_ge(S("u2_ready"), 1)
            rows(bd[:, 0], pool_b, "bd_in")
            rows(bd[:, 1], pool_scale, "bd_in")
            act.wait_ge(S("h3"), 1)
            squares(hlat, u_tok, small[:, 16:18], "sq3")
            act.wait_ge(S("ms3"), 1)
            nc.scalar.activation(small[:, 16:18], small[:, 16:18], ACT.Sqrt).then_inc(S("rt3"), 1)
            rows(bd[:, 0], mod_d[1, 0:1, 3 * D:4 * D], "bd_in")
            rows(bd[:, 1], mod_d[1, 0:1, 4 * D:5 * D], "bd_in")
            rows(bd[:, 2], mod_d[1, 0:1, 5 * D:6 * D], "bd_in")
            rows(bd[:, 3], norm_ffn[1:2, :], "bd_in")
            xT_evac(8, (0, 1))
            act.wait_ge(S("top2"), 1)
            nc.scalar.activation(small[:, 24:26], small[:, 22:24], ACT.Exp).then_inc(S("top_exp"), 1)
            act.wait_ge(S("u3_ready"), 1)
            rows(bd[:, 3], norm_final, "bd_in")

            def gather_out(half, n):
                act.wait_ge(S(f"gather{half}"), n)
                nc.scalar.activation(x_hi[:, 4 * half:4 * half + 4, 0:P], psum(7, 4, P), ACT.Copy).then_inc(S(f"gather_hi{half}"), 1)

            def expert(i, k):
                def highs(units):
                    for r in units:
                        for half in range(2):
                            s = r % NSLOT
                            loads = None
                            if half == 0:
                                loads = i * (16 * EXPERT_UNITS // NSLOT) + 16 * (FFN_LOADS[s] + r // NSLOT + 1)
                            high(i * EXPERT_PIECES + (FFN_PIECES + 2 * r + half), (2 * r + half) % NPIECE, s, half, loads)

                def silu(c):
                    act.wait_ge(S("piece_used"), expert_pieces(i, "gate", c))
                    if not (isinstance(i, int) and i == 0 and c == 0):
                        act.wait_ge(S("x_h"), i * NF1 + c)
                    nc.scalar.activation(sg, bank[c % 2][:, :], ACT.Silu).then_inc(S("x_silu"), 1)

                def hTs(c):
                    act.wait_ge(S("x_tr"), i * NF1 + c + 1)
                    act.wait_ge(S("piece_used"), expert_pieces(i, "down", c - 1) if c else i * EXPERT_PIECES + FFN_PIECES)
                    nc.scalar.activation(h_hi[:], psum(6, 4, P), ACT.Copy).then_inc(S("x_hT"), 1)

                r = 0
                for c in range(NF1):
                    highs((r, r + 1))
                    if c == 0:
                        y_out(i, k)
                    highs((r + 2,))
                    silu(c)
                    if c:
                        hTs(c - 1)
                    highs((r + 3,))
                    if c == 2:
                        act.wait_ge(S("seltr"), i + 1)
                        nc.scalar.activation(selT, bank[7][:, 0:2 * P].rearrange("p (t n) -> p t n", t=2), ACT.Copy).then_inc(S("selT_out"), 1)
                    r += 4
                    if c:
                        highs((r, r + 1))
                        r += 2
                highs((r,))
                hTs(NF1 - 1)
                gather_out(0, i + 2)
                highs((r + 1,))
                gather_out(1, i + 2)

            def y_out(i, k):
                if isinstance(i, int) and i == 0:
                    act.wait_ge(S("moe_init"), 1)
                    act.sem_inc(S("Y_out"), 2)
                    return
                act.wait_ge(S("piece_used"), i * EXPERT_PIECES + FFN_PIECES)
                act.wait_ge(S("scat_pe"), i * 4 + 4 * k)
                for j in range(2):
                    nc.scalar.activation(Ysb[:, j * 512:(j + 1) * 512], bank[4 + j][:, :], ACT.Copy).then_inc(S("Y_out"), 1)

            gather_out(0, 1)
            gather_out(1, 1)
            expert(0, 0)
            with act.Fori(1, NE) as i:
                expert(i, 0)
            y_out(NE, 0)
            act.wait_ge(S("overflow_known"), 1)
            more = act.value_load(flag_i[0:1, 0:1], min_val=0, max_val=1)
            with act.If(more):
                with act.Fori(NE, 2 * NE) as i:
                    expert(i, 1)
                y_out(2 * NE, 1)
            act.wait_ge(S("h4"), 1)
            squares(hlat, u_tok, small[:, 32:34], "sq4")
            act.wait_ge(S("ms4"), 1)
            nc.scalar.activation(small[:, 32:34], small[:, 32:34], ACT.Sqrt).then_inc(S("rt4"), 1)
            for t in range(TT):
                act.wait_ge(S("result"), t + 1)
                act.dma_start(out[t * P:(t + 1) * P, :], u_tok[:, t]).then_inc(S("out_done"), 16)
            act.wait_ge(S("out_done"), 32)

        @block.tensor
        def _(pe):
            mm, tr = nc.tensor.matmul, nc.tensor.transpose

            def ada_round(n):
                if n == 0:
                    pe.wait_ge(S("cond_silu"), 1)
                if n >= 2:
                    pe.wait_ge(S("mod_sb_full"), 4 * (n - 1))
                for k in range(KT):
                    u = n * KT + k
                    pe.wait_ge(ada_full[u % NADA], 16 * (u // NADA + 1))
                    for q in range(4):
                        ins = mm(bank[n % 2][32 * q:32 * q + 2, :], cs[:, 1, k], ring_a[:, u % NADA, q * 512:(q + 1) * 512],
                                 start=k == 0, stop=k == KT - 1, tile_position=(0, 32 * q), skip_group_check=True)
                    ins.then_inc(S("ada_used"), 1)

            def p_transpose(b):
                pe.wait_ge(S("P_ready"), b + 1)
                for j in range(4):
                    n = 4 * b + j
                    if n >= 2 and b == 0 or b > 0:
                        pe.wait_ge(S("pt_out"), n - 1)
                    if b == 2 and j == 0:
                        pe.wait_ge(S("ut_out"), KT)
                    for i in range(4):
                        g, t = 2 * j + i // 2, (P_re, P_im)[i % 2]
                        ins = tr(psum(2 + n % 2, 4, P)[:, i], t[:, g].rearrange("p k h -> p (k h)"), ident)
                    ins.then_inc(S("pt_done"), 1)

            def u_transpose():
                pe.wait_ge(S("u_ready"), 4)
                pe.wait_ge(S("pt_out"), 8)
                for k in range(KT):
                    if k >= 2:
                        pe.wait_ge(S("ut_out"), k - 1)
                    for i in range(4):
                        ins = tr(psum(2 + k % 2, 4, P)[:, i], ut[:, 1 - i // 2, i % 2, k * P:(k + 1) * P], ident)
                    ins.then_inc(S("ut_done"), 1)

            def e_matmul(b):
                pe.wait_ge(S("U_in"), 16 * CH)
                pe.wait_ge(S("pt_out"), 4 * (b + 1))
                for j in range(2):
                    if b >= 1:
                        pe.wait_ge(S("e_out"), 3 * (2 * (b - 1) + j + 1))
                    for i in range(8):
                        g, r = 4 * j + i // 2, i % 2
                        ins = mm(psum(6 + j, 8, 2 * NCH)[:, i], E_sb[:, b % 2, g, r], U_sb[:, b * BG + g], start=True, stop=True)
                    ins.then_inc(S("e_bank"), 1)
                    if j:
                        pe.wait_ge(S("e_bank"), 2 * (b + 1))
                        pe.sem_inc(S("e_done"), 1)

            def kernels(b):
                pe.wait_ge(S("g_chain"), 6 * (b + 1))
                if b >= 1:
                    pe.wait_ge(S("T_ready"), 3 * b)
                if b == 4:
                    pe.wait_ge(S("yi_out"), 4)
                for d in range(2):
                    rows = slice(64 * d, 64 * d + 64)
                    for g in range(BG):
                        q, j = g % 4, g // 4
                        lhs = [Bb_sb[rows, r, b * BG + g:b * BG + g + 2].rearrange("p g h -> p (g h)") for r in range(2)]
                        dst = psum(4 + d, 4, P)[32 * q:32 * q + 32, j]
                        for r, t in enumerate((G_re, G_nim)):
                            ins = mm(dst, lhs[r], t[rows, b % 4 * BG + g].rearrange("p k h -> p (k h)"),
                                     start=r == 0, stop=r == 1, tile_position=(64 * d, 32 * q), skip_group_check=True)
                ins.then_inc(S("tk_done"), 1)

            def inside(b):
                pe.wait_ge(S("M_in"), 16 * CH * (b // 2 + 1))
                pe.wait_ge(S("T_ready"), 3 * (b // 4 * 4 + 4))
                if b >= 2:
                    pe.wait_ge(S("yi_out"), b - 1)
                for g in range(BG):
                    ins = mm(psum(4 + b % 2, 16, NCH)[:, g], M_sb[:, b % 2, g], U_sb[:, b * BG + g, NCH:2 * NCH], start=True, stop=True)
                ins.then_inc(S("m_done"), 1)

            def from_states(h):
                pe.wait_ge(S("srhs_done"), 2 * (h + 1))
                if h:
                    pe.wait_ge(S("y_ready"), 2)
                for g in range(HG):
                    for r, t in enumerate((G_re, G_nim)):
                        ins = mm(psum(6 + g // 16, 16, NCH)[:, g % 16], t[:, g].rearrange("p k h -> p (k h)"), S_rhs[:, r, g],
                                 start=r == 0, stop=r == 1)
                ins.then_inc(S("y_done"), 1)

            pe.wait_ge(S("consts_in"), 16)
            ada_round(0)
            p_transpose(0)
            p_transpose(1)
            u_transpose()
            ada_round(1)
            for b in range(4):
                if b >= 2:
                    p_transpose(b)
                e_matmul(b)
            ada_round(2)
            ada_round(3)
            for b in range(4):
                kernels(b)
            inside(0)
            inside(1)
            ada_round(4)
            inside(2)
            inside(3)
            from_states(0)
            ada_round(5)
            for b in range(4, 8):
                p_transpose(b)
                e_matmul(b)
            for b in range(4, 8):
                kernels(b)
            for b in range(4, 8):
                inside(b)
            from_states(1)

            pe.wait_ge(S("zT_in"), 128)
            for j in range(4):
                t, c = j // 2, j % 2
                if j == 0:
                    pe.wait_ge(S("mod_sb_full"), 24)
                if j >= 2:
                    pe.wait_ge(S("zt_out"), j - 1)
                for k in range(4):
                    ins = tr(psum(j % 2, 4, P)[:, k], zT[:, 4 * c + k, t * P:(t + 1) * P], ident)
                ins.then_inc(S("zt_done"), 1)
            pe.wait_ge(S("glu_in"), 16)
            pe.wait_ge(S("y_ready"), 4)
            for j in range(4):
                t, c = j // 2, j % 2
                for k in range(KT):
                    ins = mm(bank[4 + j][:, :], zT[:, k, t * P:(t + 1) * P], glu_sb[:, k, c * 512:(c + 1) * 512],
                             start=k == 0, stop=k == KT - 1)
                ins.then_inc(S("glu_pe"), 1)

            def x_transpose(base, read):
                for j in range(4):
                    if j >= 2:
                        pe.wait_ge(S(read), base + j - 1)
                    for i in range(4):
                        ins = tr(psum(j % 2, 4, P)[:, i], u_tok[:, i % 2, (2 * j + i // 2) * P:(2 * j + i // 2 + 1) * P], ident)
                    ins.then_inc(S("xt_done"), 1)

            pe.wait_ge(S("u1_ready"), 2)
            x_transpose(0, "x_lo")
            pe.wait_ge(S("x_lo"), 4)

            def product(dst, x, w, start, stop):
                (xh, xl), (wh, wl) = x, w
                mm(dst, xh, wh, start=start, stop=False)
                mm(dst, xh, wl, start=False, stop=False)
                return mm(dst, xl, wh, start=False, stop=stop)

            def piece(b, o, n):
                return w_hi[:, b, o:o + n], w_lo[:, b, o:o + n]

            def ffn_in(bk, n, b):
                for half in range(2):
                    pe.wait_ge(S("low"), n + (half + 1))
                    for t in range(TT):
                        for k in range(4):
                            kk = 4 * half + k
                            ins = product(bank[bk][:, t * FC0:(t + 1) * FC0], (x_hi[:, kk, t * P:(t + 1) * P], x_lo[:, kk, t * P:(t + 1) * P]),
                                          piece((b + half) % NPIECE, k * FC0, FC0), t == 0 and kk == 0, t == 1 and kk == KT - 1)
                    ins.then_inc(S("piece_used"), 1)

            def ffn_gate(c, m, b):
                if not (isinstance(c, int) and c == 0):
                    pe.wait_ge(S("f_silu"), c)
                ffn_in(4, 2 * m, b)

            def ffn_up(c, m, b):
                if not (isinstance(c, int) and c == 0):
                    pe.wait_ge(S("f_h"), c)
                ffn_in(5, 2 * m, b)

            def ffn_tr(c):
                pe.wait_ge(S("f_h"), c + 1)
                if not (isinstance(c, int) and c == 0):
                    pe.wait_ge(S("f_hl"), c)
                for i in range(4):
                    ins = tr(psum(6, 4, P)[:, i], h_sb[:, (i % 2) * FC0 + (i // 2) * P:(i % 2) * FC0 + (i // 2 + 1) * P], ident)
                ins.then_inc(S("f_tr"), 1)

            def ffn_down(c, m, b, first=False, last=False):
                pe.wait_ge(S("f_hl"), c + 1)
                for f in range(2):
                    pe.wait_ge(S("low"), 2 * m + (f + 1))
                    for j in range(4):
                        t, n = j // 2, j % 2
                        ins = product(bank[j][:, :], (h_hi[:, 2 * f + t], h_lo[:, 2 * f + t]), piece((b + f) % NPIECE, n * 512, 512),
                                      first and f == 0, last and f == 1)
                    ins.then_inc(S("piece_used"), 1)

            def ffn_chunk(c, b, first=False):
                ffn_gate(c, 3 * c - 1, b)
                ffn_tr(c - 1)
                ffn_up(c, 3 * c, (b + 2) % NPIECE)
                ffn_down(c - 1, 3 * c + 1, (b + 4) % NPIECE, first=first)

            ffn_gate(0, 0, 0)
            ffn_up(0, 1, 2)
            ffn_chunk(1, 4, first=True)
            ffn_chunk(2, 4)
            with pe.Fori(1, NF0 // 2) as i:
                ffn_chunk(2 * i + 1, 4)
                ffn_chunk(2 * i + 2, 4)
            ffn_tr(NF0 - 1)
            ffn_down(NF0 - 1, FFN_UNITS - 1, 2 * (FFN_UNITS - 1) % NPIECE, last=True)

            pe.wait_ge(S("u2_ready"), 1)
            pe.wait_ge(S("pool_in"), 48)
            for j in range(4):
                if j >= 2:
                    pe.wait_ge(S("xt_out"), j - 1)
                for i in range(2):
                    k = 2 * j + i
                    for t in range(TT):
                        ins = mm(psum(j % 2, 2, SEQ)[:, i], u_tok[:, t, k * P:(k + 1) * P], poolP[:, j, t], start=t == 0, stop=t == 1)
                ins.then_inc(S("xt_done"), 1)
            pe.wait_ge(S("xt_out"), 4)
            for t in range(TT):
                for g in range(4):
                    for k in range(2):
                        ins = mm(bank[4 + 2 * t + g // 2][:, (g % 2) * 256:(g % 2) * 256 + 256], xT[:, 2 * g + k, t * P:(t + 1) * P],
                                 poolw[:, g, k], start=k == 0, stop=k == 1)
            ins.then_inc(S("pool_pe"), 1)
            pe.wait_ge(S("u3_ready"), 1)
            x_transpose(4, "xt_out")
            pe.wait_ge(S("xt_out"), 8)
            for t in range(TT):
                for k in range(KT):
                    ins = mm(psum(2, 64, NE)[:, t], xT[:, k, t * P:(t + 1) * P], rt_sb[:, k], start=k == 0, stop=k == KT - 1)
            ins.then_inc(S("logits"), 1)
            pe.wait_ge(S("mask"), 1)
            M_ = rb[:, 8]
            mm(psum(3, 64, NE)[:, 0], tri, M_[:, 0], start=True, stop=True)
            mm(psum(3, 64, NE)[:, 1], ones, M_[:, 0], start=True, stop=False)
            mm(psum(3, 64, NE)[:, 1], tri, M_[:, 1], start=False, stop=True)
            mm(psum(3, 64, NE)[:, 2], ones, M_[:, 0], start=True, stop=False)
            mm(psum(3, 64, NE)[:, 2], ones, M_[:, 1], start=False, stop=True).then_inc(S("rank_pe"), 1)

            def gather(half, n, zero=False):
                if half == 0:
                    pe.wait_ge(S("sel_ready"), n)
                else:
                    pe.wait_ge(S("gather_lo0"), n)
                for k in range(4):
                    for t in range(TT):
                        kk = 4 * half + k
                        ins = mm(psum(7, 4, P)[:, k], u_tok[:, t, kk * P:(kk + 1) * P], sel[:, t], start=t == 0, stop=t == 1)
                ins.then_inc(S(f"gather{half}"), 1)

            def scatter(r, n, y):
                if y is not None:
                    pe.wait_ge(S("Y_out"), y)
                if not (isinstance(n, int) and n == 0):
                    pe.wait_ge(S("scat_acc"), n)
                t, c = r // 2, r % 2
                mm(bank[7][:, :], selT[:, t], Ysb[:, c * 512:(c + 1) * 512], start=True, stop=True).then_inc(S("scat_pe"), 1)

            def expert(i, k):
                zero = isinstance(i, int) and i == 0

                def unit(kind, c, half):
                    return 2 * ORDER.index((kind, c, half))

                def ready(n):
                    pe.wait_ge(S("low"), i * EXPERT_PIECES + (FFN_PIECES + n + 1))

                def gate_up(kind, c):
                    back = 0 if c == 0 else 1
                    if not (zero and c - back <= 0):
                        pe.wait_ge(S("x_silu" if kind == "gate" else "x_h"), i * NF1 + c - back)
                    bk = (0 if kind == "gate" else 2) + c % 2
                    for kk in range(0, KT, 2):
                        n = unit(kind, c, kk // 4) + kk % 4 // 2
                        ready(n)
                        for k in (kk, kk + 1):
                            ins = product(bank[bk][:, :], (x_hi[:, k, 0:P], x_lo[:, k, 0:P]),
                                          piece(n % NPIECE, (k % 2) * FC1, FC1), k == 0, k == KT - 1)
                        ins.then_inc(S("piece_used"), 1)

                def trans(c):
                    pe.wait_ge(S("x_h"), i * NF1 + c + 1)
                    if not (zero and c == 0):
                        pe.wait_ge(S("x_hl"), i * NF1 + c)
                    for f in range(4):
                        ins = tr(psum(6, 4, P)[:, f], h_sb[:, f * P:(f + 1) * P], ident)
                    ins.then_inc(S("x_tr"), 1)

                def down(c, fs):
                    if fs[0] == 0:
                        pe.wait_ge(S("x_hl"), i * NF1 + c + 1)
                        if c == 0:
                            pe.wait_ge(S("Y_out"), 2 * i + 2 + 2 * k)
                    for f in fs:
                        n = unit("down", c, f // 2) + f % 2
                        ready(n)
                        for h in range(2):
                            ins = product(bank[4 + h][:, :], (h_hi[:, f], h_lo[:, f]), piece(n % NPIECE, h * 512, 512),
                                          c == 0 and f == 0, c == NF1 - 1 and f == 3)
                        ins.then_inc(S("piece_used"), 1)

                pe.wait_ge(S("gather_lo1"), i + 1)
                for c in range(NF1):
                    gate_up("gate", c)
                    if c < 2:
                        scatter(2 * c, i * 4 + 4 * k + 2 * c, 2 * i + 2 + 2 * k)
                    if c == 2:
                        pe.wait_ge(S("scat_acc"), i * 4 + 4 * k + 4)
                        for t in range(TT):
                            ins = tr(bank[7][:, t * P:(t + 1) * P], sel[:, t], ident)
                        ins.then_inc(S("seltr"), 1)
                    if c:
                        trans(c - 1)
                    gate_up("up", c)
                    if c < 2:
                        scatter(2 * c + 1, i * 4 + 4 * k + 2 * c + 1, None)
                    if c:
                        down(c - 1, (0, 1, 2, 3))
                trans(NF1 - 1)
                pe.wait_ge(S("selT_out"), i + 1)
                gather(0, i + 2)
                down(NF1 - 1, (0, 1))
                gather(1, i + 2)
                down(NF1 - 1, (2, 3))

            gather(0, 1)
            gather(1, 1)
            expert(0, 0)
            with pe.Fori(1, NE) as i:
                expert(i, 0)
            pe.wait_ge(S("gather_lo1"), NE + 1)
            for r in range(4):
                scatter(r, 4 * NE + r, 2 * NE + 2)
            pe.wait_ge(S("overflow_known"), 1)
            more = pe.value_load(flag_i[0:1, 0:1], min_val=0, max_val=1)
            with pe.If(more):
                with pe.Fori(NE, 2 * NE) as i:
                    expert(i, 1)
                pe.wait_ge(S("gather_lo1"), 2 * NE + 1)
                for r in range(4):
                    scatter(r, 8 * NE + 4 + r, 4 * NE + 4)

        @block.vector
        def _(dve):
            V = nc.vector
            tt, ts, stt = V.tensor_tensor, V.tensor_scalar, V.scalar_tensor_tensor
            chain = [0]

            def link(ins, more=None):
                chain[0] += 1
                ins.then_inc(S("dve_chain"), 1)
                dve.wait_ge(S("dve_chain"), chain[0])

            dve.wait_ge(S("lam_in"), 48)
            dve.wait_ge(S("step_exp"), 1)
            V.memset(Bb_sb[:, :, GROUPS], 0.0)
            stt(tmp[:, 6], tmp[:, 0], 0.5 ** SQ, tmp[:, 3], MUL, MUL)
            link(stt(tmp[:, 7], tmp[:, 1], 0.5 ** SQ, tmp[:, 3], MUL, MUL))
            V.tensor_copy(tmp[:, 9], tmp[:, 6])
            ts(tmp[:, 8], tmp[:, 7], -1.0, None, MUL)
            V.memset(tmp[:, 10], 1.0)
            link(V.memset(tmp[:, 11], 0.0))
            quad = lambda a: tmp[:, a:a + 4].rearrange("p (c r) g -> p c r g", c=2)
            twice = lambda a: tmp[:, a:a + 2].unsqueeze(2).to_broadcast([P, 2, 2, GROUPS])
            for n in range(ORD, 1, -1):
                stt(quad(12)[:, 0], twice(10)[:, 0], 1.0 / n, quad(6)[:, 0], MUL, MUL)
                link(stt(quad(12)[:, 1], twice(10)[:, 1], 1.0 / n, quad(6)[:, 1], MUL, MUL))
                link(tt(tmp[:, 10:12], tmp[:, 12:14], tmp[:, 14:16], ADD))
                link(ts(tmp[:, 10], tmp[:, 10], 1.0, None, ADD))
            link(tt(quad(12), twice(10), quad(6), MUL))
            link(tt(tmp[:, 16:18], tmp[:, 12:14], tmp[:, 14:16], ADD))
            for n in range(SQ):
                ts(tmp[:, 6:10:3], tmp[:, 16:17].to_broadcast([P, 2, GROUPS]), 2.0, None, ADD)
                V.tensor_copy(tmp[:, 7], tmp[:, 17])
                link(ts(tmp[:, 8], tmp[:, 17], -1.0, None, MUL))
                link(tt(quad(12), twice(16), quad(6), MUL))
                link(tt(tmp[:, 16:18], tmp[:, 12:14], tmp[:, 14:16], ADD))
            V.memset(Npow[:, 0, 0], 1.0)
            V.memset(Npow[:, 0, 1], 0.0)
            ts(Npow[:, 1, 0], tmp[:, 16], 1.0, None, ADD)
            V.tensor_copy(Npow[:, 1, 1], tmp[:, 17])
            ts(tmp[:, 28], tmp[:, 16], 1.0, None, ADD)
            link(V.tensor_copy(tmp[:, 29], tmp[:, 17]))
            for m in (1, 2, 4):
                ts(tmp[:, 18], Npow[:, m, 1], -1.0, None, MUL)
                link(V.tensor_copy(tmp[:, 19], Npow[:, m, 0]))
                lo = Npow[:, 1:1 + m]
                hi = Npow[:, 1 + m:1 + 2 * m]
                part = tmp[:, 20:20 + 2 * m].rearrange("p (m r) g -> p m r g", m=m)
                shape = [P, m, 2, GROUPS]
                tt(hi, lo[:, :, 0:1].to_broadcast(shape), Npow[:, m:m + 1].to_broadcast(shape), MUL)
                link(tt(part, lo[:, :, 1:2].to_broadcast(shape), tmp[:, 18:20].unsqueeze(1).to_broadcast(shape), MUL))
                link(tt(hi, hi, part, ADD))
            V.tensor_copy(LT[:, 0], Npow[:, CH])
            ts(LT[:, 1, 0], Npow[:, CH, 1], -1.0, None, MUL)
            V.tensor_copy(LT[:, 1, 1], Npow[:, CH, 0])
            V.tensor_copy(pw[0:64, 0:2].rearrange("p r g k -> p k r g"), Npow[0:64, 0:CH])
            link(V.tensor_copy(pw[64:P, 0:2].rearrange("p r g k -> p k r g"), Npow[64:P, 0:CH][:, ::-1]))
            ts(pw[:, 2], pw[:, 1], -1.0, None, MUL)
            ts(pw[:, 3], pw[:, 0], -1.0, None, MUL).then_inc(S("pw_ready"), 1)
            er, ei, lr, li = tmp[:, 16], tmp[:, 17], tmp[:, 0], tmp[:, 1]
            tt(tmp[:, 4], lr, lr, MUL)
            link(tt(tmp[:, 5], li, li, MUL))
            link(tt(tmp[:, 4], tmp[:, 4], tmp[:, 5], ADD))
            link(V.reciprocal(tmp[:, 5], tmp[:, 4]))
            tt(tmp[:, 6], er, lr, MUL)
            tt(tmp[:, 7], ei, li, MUL)
            tt(tmp[:, 8], ei, lr, MUL)
            link(tt(tmp[:, 9], er, li, MUL))
            tt(tmp[:, 10], tmp[:, 6], tmp[:, 7], ADD)
            link(tt(tmp[:, 11], tmp[:, 8], tmp[:, 9], SUB))
            link(tt(tmp[:, 10:12], tmp[:, 10:12], tmp[:, 5:6].to_broadcast([P, 2, GROUPS]), MUL))
            tt(tmp[:, 12], tmp[:, 28], tmp[:, 10], MUL)
            tt(tmp[:, 13], tmp[:, 29], tmp[:, 11], MUL)
            tt(tmp[:, 14], tmp[:, 28], tmp[:, 11], MUL)
            link(tt(tmp[:, 15], tmp[:, 29], tmp[:, 10], MUL))
            tt(tmp[:, 18], tmp[:, 12], tmp[:, 13], SUB)
            link(tt(tmp[:, 19], tmp[:, 14], tmp[:, 15], ADD))
            dve.wait_ge(S("b_in"), 32)
            scratch = tmpP.rearrange("p a b c -> p (a b c)").rearrange("p (g h) -> p g h", h=GW)
            for dst, f in ((Bb_sb, 10), (Bp_sb, 18)):
                fr, fi = (tmp[:, f + j].unsqueeze(2).to_broadcast([P, GROUPS, GW]) for j in range(2))
                br, bi = b_raw[:, 0], b_raw[:, 1]
                re, im = dst[:, 0, 0:GROUPS], dst[:, 1, 0:GROUPS]
                tt(re, br, fr, MUL)
                link(tt(scratch, bi, fi, MUL))
                link(tt(re, re, scratch, SUB))
                tt(im, br, fi, MUL)
                link(tt(scratch, bi, fr, MUL))
                link(tt(im, im, scratch, ADD))

            def p_table(b):
                G = slice(b * BG, (b + 1) * BG)
                Br, Bi = (Bp_sb[:, j, G].unsqueeze(2).to_broadcast([P, BG, CH, GW]) for j in range(2))
                W = [pw[:, j, G].unsqueeze(3).to_broadcast([P, BG, CH, GW]) for j in range(4)]
                if b:
                    dve.wait_ge(S("pt_done"), 4 * b)
                tt(P_re, Br, W[0], MUL)
                link(tt(tmpP, Bi, W[2], MUL))
                link(tt(P_re, P_re, tmpP, ADD))
                tt(P_im, Br, W[1], MUL)
                link(tt(tmpP, Bi, W[0], MUL))
                tt(P_im, P_im, tmpP, ADD).then_inc(S("P_ready"), 1)
                dve.wait_ge(S("P_ready"), b + 1)

            def inverse_rms(cols, sq, n, name):
                dve.wait_ge(S(f"sq{name}"), n)
                src = small[:, 0:4] if name == 0 else cols
                ts(cols, src, 1.0 / D, EPS, MUL, ADD).then_inc(S(f"ms{name}"), 1)
                dve.wait_ge(S(f"rt{name}"), 1)
                link(V.reciprocal(cols, cols))

            def mod_add(n):
                dve.wait_ge(S("ada_used"), KT * (n + 1))
                dve.wait_ge(S(f"adab_in{n % 2}"), 64 * (n // 2 + 1))
                if n:
                    dve.wait_ge(S("mod_out"), 64 * n)
                for q in range(4):
                    r = slice(32 * q, 32 * q + 2)
                    tt(mod_sb[r], bank[n % 2][r, :], adab[r, n % 2], ADD).then_inc(S("mod_sb_full"), 1)

            inverse_rms(small[:, 4:8], None, 4, 0)
            p_table(0)
            mod_add(0)
            p_table(1)
            dve.wait_ge(S("bc_in"), 80)
            nrow = at(DU_off, D, of=s5_mem)
            stt(bc[:, 1], bc[:, 1], 1.0, nrow, ADD, MUL)
            link(stt(bc[:, 3], bc[:, 3], 1.0, nrow, ADD, MUL))
            for j in range(4):
                s, t = j // 2, j % 2
                src = (hlat if s == 0 else ut[:, 1])[:, t]
                link(stt(ut[:, s, t], src, small[:, 4 + j:5 + j], bc[:, 2 * s + 1], MUL, MUL))
                tt(ut[:, s, t], ut[:, s, t], bc[:, 2 * s], ADD).then_inc(S("u_ready"), 1)

            def du(h):
                dve.wait_ge(S("du_in"), 16 * CH * (h + 1))
                if h == 0:
                    dve.wait_ge(S("d_in"), 16)
                link(tt(DU, DU,
                        D_sb[:, h * HG:(h + 1) * HG].unsqueeze(2).to_broadcast([P, HG, NCH]), MUL))

            def kernels_out(b):
                dve.wait_ge(S("tk_done"), b + 1)
                if b >= 4:
                    dve.wait_ge(S("t_out"), 64)
                T_b = T_sb[:, b % 4]
                V.tensor_copy(T_b[:, :, 0:P], psum(5, 4, P)[:, 0:2]).then_inc(S("T_ready"), 1)
                V.tensor_copy(T_b[:, :, P:240], psum(4, 4, P)[:, 0:2, GW:P]).then_inc(S("T_ready"), 1)
                dve.wait_ge(S("T_ready"), 3 * b + 2)
                tt(T_b[:, :, P - GW:P], T_b[:, :, P - GW:P], psum(4, 4, P)[:, 0:2, 0:GW], ADD).then_inc(S("T_ready"), 1)

            def inside_out(b):
                q = b % 4
                dve.wait_ge(S("m_done"), b + 1)
                tt(DU[:, q * BG:(q + 1) * BG], DU[:, q * BG:(q + 1) * BG], psum(4 + b % 2, 16, NCH)[:, 0:BG], ADD).then_inc(S("yi_out"), 1)

            def scan(h):
                dve.wait_ge(S("e_out"), 24 * (h + 1))
                L8 = LT[:, :, :, h * HG:(h + 1) * HG]
                base = h * 3 * (2 * NCH - 2)
                for i in range(1, 2 * NCH - 1):
                    prev = e_sb[:, i - 1].unsqueeze(2).to_broadcast([P, 2, 2, HG])
                    tt(sc4, prev, L8, MUL).then_inc(S("scan"), 1)
                    dve.wait_ge(S("scan"), i * 3 + base - 2)
                    tt(sc2, sc4[:, 0], e_sb[:, i], ADD).then_inc(S("scan"), 1)
                    dve.wait_ge(S("scan"), i * 3 + base - 1)
                    tt(e_sb[:, i], sc2, sc4[:, 1], ADD).then_inc(S("scan"), 1)
                    dve.wait_ge(S("scan"), i * 3 + base)
                dve.sem_inc(S("scan_done"), 1)

            def y_out(h):
                dve.wait_ge(S("y_done"), h + 1)
                dve.wait_ge(S("yi_out"), 4 * (h + 1))
                if h:
                    dve.wait_ge(S("z_out"), 16)
                for j in range(2):
                    tt(y_sb[:, 16 * j:16 * j + 16], psum(6 + j, 16, NCH), DU[:, 16 * j:16 * j + 16], ADD).then_inc(S("y_ready"), 1)

            mod_add(1)
            p_table(2)
            p_table(3)
            du(0)
            mod_add(2)
            mod_add(3)
            for b in range(4):
                kernels_out(b)
            scan(0)
            mod_add(4)
            for b in range(4):
                inside_out(b)
            p_table(4)
            y_out(0)
            mod_add(5)
            for b in range(5, 8):
                p_table(b)
            dve.wait_ge(S("y_ready"), 2)
            du(1)
            for b in range(4, 8):
                kernels_out(b)
            scan(1)
            for b in range(4, 8):
                inside_out(b)
            y_out(1)

            dve.wait_ge(S("bd_in"), 64)
            quarters = lambda v: v.rearrange("p t (c n) -> p (t c) n", c=2)
            uq, zq, hq, aq = quarters(u_tok), quarters(z_tok), quarters(hlat), quarters(acc)
            half = lambda row, j: row[:, (j % 2) * 512:(j % 2 + 1) * 512]
            for j in range(4):
                dve.wait_ge(S("glu_pe"), j + 1)
                tt(uq[:, j], bank[4 + j][:, :], half(bd[:, 0], j), ADD).then_inc(S("gate_in"), 1)
            for j in range(4):
                dve.wait_ge(S("sigm"), j + 1)
                dve.wait_ge(S("zt_out"), j + 1)
                link(tt(uq[:, j], uq[:, j], zq[:, j], MUL))
                link(tt(uq[:, j], uq[:, j], half(bd[:, 1], j), MUL))
                ins = tt(hq[:, j], hq[:, j], uq[:, j], ADD)
                link(ins)
            dve.sem_inc(S("glu_done"), 1)
            dve.sem_inc(S("h1"), 1)

            def norm(cols, name, shift, scale, gain, rows1, rows2, done, n):
                inverse_rms(cols, None, 2, name)
                dve.wait_ge(S("bd_in"), rows1)
                link(stt(scale, scale, 1.0, gain, ADD, MUL))
                dve.wait_ge(S("bd_in"), rows2)
                for t in range(TT):
                    link(stt(u_tok[:, t], hlat[:, t], cols[:, t:t + 1], scale, MUL, MUL))
                    link(tt(u_tok[:, t], u_tok[:, t], shift, ADD))
                dve.sem_inc(S(done), n)

            norm(small[:, 8:10], 1, bd[:, 0], bd[:, 2], bd[:, 3], 64, 96, "u1_ready", 2)

            for j in range(4):
                dve.wait_ge(S("x_hi"), j + 1)
                tt(x_lo[:, 2 * j:2 * j + 2], psum(j % 2, 2, SEQ), x_hi[:, 2 * j:2 * j + 2].bitcast(F32), SUB).then_inc(S("x_lo"), 1)

            def low(n, b, slot, half):
                dve.wait_ge(S("high"), n + 1)
                tt(w_lo[:, b], ring[:, slot, half * PIECE:(half + 1) * PIECE], w_hi[:, b].bitcast(F32), SUB).then_inc(S("low"), 1)

            def ffn_low(m, slot):
                for half in range(2):
                    low(2 * m + half, (2 * slot + half) % NPIECE, slot, half)

            def ffn_h(c):
                dve.wait_ge(S("f_silu"), c + 1)
                dve.wait_ge(S("piece_used"), ffn_pieces("up", c))
                if not (isinstance(c, int) and c == 0):
                    dve.wait_ge(S("f_tr"), c)
                tt(h_sb, sg, bank[5][:, :], MUL).then_inc(S("f_h"), 1)

            def ffn_hl(c):
                dve.wait_ge(S("f_hT"), c + 1)
                tt(h_lo[:], psum(6, 4, P), h_hi[:].bitcast(F32), SUB).then_inc(S("f_hl"), 1)

            def ffn_chunk(c, s):
                ffn_low(3 * c - 1, s)
                ffn_low(3 * c, (s + 1) % 6)
                ffn_hl(c - 1)
                ffn_low(3 * c + 1, (s + 2) % 6)
                ffn_h(c)

            ffn_low(0, 0)
            ffn_low(1, 1)
            ffn_h(0)
            ffn_chunk(1, 2)
            ffn_chunk(2, 5)
            with dve.Fori(1, NF0 // 2) as i:
                ffn_chunk(2 * i + 1, 2)
                ffn_chunk(2 * i + 2, 5)
            ffn_low(FFN_UNITS - 1, (FFN_UNITS - 1) % 6)
            ffn_hl(NF0 - 1)
            dve.wait_ge(S("piece_used"), FFN_PIECES)
            for j in range(4):
                link(tt(uq[:, j], bank[j][:, :], half(bd[:, 1], j), MUL))
                link(tt(hq[:, j], hq[:, j], uq[:, j], ADD))
            dve.sem_inc(S("h2"), 1)

            norm(small[:, 12:14], 2, bd[:, 0], bd[:, 1], bd[:, 3], 160, 160, "u2_ready", 1)
            dve.wait_ge(S("pool_pe"), 1)
            dve.wait_ge(S("bd_in"), 192)
            for j in range(4):
                link(tt(uq[:, j], bank[4 + j][:, :], half(bd[:, 0], j), ADD))
                link(tt(uq[:, j], uq[:, j], half(bd[:, 1], j), MUL))
                link(tt(uq[:, j], uq[:, j], half(bd[:, 2], j), MUL))
                link(tt(hq[:, j], hq[:, j], uq[:, j], ADD))
            dve.sem_inc(S("h3"), 1)
            norm(small[:, 16:18], 3, bd[:, 0], bd[:, 1], bd[:, 3], 256, 256, "u3_ready", 1)

            R = lambda k: rb[:, k]
            V.memset(acc, 0.0)
            V.memset(selT, 0.0)
            V.memset(Ysb, 0.0).then_inc(S("moe_init"), 1)
            V.memset(rankx[:, :, 2 * NE], -5.0)
            V.memset(combx, 0.0)
            for t in range(TT):
                link(ts(R(4)[:, t], iota[:, 0:NE], -float(NE), None, ADD))
            dve.wait_ge(S("logits"), 1)
            link(V.tensor_copy(R(0), psum(2, 64, NE)[:, 0:TT]))

            def best(src, top, eq, key, idx, mask):
                wide = [P, TT, NE]
                link(V.reduce_max(top, src, AX.X))
                link(tt(eq, src, top.unsqueeze(2).to_broadcast(wide), ALU.is_equal))
                link(tt(key, eq, R(4), MUL))
                link(V.tensor_reduce(idx, key, AX.X, ALU.min))
                link(tt(mask, R(4), idx.unsqueeze(2).to_broadcast(wide), ALU.is_equal))

            best(R(0), small[:, 18:20], R(1), R(2), small[:, 26:28], R(3))
            link(stt(R(5), R(3), -3.0e38, R(0), MUL, ADD))
            best(R(5), small[:, 20:22], R(1), R(2), small[:, 28:30], R(6))
            tt(small[:, 22:24], small[:, 20:22], small[:, 18:20], SUB).then_inc(S("top2"), 1)
            tt(R(8), R(3), R(6), ADD).then_inc(S("mask"), 1)
            dve.wait_ge(S("top_exp"), 1)
            dve.wait_ge(S("mask"), 1)
            link(ts(small[:, 30:32], small[:, 24:26], 1.0, None, ADD))
            link(V.reciprocal(small[:, 30:32], small[:, 30:32]))
            link(tt(small[:, 34:36], small[:, 24:26], small[:, 30:32], MUL))
            wide = [P, TT, NE]
            tt(R(9), R(3), small[:, 30:32].unsqueeze(2).to_broadcast(wide), MUL)
            link(tt(R(10), R(6), small[:, 34:36].unsqueeze(2).to_broadcast(wide), MUL))
            tt(combx[:, :, 1:NE + 1], R(9), R(10), ADD)
            tt(combx[:, :, NE + 2:2 * NE + 2], R(9), R(10), ADD)
            dve.wait_ge(S("rank_pe"), 1)
            link(stt(R(11), psum(3, 64, NE)[:, 0:TT], -1000.0, R(8), ADD, MUL))
            ts(rankx[:, :, 0:NE], R(11), 1000.0, None, ADD)
            link(ts(rankx[:, :, NE:2 * NE], R(11), 1000.0 - P, None, ADD))
            link(V.reduce_max(small[:, 36:37], psum(3, 64, NE)[:, 2], AX.X))
            ts(flag_i[:, 0:1], small[:, 36:37], float(P), None, ALU.is_gt).then_inc(S("overflow_known"), 1)

            def select(col, n):
                for t in range(TT):
                    ins = ts(sel[:, t], iota, rankx[:, t, col], None, ALU.is_equal)
                    if t:
                        ins.then_inc(S("sel_ready"), 1)

            def accumulate(r, n, col):
                dve.wait_ge(S("scat_pe"), n)
                stt(aq[:, r], bank[7][:, :], combx[:, r // 2, col], aq[:, r], MUL, ADD).then_inc(S("scat_acc"), 1)

            def gather_low(half, n):
                dve.wait_ge(S(f"gather_hi{half}"), n)
                tt(x_lo[:, 4 * half:4 * half + 4, 0:P], psum(7, 4, P), x_hi[:, 4 * half:4 * half + 4, 0:P].bitcast(F32), SUB).then_inc(S(f"gather_lo{half}"), 1)

            def expert(i, k):
                zero = isinstance(i, int) and i == 0

                def lows(*units):
                    for r in units:
                        for half in range(2):
                            low(i * EXPERT_PIECES + (FFN_PIECES + 2 * r + half), (2 * r + half) % NPIECE, r % NSLOT, half)

                def product_h(c):
                    dve.wait_ge(S("x_silu"), i * NF1 + c + 1)
                    dve.wait_ge(S("piece_used"), expert_pieces(i, "up", c))
                    if not (zero and c == 0):
                        dve.wait_ge(S("x_tr"), i * NF1 + c)
                    tt(h_sb, sg, bank[2 + c % 2][:, :], MUL).then_inc(S("x_h"), 1)

                def h_low(c):
                    dve.wait_ge(S("x_hT"), i * NF1 + c + 1)
                    tt(h_lo[:], psum(6, 4, P), h_hi[:].bitcast(F32), SUB).then_inc(S("x_hl"), 1)

                r = 0
                for c in range(NF1):
                    lows(r, r + 1, r + 2)
                    if c:
                        h_low(c - 1)
                    lows(r + 3)
                    if c < 2:
                        accumulate(2 * c, i * 4 + 4 * k + 2 * c + 1, bass.ds(i + k, 1))
                    r += 4
                    if c:
                        lows(r)
                    product_h(c)
                    if c < 2:
                        accumulate(2 * c + 1, i * 4 + 4 * k + 2 * c + 2, bass.ds(i + k, 1))
                    if c == 3:
                        dve.wait_ge(S("seltr"), i + 1)
                        select(bass.ds(i + 1, 1), i + 2)
                    if c:
                        lows(r + 1)
                        r += 2
                lows(r)
                h_low(NF1 - 1)
                gather_low(0, i + 2)
                lows(r + 1)
                gather_low(1, i + 2)

            select(bass.ds(0, 1), 1)
            gather_low(0, 1)
            gather_low(1, 1)
            expert(0, 0)
            with dve.Fori(1, NE) as i:
                expert(i, 0)
            for r in range(4):
                accumulate(r, 4 * NE + r + 1, bass.ds(NE, 1))
            dve.wait_ge(S("overflow_known"), 1)
            more = dve.value_load(flag_i[0:1, 0:1], min_val=0, max_val=1)
            with dve.If(more):
                with dve.Fori(NE, 2 * NE) as i:
                    expert(i, 1)
                for r in range(4):
                    accumulate(r, 8 * NE + 4 + r + 1, bass.ds(2 * NE + 1, 1))
            link(V.memset(small[:, 40:41], 0.0))
            for j in range(4):
                link(tt(uq[:, j], aq[:, j], half(bd[:, 2], j), MUL))
                link(tt(hq[:, j], hq[:, j], uq[:, j], ADD))
            dve.sem_inc(S("h4"), 1)
            inverse_rms(small[:, 32:34], None, 2, 4)
            dve.wait_ge(S("bd_in"), 272)
            for t in range(TT):
                stt(u_tok[:, t], hlat[:, t], small[:, 32 + t:33 + t], bd[:, 3], MUL, MUL).then_inc(S("result"), 1)


def _pool_matrix(np):
    width = 64
    m = np.zeros((4, SEQ, SEQ), np.float32)
    for g, win in enumerate((2, 4, 8, 16)):
        for tok in range(SEQ):
            row, pos = divmod(tok, width)
            lo, hi = max(pos - win // 2, 0), min(pos + win // 2, width)
            m[g, row * width + lo:row * width + hi, tok] = np.float32(1) / np.float32(hi - lo)
            m[g, tok, tok] -= np.float32(1)
    order = np.arange(SEQ).reshape(NCH, CH).T.reshape(-1)
    m = m[:, order][:, :, order]
    return np.ascontiguousarray(m.reshape(4, TT, P, SEQ).transpose(2, 0, 1, 3))


def kernel(x, c, ctx, c_ctx, ada_w, ada_b, norm_mix, norm_ffn, norm_final,
           s5_lambda_re, s5_lambda_im, s5_log_step, s5_b_re, s5_b_im, s5_c_re, s5_c_im,
           s5_d, s5_glu_w, s5_glu_b, pool_w, pool_b, pool_scale, fnet_w, fnet_b,
           ffn_w_gate, ffn_w_up, ffn_w_down, moe_router, moe_w_gate, moe_w_up, moe_w_down):
    import numpy as np
    import concourse.bacc as bacc
    from concourse.bass_utils import run_bass_kernel_spmd

    A = np.asarray

    def rows(v):
        return A(v).reshape(NCH, CH, D).transpose(1, 0, 2).reshape(SEQ, D)

    def lam(v):
        return A(v)[0].transpose(0, 2, 1).reshape(P, GROUPS)

    eye = np.eye(P, dtype=np.float32)
    tri = np.triu(np.ones((P, P), np.float32), 1)
    iota = np.tile(np.arange(P, dtype=np.float32), (P, 1))
    arrays = dict(
        x_in=rows(x), ctx_in=rows(ctx),
        cond_in=np.stack([A(c)[0], A(c_ctx)], 1).reshape(KT, P, 2).transpose(1, 0, 2),
        ada_w=A(ada_w), ada_b=A(ada_b), norm_mix=A(norm_mix), norm_ffn=A(norm_ffn), norm_final=A(norm_final)[None],
        lam_re=lam(s5_lambda_re), lam_im=lam(s5_lambda_im),
        log_step=np.broadcast_to(A(s5_log_step)[0][:, None, :], (2, NST, GROUPS)).reshape(P, GROUPS),
        b_re=A(s5_b_re)[0].transpose(0, 2, 1, 3).reshape(P, GROUPS, GW),
        b_im=A(s5_b_im)[0].transpose(0, 2, 1, 3).reshape(P, GROUPS, GW),
        c_re=A(s5_c_re)[0].transpose(0, 3, 1, 2).reshape(P, GROUPS, GW),
        c_im=A(s5_c_im)[0].transpose(0, 3, 1, 2).reshape(P, GROUPS, GW),
        d_skip=np.tile(A(s5_d)[0].reshape(GROUPS, GW).T, (CH, 1)),
        glu_w=A(s5_glu_w)[0], glu_b=A(s5_glu_b), pool_w=A(pool_w)[0], pool_b=A(pool_b), pool_scale=A(pool_scale),
        w_gate=A(ffn_w_gate)[0], w_up=A(ffn_w_up)[0], w_down=A(ffn_w_down)[0], router=A(moe_router)[0],
        e_gate=A(moe_w_gate)[0], e_up=A(moe_w_up)[0], e_down=A(moe_w_down)[0],
        consts=np.stack([eye, tri, np.ones((P, P), np.float32), iota], 1),
        pool_mat=_pool_matrix(np),
    )
    arrays = {k: np.ascontiguousarray(v) for k, v in arrays.items()}
    nc = bacc.Bacc("TRN2", target_bir_lowering=False, num_devices=1)
    aps = {k: nc.dram_tensor(k, v.shape, mybir.dt.from_np(v.dtype), kind="ExternalInput").ap() for k, v in arrays.items()}
    out = nc.dram_tensor("out", (SEQ, D), mybir.dt.float32, kind="ExternalOutput").ap()
    build(nc, out=out, **aps)
    got = run_bass_kernel_spmd(nc, [arrays], core_ids=[0]).results[0]["out"]
    return got.reshape(CH, NCH, D).transpose(1, 0, 2).reshape(1, SEQ, D)
```

```python
import concourse.bass as bass
from concourse import mybir
from contextlib import ExitStack

P = 128
D = 1024
SEQ = 256
TT = SEQ // P
KT = D // P
GROUPS, GW, NST = 64, 16, 64
CH = 8
NCH = SEQ // CH
HG = GROUPS // 2
BG = 8
NMOD = 6
DFF = 2816
FC0 = 256
NF0 = DFF // FC0
NE = 8
DFE = 3584
FC1 = 512
NF1 = DFE // FC1
NSLOT = 7
SLOT = 2048
NPIECE = 6
PIECE = 1024
NADA = 3
EPS = 1e-6
SQ = 6
ORD = 7


def build(nc, x_in, ctx_in, cond_in, ada_w, ada_b, norm_mix, norm_ffn, norm_final,
          lam_re, lam_im, log_step, b_re, b_im, c_re, c_im, d_skip, glu_w, glu_b,
          pool_w, pool_b, pool_scale, w_gate, w_up, w_down, router, e_gate, e_up, e_down,
          consts, pool_mat, out):
    F32, I32 = mybir.dt.float32, mybir.dt.int32
    ALU, ACT, AX = mybir.AluOpType, mybir.ActivationFunctionType, mybir.AxisListType
    MUL, ADD, SUB = ALU.mult, ALU.add, ALU.subtract

    mod_d = nc.dram_tensor("mod_scratch", (2, 2, NMOD * D), F32).ap()
    u_d = nc.dram_tensor("u_scratch", (GROUPS, GW, CH, 2 * NCH), F32).ap()
    t_d = nc.dram_tensor("kernel_scratch", (GROUPS, GW, 240), F32).ap()
    z_d = nc.dram_tensor("z_scratch", (SEQ, D), F32).ap()

    ctx = ExitStack()
    with ctx:
        mem = ctx.enter_context(nc.sbuf_tensor("common_mem", [P, 2560 + P], F32))
        sems = {}

        def S(name):
            if name not in sems:
                sems[name] = ctx.enter_context(nc.semaphore(name))
            return sems[name]

        def at(o, *dims, of=None):
            n = 1
            for d in dims:
                n *= d
            v = (of or mem)[:, o:o + n]
            if len(dims) == 1:
                return v
            names = "abcd"[:len(dims)]
            return v.rearrange(f"p ({' '.join(names)}) -> p {' '.join(names)}", **{k: d for k, d in zip(names, dims)})

        ident, tri, ones, iota = (at(i * P, P) for i in range(4))
        hlat = at(512, TT, D)
        flag_i = ctx.enter_context(nc.sbuf_tensor("flag", [P, 8], I32))
        small = at(2560, P)
        TOTAL = 52980 - 2560 - P
        with nc.sbuf_tensor("s5_mem", [P, TOTAL], F32) as s5_mem:
            pass
        era = [s5_mem]
        o = [0]

        def take(*dims):
            n = 1
            for d in dims:
                n *= d
            o[0] += n
            return at(o[0] - n, *dims, of=era[0])

        G_re = take(HG, CH, GW)
        G_nim = take(HG, CH, GW)
        E_off = o[0]
        E_sb = take(2, BG, 2, P)
        b_raw = at(E_off, 2, GROUPS, GW, of=s5_mem)
        e_off = o[0]
        e_sb = take(2 * NCH, 2, HG)
        bc = at(e_off, 4, D, of=s5_mem)
        U_off = o[0]
        U_sb = take(GROUPS, 2 * NCH)
        tmp = at(U_off, 32, GROUPS, of=s5_mem)
        M_off = o[0]
        M_sb = take(2, BG, P)
        S_rhs = take(2, HG, NCH)
        ut = at(M_off, 2, TT, D, of=s5_mem)
        P_re = take(BG, CH, GW)
        P_im = take(BG, CH, GW)
        C_sb = take(2, GROUPS, GW)
        Bp_sb = take(2, GROUPS, GW)
        Bb_sb = take(2, GROUPS + 1, GW)
        pw = take(4, GROUPS, CH)
        T_sb = take(4, 2, 240)
        T_mid = take(4, 2, GW)
        DU_off = o[0]
        y_in = take(BG, CH, GW)
        y_sb = take(CH, BG * GW)
        stage = at(DU_off, 4, 512, of=s5_mem)
        N_off = o[0]
        tmpP = take(BG, CH, GW)
        tmpG = take(BG, CH, GW)
        Npow = at(N_off, CH + 1, 2, GROUPS, of=s5_mem)
        LT = take(2, 2, GROUPS)
        sc4 = take(2, 2, HG)
        sc2 = take(2, HG)
        D_sb = take(GROUPS // 4)
        DD = take(GROUPS // 4, GW)
        adab = take(2, 512)
        mod_sb = take(512)
        cs = take(2, KT, 2)
        assert o[0] <= TOTAL - NADA * 2048, o[0]
        ring_a = at(TOTAL - NADA * 2048, NADA, 2048, of=s5_mem)
        LATE = 18000
        late_mem = ctx.enter_context(nc.sbuf_tensor("late_mem", [P, LATE], F32))
        era[0] = late_mem
        o = [0]
        poolw = take(4, 2, 256)
        acc = take(TT, D)
        poolP = at(o[0] - 2048, 4, TT, SEQ, of=late_mem)
        z_tok = acc
        xT = take(KT, SEQ)
        zT = xT
        u_tok = take(TT, D)
        bd = take(6, D)
        h_sb = take(512)
        sg = take(512)
        Ysb = take(D)
        sel = take(TT, P)
        selT = take(TT, P)
        rt_sb = take(KT, NE)
        rb = take(12, TT, NE)
        rankx = take(TT, 2 * NE + 1)
        combx = take(TT, 2 * NE + 2)
        assert o[0] <= LATE, o[0]
        with nc.sbuf_tensor("before_glu", [P, TOTAL - LATE - KT * D], F32), nc.sbuf_tensor("glu_sb", [P, KT, D], F32) as glu_sb:
            pass
        F32R = mybir.dt.float32r

        def parts(name, *dims):
            return ctx.enter_context(nc.sbuf_tensor(name, [P, *dims], F32R))

        x_hi, x_lo = parts("x_hi", KT, SEQ), parts("x_lo", KT, SEQ)
        h_hi, h_lo = parts("h_hi", 4, P), parts("h_lo", 4, P)
        ring = ctx.enter_context(nc.sbuf_tensor("weight_ring", [P, NSLOT, SLOT], F32))
        w_hi, w_lo = parts("w_hi", NPIECE, PIECE), parts("w_lo", NPIECE, PIECE)

        bank = [ctx.enter_context(nc.psum_tensor(f"bank{i}", [P, 512], F32)) for i in range(8)]

        def psum(i, *dims):
            v = bank[i][:, :]
            names = "abcd"[:len(dims)]
            return v.rearrange(f"p ({' '.join(names)}) -> p {' '.join(names)}", **{k: d for k, d in zip(names, dims)})

        ada_full = [S(f"ada_full{i}") for i in range(NADA)]
        full = [S(f"slot_full{i}") for i in range(NSLOT)]
        block = ctx.enter_context(nc.Block())

        ADA_UNITS = 2 * 3 * KT
        FFN_UNITS = 3 * NF0
        FFN_PIECES = 2 * FFN_UNITS
        FFN_LOADS = [len(range(s, FFN_UNITS, 6)) for s in range(6)] + [0]
        ORDER = []
        for c in range(NF1):
            ORDER += [("gate", c, 0), ("gate", c, 1), ("up", c, 0), ("up", c, 1)]
            if c:
                ORDER += [("down", c - 1, 0), ("down", c - 1, 1)]
        ORDER += [("down", NF1 - 1, 0), ("down", NF1 - 1, 1)]
        EXPERT_UNITS, EXPERT_PIECES = len(ORDER), 2 * len(ORDER)
        AHEAD = NPIECE // 2
        assert EXPERT_UNITS % NSLOT == 0 and EXPERT_PIECES % NPIECE == 0 and FFN_PIECES % NPIECE == 0

        def ffn_pieces(kind, c):
            if kind == "down":
                return FFN_PIECES if isinstance(c, int) and c == NF0 - 1 else 6 * c + 10
            if isinstance(c, int) and c == 0:
                return {"gate": 2, "up": 4}[kind]
            return 6 * c + {"gate": 0, "up": 2}[kind]

        def expert_pieces(i, kind, c):
            return i * EXPERT_PIECES + (FFN_PIECES + 2 * (ORDER.index((kind, c, 1)) + 1))

        @block.sync
        def _(sp):
            sp.dma_start(at(0, 4, P), consts).then_inc(S("consts_in"), 16)
            sp.dma_start(cs[:, 0], cond_in).then_inc(S("cond_in"), 16)
            for j, src in enumerate((lam_re, lam_im, log_step)):
                sp.dma_start(tmp[:, j], src).then_inc(S("lam_in"), 16)
            for j, src in enumerate((b_re, b_im)):
                sp.dma_start(b_raw[:, j], src).then_inc(S("b_in"), 16)
            for j, src in enumerate((c_re, c_im)):
                sp.dma_start(C_sb[:, j], src).then_inc(S("c_in"), 16)
            sp.dma_start(D_sb, d_skip).then_inc(S("d_in"), 16)
            sp.dma_start(hlat, x_in.rearrange("(t p) n -> p t n", p=P)).then_inc(S("x_in"), 16)
            sp.dma_start(ut[:, 1], ctx_in.rearrange("(t p) n -> p t n", p=P)).then_inc(S("x_in"), 16)
            for n in range(ADA_UNITS):
                l, r, k = n // (3 * KT), n // KT % 3, n % KT
                if n >= NADA:
                    sp.wait_ge(S("ada_used"), n - NADA + 1)
                sp.dma_start(ring_a[:, n % NADA], ada_w[l, k * P:(k + 1) * P, r * 2048:(r + 1) * 2048]).then_inc(ada_full[n % NADA], 16)
            glu_v = glu_w.rearrange("(k p) n -> p k n", p=P)
            sp.wait_ge(S("ada_used"), ADA_UNITS)
            sp.dma_start(glu_sb[:, 2:KT], glu_v[:, 2:KT]).then_inc(S("glu_in"), 16)
            sp.wait_ge(S("mod_out"), 6 * 64)
            sp.wait_ge(S("y_done"), 2)
            sp.dma_start(glu_sb[:, 0:2], glu_v[:, 0:2]).then_inc(S("glu_in"), 16)
            sp.wait_ge(S("z_out"), 128)
            sp.wait_ge(S("z_in"), 32)
            sp.wait_ge(S("rows_a"), 96)
            sp.dma_start(poolw, pool_w.rearrange("g (k p) n -> p g k n", p=P)).then_inc(S("pool_in"), 16)
            sp.dma_start(rt_sb, router.rearrange("(k p) n -> p k n", p=P)).then_inc(S("pool_in"), 16)
            gate_v = w_gate.rearrange("(k p) n -> p k n", p=P)
            up_v = w_up.rearrange("(k p) n -> p k n", p=P)

            def ffn_load(kind, c, m, before):
                s = m % 6
                if before is not None:
                    sp.wait_ge(S("low"), before)
                if kind == "down":
                    dst = ring[:, s].rearrange("p (f n) -> p f n", f=2)
                    src = w_down[bass.ds(c * FC0, FC0), :].rearrange("(f p) n -> p f n", p=P)
                else:
                    dst = ring[:, s].rearrange("p (k n) -> p k n", k=KT)
                    src = (gate_v if kind == "gate" else up_v)[:, :, bass.ds(c * FC0, FC0)]
                sp.dma_start(dst, src).then_inc(full[s], 16)

            ffn_load("gate", 0, 0, None)
            ffn_load("up", 0, 1, None)
            for m, (kind, c) in enumerate((("gate", 1), ("up", 1), ("down", 0), ("gate", 2), ("up", 2), ("down", 1)), 2):
                ffn_load(kind, c, m, 2 * (m - 5) if m >= 6 else None)
            sp.wait_ge(S("h1"), 2)
            sp.dma_start(poolP, pool_mat).then_inc(S("pool_in"), 16)
            with sp.Fori(1, NF0 // 2) as i:
                for n, (kind, dc) in enumerate((("gate", 1), ("up", 1), ("down", 0), ("gate", 2), ("up", 2), ("down", 1))):
                    ffn_load(kind, 2 * i + dc, (2 + n) % 6, 12 * i - 8 + 2 * n + 2)
            ffn_load("down", NF0 - 1, FFN_UNITS - 1, 2 * (FFN_UNITS - 6))

            gates = {"gate": e_gate, "up": e_up}

            def expert_loads(i, e):
                for r, (kind, c, half) in enumerate(ORDER):
                    s = r % NSLOT
                    if isinstance(i, int) and r < NSLOT:
                        if s < 6:
                            last = max(range(s, FFN_UNITS, 6))
                            sp.wait_ge(S("low"), 2 * (last + 1))
                    else:
                        sp.wait_ge(S("low"), i * EXPERT_PIECES + (FFN_PIECES + 2 * (r - NSLOT + 1)))
                    cols = slice(c * FC1, (c + 1) * FC1)
                    if kind == "down":
                        rows_ = slice(c * FC1 + half * 256, c * FC1 + half * 256 + 256)
                        src = e_down[bass.ds(e, 1), rows_, :].rearrange("o (f p) n -> p (o f) n", p=P)
                        dst = ring[:, s].rearrange("p (f n) -> p f n", f=2)
                    else:
                        src = gates[kind][bass.ds(e, 1), half * 512:(half + 1) * 512, cols].rearrange("o (k p) n -> p (o k) n", p=P)
                        dst = ring[:, s].rearrange("p (k n) -> p k n", k=4)
                    sp.dma_start(dst, src).then_inc(full[s], 16)

            expert_loads(0, 0)
            with sp.Fori(1, NE) as i:
                expert_loads(i, i)
            sp.wait_ge(S("overflow_known"), 1)
            more = sp.value_load(flag_i[0:1, 0:1], min_val=0, max_val=1)
            with sp.If(more):
                with sp.Fori(NE, 2 * NE) as i:
                    expert_loads(i, i - NE)

        @block.gpsimd
        def _(pool):
            def g_table(b):
                g0, q = b * BG, b % 4
                G = slice(g0, g0 + BG)
                Cr, Ci = (C_sb[:, j, G].unsqueeze(2).to_broadcast([P, BG, CH, GW]) for j in range(2))
                W = [pw[:, j, G].unsqueeze(3).to_broadcast([P, BG, CH, GW]) for j in range(4)]
                if b >= 4:
                    pool.wait_ge(S("y_done"), 1)
                gr, gi = (t[:, q * BG:(q + 1) * BG] for t in (G_re, G_nim))
                k = 6 * b
                nc.gpsimd.tensor_tensor(gr, Cr, W[0], MUL).then_inc(S("g_chain"), 1)
                nc.gpsimd.tensor_tensor(tmpG, Ci, W[2], MUL).then_inc(S("g_chain"), 1)
                pool.wait_ge(S("g_chain"), k + 2)
                nc.gpsimd.tensor_tensor(gr, gr, tmpG, ADD).then_inc(S("g_chain"), 1)
                nc.gpsimd.tensor_tensor(gi, Cr, W[2], MUL).then_inc(S("g_chain"), 1)
                pool.wait_ge(S("g_chain"), k + 4)
                nc.gpsimd.tensor_tensor(tmpG, Ci, W[3], MUL).then_inc(S("g_chain"), 1)
                pool.wait_ge(S("g_chain"), k + 5)
                nc.gpsimd.tensor_tensor(gi, gi, tmpG, ADD).then_inc(S("g_chain"), 1)
                pool.wait_ge(S("g_chain"), k + 6)

            pool.wait_ge(S("pw_ready"), 1)
            pool.wait_ge(S("c_in"), 32)
            for b in range(4):
                g_table(b)
            for b in (4, 5):
                Br, Bi = (Bp_sb[:, j, b * BG:(b + 1) * BG].unsqueeze(2).to_broadcast([P, BG, CH, GW]) for j in range(2))
                W = [pw[:, j, b * BG:(b + 1) * BG].unsqueeze(3).to_broadcast([P, BG, CH, GW]) for j in range(4)]
                pool.wait_ge(S("pt_done"), 4 * b)
                k = 5 * (b - 4)
                nc.gpsimd.tensor_tensor(P_re, Br, W[0], MUL).then_inc(S("p_chain"), 1)
                nc.gpsimd.tensor_tensor(tmpG, Bi, W[2], MUL).then_inc(S("p_chain"), 1)
                pool.wait_ge(S("p_chain"), k + 2)
                nc.gpsimd.tensor_tensor(P_re, P_re, tmpG, ADD).then_inc(S("p_chain"), 1)
                nc.gpsimd.tensor_tensor(P_im, Br, W[1], MUL).then_inc(S("p_chain"), 1)
                pool.wait_ge(S("p_chain"), k + 4)
                nc.gpsimd.tensor_tensor(tmpG, Bi, W[0], MUL).then_inc(S("p_chain"), 1)
                pool.wait_ge(S("p_chain"), k + 5)
                nc.gpsimd.tensor_tensor(P_im, P_im, tmpG, ADD).then_inc(S("P_ready"), 1)
                pool.wait_ge(S("P_ready"), b + 1)
            for b in (4, 5):
                g_table(b)
            for b in range(4, 8):
                pool.wait_ge(S("T_copied"), 3 * (b - 3))
                mid = T_sb[:, b % 4, :, P - GW:P]
                nc.gpsimd.tensor_tensor(mid, mid, T_mid[:, b % 4], ADD).then_inc(S("p_chain"), 1)
                pool.wait_ge(S("p_chain"), 10 + b - 3)
                nc.gpsimd.tensor_tensor(mid, mid, DD[:, 2 * b:2 * b + 2], ADD).then_inc(S("T_ready"), 3)

        @block.scalar
        def _(act):
            def copy(dst, src, name, n=1):
                nc.scalar.activation(dst, src, ACT.Copy).then_inc(S(name), n)

            act.wait_ge(S("cond_in"), 16)
            nc.scalar.activation(cs[:, 1], cs[:, 0], ACT.Silu).then_inc(S("cond_silu"), 1)
            act.wait_ge(S("lam_in"), 48)
            nc.scalar.activation(tmp[:, 3], tmp[:, 2], ACT.Exp).then_inc(S("step_exp"), 1)

            def squares(src, junk, where, name, after=None):
                for t in range(TT):
                    if after:
                        act.wait_ge(S(after), t + 1)
                    nc.scalar.activation(junk[:, t], src[:, t], ACT.Square, accum_out=where[:, t:t + 1]).then_inc(S(name), 1)

            act.wait_ge(S("x_in"), 32)
            squares(hlat, bc[:, 0:2], small[:, 0:2], "sq0")
            squares(ut[:, 1], bc[:, 2:4], small[:, 2:4], "sq0")

            def mod_bias(n):
                l, r = n // 3, n % 3
                for q in range(4):
                    act.dma_start(adab[32 * q:32 * q + 2, n % 2],
                                  ada_b[l:l + 1, r * 2048 + q * 512:r * 2048 + (q + 1) * 512].to_broadcast([2, 512])).then_inc(S(f"adab_in{n % 2}"), 16)

            def mod_out(n):
                l, r = n // 3, n % 3
                act.wait_ge(S("mod_sb_full"), 4 * (n + 1))
                for q in range(4):
                    act.dma_start(mod_d[l, :, r * 2048 + q * 512:r * 2048 + (q + 1) * 512],
                                  mod_sb[32 * q:32 * q + 2, :]).then_inc(S("mod_out"), 16)
                if n + 2 < 6:
                    mod_bias(n + 2)

            def rows(dst, src, name):
                act.dma_start(dst, src.to_broadcast([P, D])).then_inc(S(name), 16)

            mod_bias(0)
            mod_bias(1)
            act.wait_ge(S("ms0"), 1)
            nc.scalar.activation(small[:, 4:8], small[:, 4:8], ACT.Sqrt).then_inc(S("rt0"), 1)
            mod_out(0)
            act.wait_ge(S("mod_out"), 64)
            act.wait_ge(S("sq0"), 4)
            rows(bc[:, 0], mod_d[0, 0:1, 0:D], "bc_in")
            rows(bc[:, 1], mod_d[0, 0:1, D:2 * D], "bc_in")
            rows(bc[:, 2], mod_d[0, 1:2, 0:D], "bc_in")
            rows(bc[:, 3], mod_d[0, 1:2, D:2 * D], "bc_in")
            rows(at(DU_off, D, of=s5_mem), norm_mix[0:1, :], "bc_in")

            def p_evac(b):
                if b >= 2:
                    act.wait_ge(S("e_done"), b - 1)
                for j in range(4):
                    n = 4 * b + j
                    act.wait_ge(S("pt_done"), n + 1)
                    nc.scalar.activation(E_sb[:, b % 2, 2 * j:2 * j + 2], psum(2 + n % 2, 2, 2, P), ACT.Copy).then_inc(S("pt_out"), 1)

            def u_evac():
                for k in range(KT):
                    act.wait_ge(S("ut_done"), k + 1)
                    if k >= 4:
                        act.wait_ge(S(f"u_out{k % 4}"), 16 * (k // 4))
                    if k == 0:
                        act.wait_ge(S("u_ready"), 4)
                    nc.scalar.activation(stage[:, k % 4].rearrange("p (b s a) -> p s b a", b=CH, s=2),
                                         psum(2 + k % 2, 2, CH, NCH), ACT.Copy).then_inc(S("ut_out"), 1)
                    act.wait_ge(S("ut_out"), k + 1)
                    act.dma_start(u_d[k * 8:(k + 1) * 8].rearrange("g h b a -> (g h) (b a)"), stage[:, k % 4]).then_inc(S(f"u_out{k % 4}"), 16)
                for h in range(2):
                    for k in range(4):
                        act.wait_ge(S(f"u_out{k}"), 16 * (h + 1))
                    for c in range(CH):
                        act.dma_start(U_sb[c * GW:(c + 1) * GW, h * HG:(h + 1) * HG],
                                      u_d[h * HG:(h + 1) * HG, :, CH - 1 - c, :].rearrange("g h a -> h g a")).then_inc(S(f"U_in{h}"), 16)

            def e_evac(b):
                q = b % 4
                if b == 4:
                    act.wait_ge(S("srhs_done"), 2)
                for j in range(2):
                    n = 2 * b + j
                    act.wait_ge(S("e_bank"), n + 1)
                    src = psum(6 + j, 4, 2, 2 * NCH)
                    dst = e_sb.rearrange("p i r g -> p g r i")[:, q * BG + 4 * j:q * BG + 4 * j + 4]
                    nc.scalar.activation(dst[0:64], src[0:64], ACT.Copy).then_inc(S("e_out"), 1)
                    for s in range(2):
                        back = src[64:P, :, :, s * NCH:(s + 1) * NCH][:, :, :, ::-1]
                        nc.scalar.activation(dst[64:P, :, :, s * NCH:(s + 1) * NCH], back, ACT.Copy).then_inc(S("e_out"), 1)

            def kernels_to_dram(h):
                act.wait_ge(S("T_ready"), 12 * (h + 1))
                for q in range(4):
                    act.dma_start(t_d[h * HG + q:(h + 1) * HG:4].rearrange("m h n -> h m n"),
                                  T_sb[32 * q:32 * q + GW].rearrange("p b j n -> p (b j) n")).then_inc(S("t_out"), 16)

            def toeplitz_in(b):
                if b % 4 == 0:
                    act.wait_ge(S("t_out"), 16 * (b + 4))
                if b >= 2:
                    act.wait_ge(S("m_done"), b)
                for c in range(CH):
                    act.dma_start(M_sb[c * GW:(c + 1) * GW].rearrange("p b g n -> p (b g) n"),
                                  t_d[b * BG:(b + 2) * BG, :, c * GW:c * GW + P].rearrange("g h n -> h g n")).then_inc(S("M_in"), 16)

            def kernels_evac(b):
                act.wait_ge(S("tk_done"), b + 1)
                T_b = T_sb[:, b % 4]
                for dst, src in ((T_b[:, :, 0:P], psum(5, 4, P)[:, 0:2]), (T_b[:, :, P:240], psum(4, 4, P)[:, 0:2, GW:P]),
                                 (T_mid[:, b % 4], psum(4, 4, P)[:, 0:2, 0:GW])):
                    nc.scalar.activation(dst, src, ACT.Copy).then_inc(S("T_copied"), 1)

            def s_copy():
                src = e_sb[:, NCH - 1:2 * NCH - 1].rearrange("p i r g -> p r g i")
                nc.scalar.activation(S_rhs[0:64], src[0:64], ACT.Copy).then_inc(S("srhs_done"), 1)
                nc.scalar.activation(S_rhs[64:P], src[64:P][:, :, :, ::-1], ACT.Copy).then_inc(S("srhs_done"), 1)

            def y_gelu(h):
                act.wait_ge(S("y_ready"), 2 * (h + 1))
                nc.scalar.activation(y_sb, y_sb, ACT.Gelu_apprx_tanh).then_inc(S("z_ready"), 1)
                act.wait_ge(S("z_ready"), h + 1)
                for q in range(4):
                    c0 = (h * HG + q * BG) * GW
                    act.dma_start(z_d.rearrange("(b a) c -> a b c", b=CH)[:, :, c0:c0 + BG * GW],
                                  y_sb[32 * q:32 * q + 32]).then_inc(S("z_out"), 16)

            p_evac(0)
            p_evac(1)
            u_evac()
            e_evac(0)
            p_evac(2)
            e_evac(1)
            p_evac(3)
            e_evac(2)
            e_evac(3)
            kernels_to_dram(0)
            mod_out(1)
            toeplitz_in(0)
            toeplitz_in(2)
            p_evac(4)
            p_evac(5)
            act.wait_ge(S("scan_done"), 1)
            s_copy()
            y_gelu(0)
            mod_out(2)
            e_evac(4)
            p_evac(6)
            e_evac(5)
            p_evac(7)
            mod_out(3)
            e_evac(6)
            e_evac(7)
            act.wait_ge(S("t_out"), 64)
            for b in range(4, 8):
                kernels_evac(b)
            kernels_to_dram(1)
            toeplitz_in(4)
            toeplitz_in(6)
            act.wait_ge(S("scan_done"), 2)
            s_copy()
            mod_out(4)
            mod_out(5)
            y_gelu(1)

            def high(n, b, slot, half, slot_loads=None):
                if slot_loads is not None:
                    act.wait_ge(full[slot], slot_loads)
                if not (isinstance(n, int) and n < NPIECE):
                    act.wait_ge(S("piece_used"), n - (NPIECE - 1))
                nc.scalar.activation(w_hi[:, b], ring[:, slot, half * PIECE:(half + 1) * PIECE], ACT.Copy).then_inc(S("high"), 1)

            def ffn_high(m, slot, loads):
                for half in range(2):
                    high(2 * m + half, (2 * slot + half) % NPIECE, slot, half, 16 * loads if half == 0 else None)

            act.wait_ge(S("mod_out"), 6 * 64)
            act.wait_ge(S("z_out"), 128)
            for t in range(TT):
                act.dma_start(z_tok[:, t], z_d[t * P:(t + 1) * P, :]).then_inc(S("z_in"), 16)
            rows(bd[:, 0], glu_b, "rows_a")
            rows(bd[:, 1], mod_d[0, 0:1, 2 * D:3 * D], "rows_a")
            rows(bd[:, 2], mod_d[0, 0:1, 4 * D:5 * D], "rows_a")
            rows(bd[:, 3], norm_ffn[0:1, :], "rows_a")
            rows(bd[:, 4], mod_d[0, 0:1, 3 * D:4 * D], "rows_a")
            rows(bd[:, 5], mod_d[0, 0:1, 5 * D:6 * D], "rows_a")
            for j in range(4):
                act.wait_ge(S("zt_done"), j + 1)
                nc.scalar.activation(zT[:, 2 * j:2 * j + 2], psum(j % 2, 2, SEQ), ACT.Copy).then_inc(S("zt_out"), 1)
            for j in range(4):
                act.wait_ge(S("gate_in"), j + 1)
                v = u_tok.rearrange("p t (c n) -> p (t c) n", c=2)[:, j]
                nc.scalar.activation(v, v, ACT.Sigmoid).then_inc(S("sigm"), 1)
            act.wait_ge(S("glu_pe"), 4)
            ffn_high(0, 0, 1)
            ffn_high(1, 1, 1)
            squares(hlat, u_tok, small[:, 8:10], "sq1", "h1")
            act.wait_ge(S("ms1"), 1)
            nc.scalar.activation(small[:, 8:10], small[:, 8:10], ACT.Sqrt).then_inc(S("rt1"), 1)

            def xT_evac(base, bks):
                for j in range(4):
                    act.wait_ge(S("xt_done"), base + j + 1)
                    nc.scalar.activation(xT[:, 2 * j:2 * j + 2], psum(bks[j % 2], 2, SEQ), ACT.Copy).then_inc(S("xt_out"), 1)

            for j in range(4):
                act.wait_ge(S("xt_done"), j + 1)
                nc.scalar.activation(x_hi[:, 2 * j:2 * j + 2], psum(j % 2, 2, SEQ), ACT.Copy).then_inc(S("x_hi"), 1)

            def ffn_silu(c):
                act.wait_ge(S("piece_used"), ffn_pieces("gate", c))
                if not (isinstance(c, int) and c == 0):
                    act.wait_ge(S("f_h"), c)
                nc.scalar.activation(sg, bank[4][:, :], ACT.Silu).then_inc(S("f_silu"), 1)

            def ffn_hT(c):
                act.wait_ge(S("f_h"), c + 1)
                if not (isinstance(c, int) and c == 0):
                    act.wait_ge(S("piece_used"), ffn_pieces("down", c - 1))
                nc.scalar.activation(h_hi[:], h_sb.rearrange("p (a b) -> p a b", a=4), ACT.Copy).then_inc(S("f_hT"), 1)

            def ffn_chunk(c, s, loads):
                m = 3 * c - 1
                ffn_high(m, s, loads[0])
                ffn_high(m + 1, (s + 1) % 6, loads[1])
                ffn_silu(c)
                ffn_hT(c - 1)
                ffn_high(m + 2, (s + 2) % 6, loads[2])

            act.wait_ge(S("u1_ready"), 2)
            rows(bd[:, 0], mod_d[1, 0:1, 0:D], "rows_b")
            rows(bd[:, 1], mod_d[1, 0:1, D:2 * D], "rows_b")
            rows(bd[:, 2], mod_d[1, 0:1, 2 * D:3 * D], "rows_b")
            rows(bd[:, 3], norm_mix[1:2, :], "rows_b")
            rows(bd[:, 4], pool_b, "rows_b")
            rows(Ysb, pool_scale, "rows_b")
            ffn_silu(0)
            ffn_chunk(1, 2, (1, 1, 1))
            ffn_chunk(2, 5, (1, 2, 2))
            with act.Fori(1, NF0 // 2) as i:
                ffn_chunk(2 * i + 1, 2, (i + 1, i + 1, i + 1))
                ffn_chunk(2 * i + 2, 5, (i + 1, i + 2, i + 2))
            ffn_high(FFN_UNITS - 1, (FFN_UNITS - 1) % 6, (FFN_UNITS - 1) // 6 + 1)
            ffn_hT(NF0 - 1)

            squares(hlat, u_tok, small[:, 12:14], "sq2", "h2")
            act.wait_ge(S("ms2"), 1)
            nc.scalar.activation(small[:, 12:14], small[:, 12:14], ACT.Sqrt).then_inc(S("rt2"), 1)
            act.wait_ge(S("u2_ready"), 1)
            rows(bd[:, 0], mod_d[1, 0:1, 3 * D:4 * D], "rows_c")
            rows(bd[:, 1], mod_d[1, 0:1, 4 * D:5 * D], "rows_c")
            rows(bd[:, 5], mod_d[1, 0:1, 5 * D:6 * D], "rows_c")
            rows(bd[:, 3], norm_ffn[1:2, :], "rows_c")
            xT_evac(4, (0, 1))
            for r in range(AHEAD):
                for half in range(2):
                    high(FFN_PIECES + 2 * r + half, 2 * r + half, r, half, 16 * (FFN_LOADS[r] + 1) if half == 0 else None)
            squares(hlat, u_tok, small[:, 16:18], "sq3", "h3")
            act.wait_ge(S("ms3"), 1)
            nc.scalar.activation(small[:, 16:18], small[:, 16:18], ACT.Sqrt).then_inc(S("rt3"), 1)
            xT_evac(8, (0, 1))
            act.wait_ge(S("top2"), 1)
            nc.scalar.activation(small[:, 24:26], small[:, 22:24], ACT.Exp).then_inc(S("top_exp"), 1)
            act.wait_ge(S("u3_ready"), 1)
            rows(bd[:, 3], norm_final, "rows_d")

            def gather_out(half, n):
                act.wait_ge(S(f"gather{half}"), n)
                nc.scalar.activation(x_hi[:, 4 * half:4 * half + 4, 0:P], psum(7, 4, P), ACT.Copy).then_inc(S(f"gather_hi{half}"), 1)

            def expert(i, k):
                def highs(units):
                    for r in units:
                        if isinstance(i, int) and i == 0 and r < AHEAD:
                            continue
                        for half in range(2):
                            s = r % NSLOT
                            loads = None
                            if half == 0:
                                loads = i * (16 * EXPERT_UNITS // NSLOT) + 16 * (FFN_LOADS[s] + r // NSLOT + 1)
                            high(i * EXPERT_PIECES + (FFN_PIECES + 2 * r + half), (2 * r + half) % NPIECE, s, half, loads)

                def silu(c):
                    act.wait_ge(S("piece_used"), expert_pieces(i, "gate", c))
                    if not (isinstance(i, int) and i == 0 and c == 0):
                        act.wait_ge(S("x_h"), i * NF1 + c)
                    nc.scalar.activation(sg, bank[c % 2][:, :], ACT.Silu).then_inc(S("x_silu"), 1)

                def hTs(c):
                    act.wait_ge(S("x_tr"), i * NF1 + c + 1)
                    act.wait_ge(S("piece_used"), expert_pieces(i, "down", c - 1) if c else i * EXPERT_PIECES + FFN_PIECES)
                    nc.scalar.activation(h_hi[:], psum(6, 4, P), ACT.Copy).then_inc(S("x_hT"), 1)

                r = 0
                for c in range(NF1):
                    highs((r, r + 1))
                    if c == 0:
                        y_out(i, k)
                    highs((r + 2,))
                    silu(c)
                    if c:
                        hTs(c - 1)
                    highs((r + 3,))
                    if c == 2:
                        act.wait_ge(S("seltr"), i + 1)
                        nc.scalar.activation(selT, bank[7][:, 0:2 * P].rearrange("p (t n) -> p t n", t=2), ACT.Copy).then_inc(S("selT_out"), 1)
                    r += 4
                    if c:
                        highs((r, r + 1))
                        r += 2
                highs((r,))
                hTs(NF1 - 1)
                gather_out(0, i + 2)
                highs((r + 1,))
                gather_out(1, i + 2)

            def y_out(i, k):
                if isinstance(i, int) and i == 0:
                    act.wait_ge(S("moe_init"), 1)
                    act.sem_inc(S("Y_out"), 2)
                    return
                act.wait_ge(S("piece_used"), i * EXPERT_PIECES + FFN_PIECES)
                act.wait_ge(S("scat_pe"), i * 4 + 4 * k)
                for j in range(2):
                    nc.scalar.activation(Ysb[:, j * 512:(j + 1) * 512], bank[4 + j][:, :], ACT.Copy).then_inc(S("Y_out"), 1)

            gather_out(0, 1)
            gather_out(1, 1)
            expert(0, 0)
            with act.Fori(1, NE) as i:
                expert(i, 0)
            y_out(NE, 0)
            act.wait_ge(S("overflow_known"), 1)
            more = act.value_load(flag_i[0:1, 0:1], min_val=0, max_val=1)
            with act.If(more):
                with act.Fori(NE, 2 * NE) as i:
                    expert(i, 1)
                y_out(2 * NE, 1)
            squares(hlat, u_tok, small[:, 32:34], "sq4", "h4")
            act.wait_ge(S("ms4"), 1)
            nc.scalar.activation(small[:, 32:34], small[:, 32:34], ACT.Sqrt).then_inc(S("rt4"), 1)
            for t in range(TT):
                act.wait_ge(S("result"), t + 1)
                act.dma_start(out[t * P:(t + 1) * P, :], u_tok[:, t]).then_inc(S("out_done"), 16)
            act.wait_ge(S("out_done"), 32)

        @block.tensor
        def _(pe):
            mm, tr = nc.tensor.matmul, nc.tensor.transpose

            def ada(first, last):
                for u in range(first, last):
                    n, k = u // KT, u % KT
                    if u == 0:
                        pe.wait_ge(S("cond_silu"), 1)
                    if n >= 2 and k == 0:
                        pe.wait_ge(S("mod_sb_full"), 4 * (n - 1))
                    pe.wait_ge(ada_full[u % NADA], 16 * (u // NADA + 1))
                    for q in range(4):
                        ins = mm(bank[n % 2][32 * q:32 * q + 2, :], cs[:, 1, k], ring_a[:, u % NADA, q * 512:(q + 1) * 512],
                                 start=k == 0, stop=k == KT - 1, tile_position=(0, 32 * q), skip_group_check=True)
                    ins.then_inc(S("ada_used"), 1)

            def p_transpose(b):
                pe.wait_ge(S("P_ready"), b + 1)
                for j in range(4):
                    n = 4 * b + j
                    if n >= 2 and b == 0 or b > 0:
                        pe.wait_ge(S("pt_out"), n - 1)
                    if b == 2 and j == 0:
                        pe.wait_ge(S("ut_out"), KT)
                    for i in range(4):
                        g, t = 2 * j + i // 2, (P_re, P_im)[i % 2]
                        ins = tr(psum(2 + n % 2, 4, P)[:, i], t[:, g].rearrange("p k h -> p (k h)"), ident)
                    ins.then_inc(S("pt_done"), 1)

            def u_transpose():
                pe.wait_ge(S("u_ready"), 4)
                pe.wait_ge(S("pt_out"), 8)
                for k in range(KT):
                    if k >= 2:
                        pe.wait_ge(S("ut_out"), k - 1)
                    for i in range(4):
                        ins = tr(psum(2 + k % 2, 4, P)[:, i], ut[:, 1 - i // 2, i % 2, k * P:(k + 1) * P], ident)
                    ins.then_inc(S("ut_done"), 1)

            def e_matmul(b):
                pe.wait_ge(S(f"U_in{b // 4}"), 16 * CH)
                pe.wait_ge(S("pt_out"), 4 * (b + 1))
                for j in range(2):
                    if b >= 1:
                        pe.wait_ge(S("e_out"), 3 * (2 * (b - 1) + j + 1))
                    if b == 4:
                        pe.wait_ge(S("y_ready"), 2)
                    for i in range(8):
                        g, r = 4 * j + i // 2, i % 2
                        ins = mm(psum(6 + j, 8, 2 * NCH)[:, i], E_sb[:, b % 2, g, r], U_sb[:, b * BG + g], start=True, stop=True)
                    ins.then_inc(S("e_bank"), 1)
                    if j:
                        pe.wait_ge(S("e_bank"), 2 * (b + 1))
                        pe.sem_inc(S("e_done"), 1)

            def kernels(b):
                if b < 6:
                    pe.wait_ge(S("g_chain"), 6 * (b + 1))
                else:
                    pe.wait_ge(S("g_dve"), b - 5)
                if 1 <= b <= 4:
                    pe.wait_ge(S("T_ready"), 3 * b)
                if b >= 5:
                    pe.wait_ge(S("T_copied"), 3 * (b - 4))
                if b == 4:
                    pe.wait_ge(S("yi_out"), 2)
                for n in range(4 * BG):
                    j, r, d, q = n // 16, n // 8 % 2, n // 4 % 2, n % 4
                    rows = slice(64 * d, 64 * d + 64)
                    g, t = 4 * j + q, (G_re, G_nim)[r]
                    lhs = Bb_sb[rows, r, b * BG + g:b * BG + g + 2].rearrange("p g h -> p (g h)")
                    ins = mm(psum(4 + d, 4, P)[32 * q:32 * q + 32, j], lhs, t[rows, b % 4 * BG + g].rearrange("p k h -> p (k h)"),
                             start=r == 0, stop=r == 1, tile_position=(64 * d, 32 * q), skip_group_check=True)
                ins.then_inc(S("tk_done"), 1)

            def inside(b):
                pe.wait_ge(S("M_in"), 16 * CH * (b // 2 + 1))
                pe.wait_ge(S("T_ready"), 3 * (b // 4 * 4 + 4))
                for g in range(BG):
                    q = b % 4
                    ins = mm(psum(4 + g // 4, 4, P)[32 * q:32 * q + 32, g % 4], U_sb[:, b * BG + g, NCH:2 * NCH], M_sb[:, b % 2, g],
                             start=True, stop=True, tile_position=(0, 32 * q), skip_group_check=True)
                ins.then_inc(S("m_done"), 1)

            def from_states(h):
                pe.wait_ge(S("srhs_done"), 2 * (h + 1))
                if h:
                    pe.wait_ge(S("y_ready"), 2)
                for g in range(BG):
                    for r, t in enumerate((G_re, G_nim)):
                        for q in range(4):
                            n = q * BG + g
                            ins = mm(psum(6 + g // 4, 4, P)[32 * q:32 * q + 32, g % 4], S_rhs[:, r, n], t[:, n].rearrange("p k h -> p (k h)"),
                                     start=r == 0, stop=r == 1, tile_position=(0, 32 * q), skip_group_check=True)
                ins.then_inc(S("y_done"), 1)

            pe.wait_ge(S("consts_in"), 16)
            ada(0, 8)
            p_transpose(0)
            p_transpose(1)
            u_transpose()
            for b in range(4):
                kernels(b)
            ada(8, 10)
            e_matmul(0)
            p_transpose(2)
            ada(10, 13)
            e_matmul(1)
            p_transpose(3)
            ada(13, 16)
            e_matmul(2)
            e_matmul(3)
            ada(16, 24)
            inside(0)
            inside(1)
            p_transpose(4)
            ada(24, 28)
            inside(2)
            inside(3)
            p_transpose(5)
            ada(28, 31)
            from_states(0)
            e_matmul(4)
            ada(31, 34)
            p_transpose(6)
            e_matmul(5)
            ada(34, 36)
            p_transpose(7)
            e_matmul(6)
            ada(36, 40)
            e_matmul(7)
            for b in range(4, 8):
                kernels(b)
            ada(40, 43)
            inside(4)
            inside(5)
            ada(43, 48)
            inside(6)
            inside(7)
            from_states(1)

            def transpose_rows(src, done, read, base):
                for j in range(4):
                    if j >= 2:
                        pe.wait_ge(S(read), base + j - 1)
                    for i in range(4):
                        ins = tr(psum(j % 2, 4, P)[:, i], src[:, i % 2, (2 * j + i // 2) * P:(2 * j + i // 2 + 1) * P], ident)
                    ins.then_inc(S(done), 1)

            pe.wait_ge(S("z_in"), 32)
            pe.wait_ge(S("mod_sb_full"), 24)
            transpose_rows(z_tok, "zt_done", "zt_out", 0)
            pe.wait_ge(S("zt_out"), 4)
            pe.wait_ge(S("glu_in"), 32)
            pe.wait_ge(S("y_ready"), 4)
            for j in range(4):
                t, c = j // 2, j % 2
                for k in range(KT):
                    ins = mm(bank[4 + j][:, :], zT[:, k, t * P:(t + 1) * P], glu_sb[:, k, c * 512:(c + 1) * 512],
                             start=k == 0, stop=k == KT - 1)
                ins.then_inc(S("glu_pe"), 1)

            pe.wait_ge(S("u1_ready"), 2)
            transpose_rows(u_tok, "xt_done", "x_lo", 0)
            pe.wait_ge(S("x_lo"), 4)

            def product(dst, x, w, start, stop):
                (xh, xl), (wh, wl) = x, w
                mm(dst, xh, wh, start=start, stop=False)
                mm(dst, xh, wl, start=False, stop=False)
                return mm(dst, xl, wh, start=False, stop=stop)

            def piece(b, o, n):
                return w_hi[:, b, o:o + n], w_lo[:, b, o:o + n]

            def ffn_in(bk, n, b):
                for half in range(2):
                    pe.wait_ge(S("low"), n + (half + 1))
                    wh, wl = (v[:, (b + half) % NPIECE].rearrange("p (k n) -> p k n", k=4) for v in (w_hi, w_lo))
                    for f in range(2):
                        F = slice(f * P, (f + 1) * P)
                        for k in range(4):
                            kk = 4 * half + k
                            ins = product(bank[bk][:, f * SEQ:(f + 1) * SEQ], (wh[:, k, F], wl[:, k, F]), (x_hi[:, kk], x_lo[:, kk]),
                                          f == 0 and kk == 0, f == 1 and kk == KT - 1)
                    ins.then_inc(S("piece_used"), 1)

            def ffn_gate(c, m, b):
                if not (isinstance(c, int) and c == 0):
                    pe.wait_ge(S("f_silu"), c)
                ffn_in(4, 2 * m, b)

            def ffn_up(c, m, b):
                if not (isinstance(c, int) and c == 0):
                    pe.wait_ge(S("f_h"), c)
                ffn_in(5, 2 * m, b)

            def ffn_down(c, m, b, first=False, last=False):
                pe.wait_ge(S("f_hl"), c + 1)
                for f in range(2):
                    pe.wait_ge(S("low"), 2 * m + (f + 1))
                    for j in range(4):
                        t, n = j // 2, j % 2
                        ins = product(bank[j][:, :], (h_hi[:, 2 * f + t], h_lo[:, 2 * f + t]), piece((b + f) % NPIECE, n * 512, 512),
                                      first and f == 0, last and f == 1)
                    ins.then_inc(S("piece_used"), 1)

            def ffn_chunk(c, b, first=False):
                ffn_gate(c, 3 * c - 1, b)
                ffn_up(c, 3 * c, (b + 2) % NPIECE)
                ffn_down(c - 1, 3 * c + 1, (b + 4) % NPIECE, first=first)

            ffn_gate(0, 0, 0)
            ffn_up(0, 1, 2)
            ffn_chunk(1, 4, first=True)
            ffn_chunk(2, 4)
            with pe.Fori(1, NF0 // 2) as i:
                ffn_chunk(2 * i + 1, 4)
                ffn_chunk(2 * i + 2, 4)
            ffn_down(NF0 - 1, FFN_UNITS - 1, 2 * (FFN_UNITS - 1) % NPIECE, last=True)

            pe.wait_ge(S("u2_ready"), 1)
            pe.wait_ge(S("pool_in"), 48)
            for j in range(4):
                if j >= 2:
                    pe.wait_ge(S("xt_out"), j - 1)
                for i in range(2):
                    k = 2 * j + i
                    for t in range(TT):
                        ins = mm(psum(j % 2, 2, SEQ)[:, i], u_tok[:, t, k * P:(k + 1) * P], poolP[:, j, t], start=t == 0, stop=t == 1)
                ins.then_inc(S("xt_done"), 1)
            pe.wait_ge(S("xt_out"), 4)
            for t in range(TT):
                for g in range(4):
                    for k in range(2):
                        ins = mm(bank[4 + 2 * t + g // 2][:, (g % 2) * 256:(g % 2) * 256 + 256], xT[:, 2 * g + k, t * P:(t + 1) * P],
                                 poolw[:, g, k], start=k == 0, stop=k == 1)
            ins.then_inc(S("pool_pe"), 1)
            pe.wait_ge(S("u3_ready"), 1)
            transpose_rows(u_tok, "xt_done", "xt_out", 4)
            pe.wait_ge(S("xt_out"), 8)
            for t in range(TT):
                for k in range(KT):
                    ins = mm(psum(2, 64, NE)[:, t], xT[:, k, t * P:(t + 1) * P], rt_sb[:, k], start=k == 0, stop=k == KT - 1)
            ins.then_inc(S("logits"), 1)
            pe.wait_ge(S("mask"), 1)
            M_ = rb[:, 8]
            mm(psum(3, 64, NE)[:, 0], tri, M_[:, 0], start=True, stop=True)
            mm(psum(3, 64, NE)[:, 1], ones, M_[:, 0], start=True, stop=False)
            mm(psum(3, 64, NE)[:, 1], tri, M_[:, 1], start=False, stop=True)
            mm(psum(3, 64, NE)[:, 2], ones, M_[:, 0], start=True, stop=False)
            mm(psum(3, 64, NE)[:, 2], ones, M_[:, 1], start=False, stop=True).then_inc(S("rank_pe"), 1)

            def gather(half, n, zero=False):
                if half == 0:
                    pe.wait_ge(S("sel_ready"), n)
                else:
                    pe.wait_ge(S("gather_lo0"), n)
                for k in range(4):
                    for t in range(TT):
                        kk = 4 * half + k
                        ins = mm(psum(7, 4, P)[:, k], u_tok[:, t, kk * P:(kk + 1) * P], sel[:, t], start=t == 0, stop=t == 1)
                ins.then_inc(S(f"gather{half}"), 1)

            def scatter(r, n, y):
                if y is not None:
                    pe.wait_ge(S("Y_out"), y)
                if not (isinstance(n, int) and n == 0):
                    pe.wait_ge(S("scat_acc"), n)
                t, c = r // 2, r % 2
                mm(bank[7][:, :], selT[:, t], Ysb[:, c * 512:(c + 1) * 512], start=True, stop=True).then_inc(S("scat_pe"), 1)

            def expert(i, k):
                zero = isinstance(i, int) and i == 0

                def unit(kind, c, half):
                    return 2 * ORDER.index((kind, c, half))

                def ready(n):
                    pe.wait_ge(S("low"), i * EXPERT_PIECES + (FFN_PIECES + n + 1))

                def gate_up(kind, c):
                    back = 0 if c == 0 else 1
                    if not (zero and c - back <= 0):
                        pe.wait_ge(S("x_silu" if kind == "gate" else "x_h"), i * NF1 + c - back)
                    bk = (0 if kind == "gate" else 2) + c % 2
                    for kk in range(0, KT, 2):
                        n = unit(kind, c, kk // 4) + kk % 4 // 2
                        ready(n)
                        for k in (kk, kk + 1):
                            ins = product(bank[bk][:, :], (x_hi[:, k, 0:P], x_lo[:, k, 0:P]),
                                          piece(n % NPIECE, (k % 2) * FC1, FC1), k == 0, k == KT - 1)
                        ins.then_inc(S("piece_used"), 1)

                def trans(c):
                    pe.wait_ge(S("x_h"), i * NF1 + c + 1)
                    if not (zero and c == 0):
                        pe.wait_ge(S("x_hl"), i * NF1 + c)
                    for f in range(4):
                        ins = tr(psum(6, 4, P)[:, f], h_sb[:, f * P:(f + 1) * P], ident)
                    ins.then_inc(S("x_tr"), 1)

                def down(c, fs):
                    if fs[0] == 0:
                        pe.wait_ge(S("x_hl"), i * NF1 + c + 1)
                        if c == 0:
                            pe.wait_ge(S("Y_out"), 2 * i + 2 + 2 * k)
                    for f in fs:
                        n = unit("down", c, f // 2) + f % 2
                        ready(n)
                        for h in range(2):
                            ins = product(bank[4 + h][:, :], (h_hi[:, f], h_lo[:, f]), piece(n % NPIECE, h * 512, 512),
                                          c == 0 and f == 0, c == NF1 - 1 and f == 3)
                        ins.then_inc(S("piece_used"), 1)

                pe.wait_ge(S("gather_lo1"), i + 1)
                for c in range(NF1):
                    gate_up("gate", c)
                    if c < 2:
                        scatter(2 * c, i * 4 + 4 * k + 2 * c, 2 * i + 2 + 2 * k)
                    if c == 2:
                        pe.wait_ge(S("scat_acc"), i * 4 + 4 * k + 4)
                        for t in range(TT):
                            ins = tr(bank[7][:, t * P:(t + 1) * P], sel[:, t], ident)
                        ins.then_inc(S("seltr"), 1)
                    if c:
                        trans(c - 1)
                    gate_up("up", c)
                    if c < 2:
                        scatter(2 * c + 1, i * 4 + 4 * k + 2 * c + 1, None)
                    if c:
                        down(c - 1, (0, 1, 2, 3))
                trans(NF1 - 1)
                pe.wait_ge(S("selT_out"), i + 1)
                gather(0, i + 2)
                down(NF1 - 1, (0, 1))
                gather(1, i + 2)
                down(NF1 - 1, (2, 3))

            gather(0, 1)
            gather(1, 1)
            expert(0, 0)
            with pe.Fori(1, NE) as i:
                expert(i, 0)
            pe.wait_ge(S("gather_lo1"), NE + 1)
            for r in range(4):
                scatter(r, 4 * NE + r, 2 * NE + 2)
            pe.wait_ge(S("overflow_known"), 1)
            more = pe.value_load(flag_i[0:1, 0:1], min_val=0, max_val=1)
            with pe.If(more):
                with pe.Fori(NE, 2 * NE) as i:
                    expert(i, 1)
                pe.wait_ge(S("gather_lo1"), 2 * NE + 1)
                for r in range(4):
                    scatter(r, 8 * NE + 4 + r, 4 * NE + 4)

        @block.vector
        def _(dve):
            V = nc.vector
            tt, ts, stt = V.tensor_tensor, V.tensor_scalar, V.scalar_tensor_tensor
            chain = [0]

            def link(ins, more=None):
                chain[0] += 1
                ins.then_inc(S("dve_chain"), 1)
                dve.wait_ge(S("dve_chain"), chain[0])

            dve.wait_ge(S("lam_in"), 48)
            dve.wait_ge(S("step_exp"), 1)
            V.memset(Bb_sb[:, :, GROUPS], 0.0)
            stt(tmp[:, 6], tmp[:, 0], 0.5 ** SQ, tmp[:, 3], MUL, MUL)
            link(stt(tmp[:, 7], tmp[:, 1], 0.5 ** SQ, tmp[:, 3], MUL, MUL))
            V.tensor_copy(tmp[:, 9], tmp[:, 6])
            ts(tmp[:, 8], tmp[:, 7], -1.0, None, MUL)
            V.memset(tmp[:, 10], 1.0)
            link(V.memset(tmp[:, 11], 0.0))
            quad = lambda a: tmp[:, a:a + 4].rearrange("p (c r) g -> p c r g", c=2)
            twice = lambda a: tmp[:, a:a + 2].unsqueeze(2).to_broadcast([P, 2, 2, GROUPS])
            for n in range(ORD, 1, -1):
                stt(quad(12)[:, 0], twice(10)[:, 0], 1.0 / n, quad(6)[:, 0], MUL, MUL)
                link(stt(quad(12)[:, 1], twice(10)[:, 1], 1.0 / n, quad(6)[:, 1], MUL, MUL))
                link(tt(tmp[:, 10:12], tmp[:, 12:14], tmp[:, 14:16], ADD))
                link(ts(tmp[:, 10], tmp[:, 10], 1.0, None, ADD))
            link(tt(quad(12), twice(10), quad(6), MUL))
            link(tt(tmp[:, 16:18], tmp[:, 12:14], tmp[:, 14:16], ADD))
            for n in range(SQ):
                ts(tmp[:, 6:10:3], tmp[:, 16:17].to_broadcast([P, 2, GROUPS]), 2.0, None, ADD)
                V.tensor_copy(tmp[:, 7], tmp[:, 17])
                link(ts(tmp[:, 8], tmp[:, 17], -1.0, None, MUL))
                link(tt(quad(12), twice(16), quad(6), MUL))
                link(tt(tmp[:, 16:18], tmp[:, 12:14], tmp[:, 14:16], ADD))
            V.memset(Npow[:, 0, 0], 1.0)
            V.memset(Npow[:, 0, 1], 0.0)
            ts(Npow[:, 1, 0], tmp[:, 16], 1.0, None, ADD)
            V.tensor_copy(Npow[:, 1, 1], tmp[:, 17])
            ts(tmp[:, 28], tmp[:, 16], 1.0, None, ADD)
            link(V.tensor_copy(tmp[:, 29], tmp[:, 17]))
            for m in (1, 2, 4):
                ts(tmp[:, 18], Npow[:, m, 1], -1.0, None, MUL)
                link(V.tensor_copy(tmp[:, 19], Npow[:, m, 0]))
                lo = Npow[:, 1:1 + m]
                hi = Npow[:, 1 + m:1 + 2 * m]
                part = tmp[:, 20:20 + 2 * m].rearrange("p (m r) g -> p m r g", m=m)
                shape = [P, m, 2, GROUPS]
                tt(hi, lo[:, :, 0:1].to_broadcast(shape), Npow[:, m:m + 1].to_broadcast(shape), MUL)
                link(tt(part, lo[:, :, 1:2].to_broadcast(shape), tmp[:, 18:20].unsqueeze(1).to_broadcast(shape), MUL))
                link(tt(hi, hi, part, ADD))
            V.tensor_copy(LT[:, 0], Npow[:, CH])
            ts(LT[:, 1, 0], Npow[:, CH, 1], -1.0, None, MUL)
            V.tensor_copy(LT[:, 1, 1], Npow[:, CH, 0])
            V.tensor_copy(pw[0:64, 0:2].rearrange("p r g k -> p k r g"), Npow[0:64, 0:CH])
            link(V.tensor_copy(pw[64:P, 0:2].rearrange("p r g k -> p k r g"), Npow[64:P, 0:CH][:, ::-1]))
            ts(pw[:, 2], pw[:, 1], -1.0, None, MUL)
            ts(pw[:, 3], pw[:, 0], -1.0, None, MUL).then_inc(S("pw_ready"), 1)
            er, ei, lr, li = tmp[:, 16], tmp[:, 17], tmp[:, 0], tmp[:, 1]
            tt(tmp[:, 4], lr, lr, MUL)
            link(tt(tmp[:, 5], li, li, MUL))
            link(tt(tmp[:, 4], tmp[:, 4], tmp[:, 5], ADD))
            link(V.reciprocal(tmp[:, 5], tmp[:, 4]))
            tt(tmp[:, 6], er, lr, MUL)
            tt(tmp[:, 7], ei, li, MUL)
            tt(tmp[:, 8], ei, lr, MUL)
            link(tt(tmp[:, 9], er, li, MUL))
            tt(tmp[:, 10], tmp[:, 6], tmp[:, 7], ADD)
            link(tt(tmp[:, 11], tmp[:, 8], tmp[:, 9], SUB))
            link(tt(tmp[:, 10:12], tmp[:, 10:12], tmp[:, 5:6].to_broadcast([P, 2, GROUPS]), MUL))
            tt(tmp[:, 12], tmp[:, 28], tmp[:, 10], MUL)
            tt(tmp[:, 13], tmp[:, 29], tmp[:, 11], MUL)
            tt(tmp[:, 14], tmp[:, 28], tmp[:, 11], MUL)
            link(tt(tmp[:, 15], tmp[:, 29], tmp[:, 10], MUL))
            tt(tmp[:, 18], tmp[:, 12], tmp[:, 13], SUB)
            link(tt(tmp[:, 19], tmp[:, 14], tmp[:, 15], ADD))
            dve.wait_ge(S("b_in"), 32)
            scratch = tmpP.rearrange("p a b c -> p (a b c)").rearrange("p (g h) -> p g h", h=GW)
            for dst, f in ((Bb_sb, 10), (Bp_sb, 18)):
                fr, fi = (tmp[:, f + j].unsqueeze(2).to_broadcast([P, GROUPS, GW]) for j in range(2))
                br, bi = b_raw[:, 0], b_raw[:, 1]
                re, im = dst[:, 0, 0:GROUPS], dst[:, 1, 0:GROUPS]
                tt(re, br, fr, MUL)
                link(tt(scratch, bi, fi, MUL))
                link(tt(re, re, scratch, SUB))
                tt(im, br, fi, MUL)
                link(tt(scratch, bi, fr, MUL))
                link(tt(im, im, scratch, ADD))

            def p_table(b):
                G = slice(b * BG, (b + 1) * BG)
                Br, Bi = (Bp_sb[:, j, G].unsqueeze(2).to_broadcast([P, BG, CH, GW]) for j in range(2))
                W = [pw[:, j, G].unsqueeze(3).to_broadcast([P, BG, CH, GW]) for j in range(4)]
                if b:
                    dve.wait_ge(S("pt_done"), 4 * b)
                tt(P_re, Br, W[0], MUL)
                link(tt(tmpP, Bi, W[2], MUL))
                link(tt(P_re, P_re, tmpP, ADD))
                tt(P_im, Br, W[1], MUL)
                link(tt(tmpP, Bi, W[0], MUL))
                tt(P_im, P_im, tmpP, ADD).then_inc(S("P_ready"), 1)
                dve.wait_ge(S("P_ready"), b + 1)

            def inverse_rms(cols, sq, n, name):
                dve.wait_ge(S(f"sq{name}"), n)
                src = small[:, 0:4] if name == 0 else cols
                ts(cols, src, 1.0 / D, EPS, MUL, ADD).then_inc(S(f"ms{name}"), 1)
                dve.wait_ge(S(f"rt{name}"), 1)
                link(V.reciprocal(cols, cols))

            def mod_add(n):
                dve.wait_ge(S("ada_used"), KT * (n + 1))
                dve.wait_ge(S(f"adab_in{n % 2}"), 64 * (n // 2 + 1))
                if n:
                    dve.wait_ge(S("mod_out"), 64 * n)
                for q in range(4):
                    r = slice(32 * q, 32 * q + 2)
                    tt(mod_sb[r], bank[n % 2][r, :], adab[r, n % 2], ADD).then_inc(S("mod_sb_full"), 1)

            inverse_rms(small[:, 4:8], None, 4, 0)
            p_table(0)
            mod_add(0)
            p_table(1)
            dve.wait_ge(S("bc_in"), 80)
            nrow = at(DU_off, D, of=s5_mem)
            stt(bc[:, 1], bc[:, 1], 1.0, nrow, ADD, MUL)
            link(stt(bc[:, 3], bc[:, 3], 1.0, nrow, ADD, MUL))
            for j in range(4):
                s, t = j // 2, j % 2
                src = (hlat if s == 0 else ut[:, 1])[:, t]
                link(stt(ut[:, s, t], src, small[:, 4 + j:5 + j], bc[:, 2 * s + 1], MUL, MUL))
                tt(ut[:, s, t], ut[:, s, t], bc[:, 2 * s], ADD).then_inc(S("u_ready"), 1)

            dve.wait_ge(S("d_in"), 16)
            dve.wait_ge(S("consts_in"), 16)
            for q in range(4):
                r = slice(32 * q, 32 * q + 32)
                ins = tt(DD[r], D_sb[r].unsqueeze(2).to_broadcast([32, GROUPS // 4, GW]),
                         ident[r, 32 * q:32 * q + GW].unsqueeze(1).to_broadcast([32, GROUPS // 4, GW]), MUL)
            link(ins)

            def kernels_out(b):
                dve.wait_ge(S("tk_done"), b + 1)
                if b >= 4:
                    dve.wait_ge(S("t_out"), 64)
                T_b = T_sb[:, b % 4]
                V.tensor_copy(T_b[:, :, 0:P], psum(5, 4, P)[:, 0:2]).then_inc(S("T_ready"), 1)
                V.tensor_copy(T_b[:, :, P:240], psum(4, 4, P)[:, 0:2, GW:P]).then_inc(S("T_ready"), 1)
                dve.wait_ge(S("T_ready"), 3 * b + 2)
                link(tt(T_b[:, :, P - GW:P], T_b[:, :, P - GW:P], psum(4, 4, P)[:, 0:2, 0:GW], ADD))
                tt(T_b[:, :, P - GW:P], T_b[:, :, P - GW:P], DD[:, 2 * b:2 * b + 2], ADD).then_inc(S("T_ready"), 1)

            def inside_out(h):
                dve.wait_ge(S("m_done"), 4 * (h + 1))
                for j in range(2):
                    V.tensor_copy(y_in[:, 4 * j:4 * j + 4], psum(4 + j, 4, CH, GW)).then_inc(S("yi_out"), 1)

            def scan(h):
                dve.wait_ge(S("e_out"), 24 * (h + 1))
                base = h * 6 * (2 * NCH - 2)
                sets = [slice(0, HG // 2), slice(HG // 2, HG)]
                for i in range(1, 2 * NCH - 1):
                    n = base + 6 * (i - 1)
                    for j, G in enumerate(sets):
                        if i > 1:
                            dve.wait_ge(S("scan"), n - 1 + j)
                        prev = e_sb[:, i - 1, :, G].unsqueeze(2).to_broadcast([P, 2, 2, HG // 2])
                        tt(sc4[:, :, :, G], prev, LT[:, :, :, h * HG + G.start:h * HG + G.stop], MUL).then_inc(S("scan"), 1)
                    for j, G in enumerate(sets):
                        dve.wait_ge(S("scan"), n + 1 + j)
                        tt(sc2[:, :, G], sc4[:, 0, :, G], e_sb[:, i, :, G], ADD).then_inc(S("scan"), 1)
                    for j, G in enumerate(sets):
                        dve.wait_ge(S("scan"), n + 3 + j)
                        tt(e_sb[:, i, :, G], sc2[:, :, G], sc4[:, 1, :, G], ADD).then_inc(S("scan"), 1)
                dve.wait_ge(S("scan"), base + 6 * (2 * NCH - 2))
                dve.sem_inc(S("scan_done"), 1)

            def y_out(h):
                dve.wait_ge(S("y_done"), h + 1)
                dve.wait_ge(S("yi_out"), 2 * (h + 1))
                if h:
                    dve.wait_ge(S("z_out"), 64)
                for j in range(2):
                    tt(y_sb[:, :, 64 * j:64 * j + 64].rearrange("p b (g h) -> p g b h", g=4), psum(6 + j, 4, CH, GW),
                       y_in[:, 4 * j:4 * j + 4], ADD).then_inc(S("y_ready"), 1)

            def g_table(b):
                G = slice(b * BG, (b + 1) * BG)
                Cr, Ci = (C_sb[:, j, G].unsqueeze(2).to_broadcast([P, BG, CH, GW]) for j in range(2))
                W = [pw[:, j, G].unsqueeze(3).to_broadcast([P, BG, CH, GW]) for j in range(4)]
                gr, gi = (t[:, b % 4 * BG:(b % 4 + 1) * BG] for t in (G_re, G_nim))
                dve.wait_ge(S("y_done"), 1)
                tt(gr, Cr, W[0], MUL)
                link(tt(tmpP, Ci, W[2], MUL))
                link(tt(gr, gr, tmpP, ADD))
                tt(gi, Cr, W[2], MUL)
                link(tt(tmpP, Ci, W[3], MUL))
                tt(gi, gi, tmpP, ADD).then_inc(S("g_dve"), 1)
                dve.wait_ge(S("g_dve"), b - 5)

            p_table(2)
            for b in range(4):
                kernels_out(b)
            p_table(3)
            mod_add(1)
            scan(0)
            mod_add(2)
            inside_out(0)
            y_out(0)
            p_table(6)
            g_table(6)
            p_table(7)
            mod_add(3)
            g_table(7)
            scan(1)
            mod_add(4)
            mod_add(5)
            inside_out(1)
            y_out(1)

            dve.wait_ge(S("rows_a"), 96)
            link(stt(bd[:, 2], bd[:, 2], 1.0, bd[:, 3], ADD, MUL))
            quarters = lambda v: v.rearrange("p t (c n) -> p (t c) n", c=2)
            uq, zq, hq, aq = quarters(u_tok), quarters(z_tok), quarters(hlat), quarters(acc)
            half = lambda row, j: row[:, (j % 2) * 512:(j % 2 + 1) * 512]
            for j in range(4):
                dve.wait_ge(S("glu_pe"), j + 1)
                tt(uq[:, j], bank[4 + j][:, :], half(bd[:, 0], j), ADD).then_inc(S("gate_in"), 1)
            for j in range(4):
                dve.wait_ge(S("sigm"), j + 1)
                dve.wait_ge(S("z_in"), 32)
                link(tt(uq[:, j], uq[:, j], zq[:, j], MUL))
                link(tt(uq[:, j], uq[:, j], half(bd[:, 1], j), MUL))
                ins = tt(hq[:, j], hq[:, j], uq[:, j], ADD)
                link(ins)
                if j % 2:
                    dve.sem_inc(S("h1"), 1)

            def norm(cols, name, shift, scale, done, n):
                inverse_rms(cols, None, 2, name)
                for t in range(TT):
                    link(stt(u_tok[:, t], hlat[:, t], cols[:, t:t + 1], scale, MUL, MUL))
                    link(tt(u_tok[:, t], u_tok[:, t], shift, ADD))
                dve.sem_inc(S(done), n)

            norm(small[:, 8:10], 1, bd[:, 4], bd[:, 2], "u1_ready", 2)

            def low(n, b, slot, half):
                dve.wait_ge(S("high"), n + 1)
                tt(w_lo[:, b], ring[:, slot, half * PIECE:(half + 1) * PIECE], w_hi[:, b].bitcast(F32), SUB).then_inc(S("low"), 1)

            def ffn_low(m, slot):
                for half in range(2):
                    low(2 * m + half, (2 * slot + half) % NPIECE, slot, half)

            ffn_low(0, 0)
            ffn_low(1, 1)
            for j in range(4):
                dve.wait_ge(S("x_hi"), j + 1)
                tt(x_lo[:, 2 * j:2 * j + 2], psum(j % 2, 2, SEQ), x_hi[:, 2 * j:2 * j + 2].bitcast(F32), SUB).then_inc(S("x_lo"), 1)

            def ffn_h(c):
                dve.wait_ge(S("f_silu"), c + 1)
                dve.wait_ge(S("piece_used"), ffn_pieces("up", c))
                if not (isinstance(c, int) and c == 0):
                    dve.wait_ge(S("f_hl"), c)
                tt(h_sb, sg, bank[5][:, :], MUL).then_inc(S("f_h"), 1)

            def ffn_hl(c):
                dve.wait_ge(S("f_hT"), c + 1)
                tt(h_lo[:], h_sb.rearrange("p (a b) -> p a b", a=4), h_hi[:].bitcast(F32), SUB).then_inc(S("f_hl"), 1)

            def ffn_chunk(c, s):
                ffn_low(3 * c - 1, s)
                ffn_low(3 * c, (s + 1) % 6)
                ffn_hl(c - 1)
                ffn_low(3 * c + 1, (s + 2) % 6)
                ffn_h(c)

            ffn_h(0)
            ffn_chunk(1, 2)
            ffn_chunk(2, 5)
            dve.wait_ge(S("rows_b"), 96)
            stt(bd[:, 1], bd[:, 1], 1.0, bd[:, 3], ADD, MUL)
            link(tt(Ysb, Ysb, bd[:, 2], MUL))
            with dve.Fori(1, NF0 // 2) as i:
                ffn_chunk(2 * i + 1, 2)
                ffn_chunk(2 * i + 2, 5)
            ffn_low(FFN_UNITS - 1, (FFN_UNITS - 1) % 6)
            ffn_hl(NF0 - 1)
            dve.wait_ge(S("piece_used"), FFN_PIECES)
            for j in range(4):
                link(tt(uq[:, j], bank[j][:, :], half(bd[:, 5], j), MUL))
                link(tt(hq[:, j], hq[:, j], uq[:, j], ADD))
                if j % 2:
                    dve.sem_inc(S("h2"), 1)

            norm(small[:, 12:14], 2, bd[:, 0], bd[:, 1], "u2_ready", 1)
            dve.wait_ge(S("rows_c"), 64)
            link(stt(bd[:, 1], bd[:, 1], 1.0, bd[:, 3], ADD, MUL))
            dve.wait_ge(S("pool_pe"), 1)
            for j in range(4):
                link(tt(uq[:, j], bank[4 + j][:, :], half(bd[:, 4], j), ADD))
                link(tt(uq[:, j], uq[:, j], half(Ysb, j), MUL))
                link(tt(hq[:, j], hq[:, j], uq[:, j], ADD))
                if j % 2:
                    dve.sem_inc(S("h3"), 1)
            norm(small[:, 16:18], 3, bd[:, 0], bd[:, 1], "u3_ready", 1)

            R = lambda k: rb[:, k]
            V.memset(acc, 0.0)
            V.memset(selT, 0.0)
            V.memset(Ysb, 0.0).then_inc(S("moe_init"), 1)
            V.memset(rankx[:, :, 2 * NE], -5.0)
            V.memset(combx, 0.0)
            for t in range(TT):
                link(ts(R(4)[:, t], iota[:, 0:NE], -float(NE), None, ADD))
            for r in range(AHEAD):
                for part in range(2):
                    low(FFN_PIECES + 2 * r + part, 2 * r + part, r, part)
            dve.wait_ge(S("logits"), 1)
            link(V.tensor_copy(R(0), psum(2, 64, NE)[:, 0:TT]))

            def best(src, top, eq, key, idx, mask):
                wide = [P, TT, NE]
                link(V.reduce_max(top, src, AX.X))
                link(tt(eq, src, top.unsqueeze(2).to_broadcast(wide), ALU.is_equal))
                link(tt(key, eq, R(4), MUL))
                link(V.tensor_reduce(idx, key, AX.X, ALU.min))
                link(tt(mask, R(4), idx.unsqueeze(2).to_broadcast(wide), ALU.is_equal))

            best(R(0), small[:, 18:20], R(1), R(2), small[:, 26:28], R(3))
            link(stt(R(5), R(3), -3.0e38, R(0), MUL, ADD))
            best(R(5), small[:, 20:22], R(1), R(2), small[:, 28:30], R(6))
            tt(small[:, 22:24], small[:, 20:22], small[:, 18:20], SUB).then_inc(S("top2"), 1)
            tt(R(8), R(3), R(6), ADD).then_inc(S("mask"), 1)
            dve.wait_ge(S("top_exp"), 1)
            dve.wait_ge(S("mask"), 1)
            link(ts(small[:, 30:32], small[:, 24:26], 1.0, None, ADD))
            link(V.reciprocal(small[:, 30:32], small[:, 30:32]))
            link(tt(small[:, 34:36], small[:, 24:26], small[:, 30:32], MUL))
            wide = [P, TT, NE]
            tt(R(9), R(3), small[:, 30:32].unsqueeze(2).to_broadcast(wide), MUL)
            link(tt(R(10), R(6), small[:, 34:36].unsqueeze(2).to_broadcast(wide), MUL))
            tt(combx[:, :, 1:NE + 1], R(9), R(10), ADD)
            tt(combx[:, :, NE + 2:2 * NE + 2], R(9), R(10), ADD)
            dve.wait_ge(S("rank_pe"), 1)
            link(stt(R(11), psum(3, 64, NE)[:, 0:TT], -1000.0, R(8), ADD, MUL))
            ts(rankx[:, :, 0:NE], R(11), 1000.0, None, ADD)
            link(ts(rankx[:, :, NE:2 * NE], R(11), 1000.0 - P, None, ADD))
            link(V.reduce_max(small[:, 36:37], psum(3, 64, NE)[:, 2], AX.X))
            ts(flag_i[:, 0:1], small[:, 36:37], float(P), None, ALU.is_gt).then_inc(S("overflow_known"), 1)

            def select(col, n):
                for t in range(TT):
                    ins = ts(sel[:, t], iota, rankx[:, t, col], None, ALU.is_equal)
                    if t:
                        ins.then_inc(S("sel_ready"), 1)

            def accumulate(r, n, col):
                dve.wait_ge(S("scat_pe"), n)
                stt(aq[:, r], bank[7][:, :], combx[:, r // 2, col], aq[:, r], MUL, ADD).then_inc(S("scat_acc"), 1)

            def gather_low(half, n):
                dve.wait_ge(S(f"gather_hi{half}"), n)
                tt(x_lo[:, 4 * half:4 * half + 4, 0:P], psum(7, 4, P), x_hi[:, 4 * half:4 * half + 4, 0:P].bitcast(F32), SUB).then_inc(S(f"gather_lo{half}"), 1)

            def expert(i, k):
                zero = isinstance(i, int) and i == 0

                def lows(*units):
                    for r in units:
                        if zero and r < AHEAD:
                            continue
                        for half in range(2):
                            low(i * EXPERT_PIECES + (FFN_PIECES + 2 * r + half), (2 * r + half) % NPIECE, r % NSLOT, half)

                def product_h(c):
                    dve.wait_ge(S("x_silu"), i * NF1 + c + 1)
                    dve.wait_ge(S("piece_used"), expert_pieces(i, "up", c))
                    if not (zero and c == 0):
                        dve.wait_ge(S("x_tr"), i * NF1 + c)
                    tt(h_sb, sg, bank[2 + c % 2][:, :], MUL).then_inc(S("x_h"), 1)

                def h_low(c):
                    dve.wait_ge(S("x_hT"), i * NF1 + c + 1)
                    tt(h_lo[:], psum(6, 4, P), h_hi[:].bitcast(F32), SUB).then_inc(S("x_hl"), 1)

                r = 0
                for c in range(NF1):
                    lows(r, r + 1, r + 2)
                    if c:
                        h_low(c - 1)
                    lows(r + 3)
                    if c < 2:
                        accumulate(2 * c, i * 4 + 4 * k + 2 * c + 1, bass.ds(i + k, 1))
                    r += 4
                    if c:
                        lows(r)
                    product_h(c)
                    if c < 2:
                        accumulate(2 * c + 1, i * 4 + 4 * k + 2 * c + 2, bass.ds(i + k, 1))
                    if c == 3:
                        dve.wait_ge(S("seltr"), i + 1)
                        select(bass.ds(i + 1, 1), i + 2)
                    if c:
                        lows(r + 1)
                        r += 2
                lows(r)
                h_low(NF1 - 1)
                gather_low(0, i + 2)
                lows(r + 1)
                gather_low(1, i + 2)

            select(bass.ds(0, 1), 1)
            gather_low(0, 1)
            gather_low(1, 1)
            expert(0, 0)
            with dve.Fori(1, NE) as i:
                expert(i, 0)
            for r in range(4):
                accumulate(r, 4 * NE + r + 1, bass.ds(NE, 1))
            dve.wait_ge(S("overflow_known"), 1)
            more = dve.value_load(flag_i[0:1, 0:1], min_val=0, max_val=1)
            with dve.If(more):
                with dve.Fori(NE, 2 * NE) as i:
                    expert(i, 1)
                for r in range(4):
                    accumulate(r, 8 * NE + 4 + r + 1, bass.ds(2 * NE + 1, 1))
            link(V.memset(small[:, 40:41], 0.0))
            for j in range(4):
                link(tt(uq[:, j], aq[:, j], half(bd[:, 5], j), MUL))
                link(tt(hq[:, j], hq[:, j], uq[:, j], ADD))
                if j % 2:
                    dve.sem_inc(S("h4"), 1)
            inverse_rms(small[:, 32:34], None, 2, 4)
            dve.wait_ge(S("rows_d"), 16)
            for t in range(TT):
                stt(u_tok[:, t], hlat[:, t], small[:, 32 + t:33 + t], bd[:, 3], MUL, MUL).then_inc(S("result"), 1)


def _pool_matrix(np):
    width = 64
    m = np.zeros((4, SEQ, SEQ), np.float32)
    for g, win in enumerate((2, 4, 8, 16)):
        for tok in range(SEQ):
            row, pos = divmod(tok, width)
            lo, hi = max(pos - win // 2, 0), min(pos + win // 2, width)
            m[g, row * width + lo:row * width + hi, tok] = np.float32(1) / np.float32(hi - lo)
            m[g, tok, tok] -= np.float32(1)
    order = np.arange(SEQ).reshape(NCH, CH).T.reshape(-1)
    m = m[:, order][:, :, order]
    return np.ascontiguousarray(m.reshape(4, TT, P, SEQ).transpose(2, 0, 1, 3))


def kernel(x, c, ctx, c_ctx, ada_w, ada_b, norm_mix, norm_ffn, norm_final,
           s5_lambda_re, s5_lambda_im, s5_log_step, s5_b_re, s5_b_im, s5_c_re, s5_c_im,
           s5_d, s5_glu_w, s5_glu_b, pool_w, pool_b, pool_scale, fnet_w, fnet_b,
           ffn_w_gate, ffn_w_up, ffn_w_down, moe_router, moe_w_gate, moe_w_up, moe_w_down):
    import numpy as np
    import concourse.bacc as bacc
    from concourse.bass_utils import run_bass_kernel_spmd

    A = np.asarray

    def rows(v):
        return A(v).reshape(NCH, CH, D).transpose(1, 0, 2).reshape(SEQ, D)

    def lam(v):
        return A(v)[0].transpose(0, 2, 1).reshape(P, GROUPS)

    eye = np.eye(P, dtype=np.float32)
    tri = np.triu(np.ones((P, P), np.float32), 1)
    iota = np.tile(np.arange(P, dtype=np.float32), (P, 1))
    arrays = dict(
        x_in=rows(x), ctx_in=rows(ctx),
        cond_in=np.stack([A(c)[0], A(c_ctx)], 1).reshape(KT, P, 2).transpose(1, 0, 2),
        ada_w=A(ada_w), ada_b=A(ada_b), norm_mix=A(norm_mix), norm_ffn=A(norm_ffn), norm_final=A(norm_final)[None],
        lam_re=lam(s5_lambda_re), lam_im=lam(s5_lambda_im),
        log_step=np.broadcast_to(A(s5_log_step)[0][:, None, :], (2, NST, GROUPS)).reshape(P, GROUPS),
        b_re=A(s5_b_re)[0].transpose(0, 2, 1, 3).reshape(P, GROUPS, GW),
        b_im=A(s5_b_im)[0].transpose(0, 2, 1, 3).reshape(P, GROUPS, GW),
        c_re=A(s5_c_re)[0].transpose(0, 3, 1, 2).reshape(P, GROUPS, GW),
        c_im=A(s5_c_im)[0].transpose(0, 3, 1, 2).reshape(P, GROUPS, GW),
        d_skip=np.pad(A(s5_d)[0].reshape(GROUPS // 4, 4, GW), ((0, 0), (0, 0), (0, GW))).transpose(1, 2, 0).reshape(P, GROUPS // 4),
        glu_w=A(s5_glu_w)[0], glu_b=A(s5_glu_b), pool_w=A(pool_w)[0], pool_b=A(pool_b), pool_scale=A(pool_scale),
        w_gate=A(ffn_w_gate)[0], w_up=A(ffn_w_up)[0], w_down=A(ffn_w_down)[0], router=A(moe_router)[0],
        e_gate=A(moe_w_gate)[0], e_up=A(moe_w_up)[0], e_down=A(moe_w_down)[0],
        consts=np.stack([eye, tri, np.ones((P, P), np.float32), iota], 1),
        pool_mat=_pool_matrix(np),
    )
    arrays = {k: np.ascontiguousarray(v) for k, v in arrays.items()}
    nc = bacc.Bacc("TRN2", target_bir_lowering=False, num_devices=1)
    aps = {k: nc.dram_tensor(k, v.shape, mybir.dt.from_np(v.dtype), kind="ExternalInput").ap() for k, v in arrays.items()}
    out = nc.dram_tensor("out", (SEQ, D), mybir.dt.float32, kind="ExternalOutput").ap()
    build(nc, out=out, **aps)
    got = run_bass_kernel_spmd(nc, [arrays], core_ids=[0]).results[0]["out"]
    return got.reshape(CH, NCH, D).transpose(1, 0, 2).reshape(1, SEQ, D)
```
